# Optimizing a Trainium2 kernel written in Bass

```python
import math
import jax, jax.numpy as jnp
from jax import lax
import numpy as np
import jax
import jax.numpy as jnp

D_MODEL = 1024
BATCH = 1
SEQ = 256
DEPTH = 1

SSM_EXPAND = 2
SSM_D_INNER = SSM_EXPAND * D_MODEL
SSM_HEAD_DIM = 64
SSM_HEADS = SSM_D_INNER // SSM_HEAD_DIM
SSM_GROUPS = 4
SSM_HEADS_PER_GROUP = SSM_HEADS // SSM_GROUPS
SSM_D_STATE = 128
SSM_CONV = 4
SSM_CHUNK = 128
SSM_BC_DIM = SSM_GROUPS * SSM_D_STATE
SSM_CONV_DIM = SSM_D_INNER + 2 * SSM_BC_DIM
SSM_NORM_GROUP = SSM_D_INNER // SSM_GROUPS
SSM_DT_MIN = 0.001
SSM_DT_MAX = 0.1

LRU_WIDTH = 1280
LRU_BLOCKS = 10
LRU_BLOCK = LRU_WIDTH // LRU_BLOCKS
LRU_CONV = 4
LRU_C = 8.0

FFN_HIDDEN = -(-8 * D_MODEL // (3 * 256)) * 256

RMS_EPS = 1e-6

N_GATES = 2 * D_MODEL
IN_PROJ_DIM = N_GATES + SSM_D_INNER + SSM_CONV_DIM + SSM_HEADS + 2 * LRU_WIDTH
IN_SPLITS = (
    N_GATES,
    N_GATES + SSM_D_INNER,
    N_GATES + SSM_D_INNER + SSM_CONV_DIM,
    N_GATES + SSM_D_INNER + SSM_CONV_DIM + SSM_HEADS,
    N_GATES + SSM_D_INNER + SSM_CONV_DIM + SSM_HEADS + LRU_WIDTH,
)


def rmsnorm(x, w, eps=RMS_EPS):
    xf = x.astype(jnp.float32)
    y = xf * lax.rsqrt(jnp.mean(xf * xf, axis=-1, keepdims=True) + eps)
    return (y * w.astype(jnp.float32)).astype(x.dtype)

def causal_dwconv(u, w, b):
    k_width = w.shape[0]
    length = u.shape[1]
    up = jnp.pad(u, ((0, 0), (k_width - 1, 0), (0, 0)))
    out = b + up[:, 0:length] * w[0]
    for k in range(1, k_width):
        out = out + up[:, k:k + length] * w[k]
    return out

def segsum_exp(cs):
    t = cs.shape[-1]
    mask = jnp.tril(jnp.ones((t, t), dtype=bool))
    diff = cs[..., :, None] - cs[..., None, :]
    return jnp.exp(jnp.where(mask, diff, -jnp.inf))

def ssd_chunked(xdt, dA, bm, cm):
    b, length, g, r, p = xdt.shape
    n = bm.shape[-1]
    l = SSM_CHUNK
    c = length // l
    xdt = xdt.reshape(b, c, l, g, r, p)
    dA = dA.reshape(b, c, l, g, r)
    bm = bm.reshape(b, c, l, g, n)
    cm = cm.reshape(b, c, l, g, n)

    cs = jnp.cumsum(dA, axis=2)
    lmat = segsum_exp(jnp.moveaxis(cs, 2, -1))
    cb = jnp.einsum('bclgn,bcsgn->bcgls', cm, bm)
    y_diag = jnp.einsum('bcgls,bcgrls,bcsgrp->bclgrp', cb, lmat, xdt)
    decay_states = jnp.exp(cs[:, :, -1:] - cs)
    states = jnp.einsum('bclgn,bclgr,bclgrp->bcgrpn', bm, decay_states, xdt)
    chunk_tot = jnp.moveaxis(cs[:, :, -1], 1, -1)
    chunk_cs = jnp.cumsum(jnp.pad(chunk_tot, ((0, 0), (0, 0), (0, 0), (1, 0))), axis=-1)
    decay_chunk = segsum_exp(chunk_cs)
    states = jnp.concatenate([jnp.zeros_like(states[:, :1]), states], axis=1)
    states_in = jnp.einsum('bgrzc,bcgrpn->bzgrpn', decay_chunk[..., :-1, :], states)
    y_off = jnp.einsum('bclgn,bcgrpn,bclgr->bclgrp', cm, states_in, jnp.exp(cs))
    return (y_diag + y_off).reshape(b, length, g, r, p)

def mamba2_mixer(z, xbc, dt_raw, conv_w, conv_b, dt_bias, a_log, d_skip, norm_w):
    b, length, _ = z.shape
    f32 = jnp.float32
    xbc = jax.nn.silu(causal_dwconv(xbc, conv_w, conv_b))
    xs, bm, cm = jnp.split(xbc, [SSM_D_INNER, SSM_D_INNER + SSM_BC_DIM], axis=-1)
    dt = jax.nn.softplus(dt_raw.astype(f32) + dt_bias.astype(f32))
    a = -jnp.exp(a_log.astype(f32))
    g, r, p, n = SSM_GROUPS, SSM_HEADS_PER_GROUP, SSM_HEAD_DIM, SSM_D_STATE
    xs_h = xs.astype(f32).reshape(b, length, g, r, p)
    dt_h = dt.reshape(b, length, g, r)
    y = ssd_chunked(xs_h * dt_h[..., None], dt_h * a.reshape(g, r),
                    bm.astype(f32).reshape(b, length, g, n),
                    cm.astype(f32).reshape(b, length, g, n))
    y = y + xs_h * d_skip.astype(f32).reshape(g, r, 1)
    y = y.reshape(b, length, SSM_D_INNER) * jax.nn.silu(z.astype(f32))
    yg = y.reshape(b, length, SSM_GROUPS, SSM_NORM_GROUP)
    yg = yg * lax.rsqrt(jnp.mean(yg * yg, axis=-1, keepdims=True) + RMS_EPS)
    y = yg.reshape(b, length, SSM_D_INNER) * norm_w.astype(f32)
    return y.astype(z.dtype)

def rglru_mixer(xl, yl, conv_w, conv_b, w_r, b_r, w_i, b_i, lam):
    b, length, _ = xl.shape
    f32 = jnp.float32
    u = causal_dwconv(xl, conv_w, conv_b)
    ub = u.reshape(b, length, LRU_BLOCKS, LRU_BLOCK)
    r_gate = jax.nn.sigmoid((jnp.einsum('blhi,hij->blhj', ub, w_r).reshape(b, length, LRU_WIDTH) + b_r).astype(f32))
    i_gate = jax.nn.sigmoid((jnp.einsum('blhi,hij->blhj', ub, w_i).reshape(b, length, LRU_WIDTH) + b_i).astype(f32))
    log_a = -LRU_C * r_gate * jax.nn.softplus(-lam.astype(f32))
    a_t = jnp.exp(log_a)
    b_t = jnp.sqrt(-jnp.expm1(2.0 * log_a)) * (i_gate * u.astype(f32))

    def combine(left, right):
        a1, b1 = left
        a2, b2 = right
        return a1 * a2, a2 * b1 + b2

    _, h = lax.associative_scan(combine, (a_t, b_t), axis=1)
    out = h * jax.nn.gelu(yl.astype(f32), approximate=True)
    return out.astype(xl.dtype)

def first_inputs(seed: int = 0) -> dict:
    key = jax.random.key(seed)
    ks = jax.random.split(key, 32)
    f32 = jnp.float32
    nrm = lambda k, shape, scale: jax.random.normal(k, shape, f32) * scale
    L = DEPTH

    x = jax.random.normal(ks[0], (BATCH, SEQ, D_MODEL), f32)
    norm1_w = 1.0 + nrm(ks[1], (L, D_MODEL), 0.05)
    w_in = nrm(ks[2], (L, D_MODEL, IN_PROJ_DIM), D_MODEL ** -0.5)
    b_branch_gate = nrm(ks[3], (L, N_GATES), 0.1)

    ssm_conv_w = nrm(ks[4], (L, SSM_CONV, SSM_CONV_DIM), SSM_CONV ** -0.5)
    ssm_conv_b = nrm(ks[5], (L, SSM_CONV_DIM), 0.02)
    u = jax.random.uniform(ks[6], (L, SSM_HEADS), f32)
    dt0 = jnp.exp(u * (math.log(SSM_DT_MAX) - math.log(SSM_DT_MIN)) + math.log(SSM_DT_MIN))
    dt0 = jnp.maximum(dt0, 1e-4)
    ssm_dt_bias = dt0 + jnp.log(-jnp.expm1(-dt0))
    ssm_a_log = jnp.log(jax.random.uniform(ks[7], (L, SSM_HEADS), f32, 1.0, 16.0))
    ssm_d = 1.0 + nrm(ks[8], (L, SSM_HEADS), 0.1)
    ssm_norm_w = 1.0 + nrm(ks[9], (L, SSM_D_INNER), 0.05)
    w_out_ssm = nrm(ks[10], (L, SSM_D_INNER, D_MODEL), SSM_D_INNER ** -0.5)

    lru_conv_w = nrm(ks[11], (L, LRU_CONV, LRU_WIDTH), LRU_CONV ** -0.5)
    lru_conv_b = nrm(ks[12], (L, LRU_WIDTH), 0.02)
    lru_w_r = nrm(ks[13], (L, LRU_BLOCKS, LRU_BLOCK, LRU_BLOCK), LRU_BLOCK ** -0.5)
    lru_b_r = nrm(ks[14], (L, LRU_WIDTH), 0.02)
    lru_w_i = nrm(ks[15], (L, LRU_BLOCKS, LRU_BLOCK, LRU_BLOCK), LRU_BLOCK ** -0.5)
    lru_b_i = nrm(ks[16], (L, LRU_WIDTH), 0.02)
    a0 = jax.random.uniform(ks[17], (L, LRU_WIDTH), f32, 0.9, 0.999)
    s0 = a0 ** (1.0 / LRU_C)
    lru_lambda = jnp.log(s0) - jnp.log1p(-s0)
    w_out_lru = nrm(ks[18], (L, LRU_WIDTH, D_MODEL), LRU_WIDTH ** -0.5)

    w_out = nrm(ks[19], (L, D_MODEL, D_MODEL), D_MODEL ** -0.5)
    norm2_w = 1.0 + nrm(ks[20], (L, D_MODEL), 0.05)
    w_ffn_in = nrm(ks[21], (L, D_MODEL, 2 * FFN_HIDDEN), D_MODEL ** -0.5)
    w_ffn_out = nrm(ks[22], (L, FFN_HIDDEN, D_MODEL), FFN_HIDDEN ** -0.5)
    norm_f_w = 1.0 + nrm(ks[23], (D_MODEL,), 0.05)

    return {
        "x": x, "norm1_w": norm1_w, "w_in": w_in, "b_branch_gate": b_branch_gate,
        "ssm_conv_w": ssm_conv_w, "ssm_conv_b": ssm_conv_b, "ssm_dt_bias": ssm_dt_bias,
        "ssm_a_log": ssm_a_log, "ssm_d": ssm_d, "ssm_norm_w": ssm_norm_w, "w_out_ssm": w_out_ssm,
        "lru_conv_w": lru_conv_w, "lru_conv_b": lru_conv_b, "lru_w_r": lru_w_r, "lru_b_r": lru_b_r,
        "lru_w_i": lru_w_i, "lru_b_i": lru_b_i, "lru_lambda": lru_lambda, "w_out_lru": w_out_lru,
        "w_out": w_out, "norm2_w": norm2_w, "w_ffn_in": w_ffn_in, "w_ffn_out": w_ffn_out,
        "norm_f_w": norm_f_w,
    }

def first_block(x, norm1_w, w_in, b_branch_gate, ssm_conv_w, ssm_conv_b, ssm_dt_bias, ssm_a_log,
              ssm_d, ssm_norm_w, w_out_ssm, lru_conv_w, lru_conv_b, lru_w_r, lru_b_r, lru_w_i,
              lru_b_i, lru_lambda, w_out_lru, w_out, norm2_w, w_ffn_in, w_ffn_out, norm_f_w):
    h = x
    for l in range(DEPTH):
        hn = rmsnorm(h, norm1_w[l])
        proj = hn @ w_in[l]
        gates, z, xbc, dt_raw, lru_x, lru_y = jnp.split(proj, IN_SPLITS, axis=-1)
        gates = jax.nn.sigmoid(gates + b_branch_gate[l])
        g_ssm, g_lru = jnp.split(gates, 2, axis=-1)
        y_ssm = mamba2_mixer(z, xbc, dt_raw, ssm_conv_w[l], ssm_conv_b[l], ssm_dt_bias[l],
                             ssm_a_log[l], ssm_d[l], ssm_norm_w[l]) @ w_out_ssm[l]
        y_lru = rglru_mixer(lru_x, lru_y, lru_conv_w[l], lru_conv_b[l], lru_w_r[l], lru_b_r[l],
                            lru_w_i[l], lru_b_i[l], lru_lambda[l]) @ w_out_lru[l]
        h = h + (g_ssm * y_ssm + g_lru * y_lru) @ w_out[l]
        hn = rmsnorm(h, norm2_w[l])
        gate, up = jnp.split(hn @ w_ffn_in[l], 2, axis=-1)
        h = h + (jax.nn.silu(gate) * up) @ w_ffn_out[l]
    return rmsnorm(h, norm_f_w)


DEPTH_2 = 2

HEAD_DIM = 64
RET_HEADS = 4
DSA_HEADS = 4
DIL_HEADS = 8
RET_W = RET_HEADS * HEAD_DIM
DSA_W = DSA_HEADS * HEAD_DIM
DIL_W = DIL_HEADS * HEAD_DIM
D_MIX = RET_W + DSA_W + DIL_W
RET_CHUNK = 128
RET_ROPE_BASE = 10000.0
KV_LATENT = 128
IDX_HEADS = 8
IDX_DIM = 64
TOPK_MAX = 256
QUERY_BLOCK = 128
DIL_PATTERNS = ((128, 1), (512, 4), (2048, 16))
D_FF = 4 * D_MODEL
NORM_EPS = 1e-6
RET_COLS = 4 * RET_W
DSA_SIZES = (DSA_W, KV_LATENT, IDX_HEADS * IDX_DIM, IDX_DIM, IDX_HEADS)
DSA_COLS = sum(DSA_SIZES)
DIL_COLS = 3 * DIL_W
N_IN = RET_COLS + DSA_COLS + DIL_COLS


def _offsets(sizes):
    return [int(o) for o in np.cumsum(sizes)[:-1]]

def rms_norm(x, w):
    xf = x.astype(jnp.float32)
    y = xf * lax.rsqrt(jnp.mean(xf * xf, axis=-1, keepdims=True) + NORM_EPS)
    return (y * w.astype(jnp.float32)).astype(x.dtype)

def rotary(x, pos):
    half = x.shape[-1] // 2
    inv = RET_ROPE_BASE ** (-jnp.arange(half, dtype=jnp.float32) / half)
    ang = pos.astype(jnp.float32)[:, None] * inv[None, :]
    cos = jnp.cos(ang)[None, :, None, :]
    sin = jnp.sin(ang)[None, :, None, :]
    xf = x.astype(jnp.float32)
    x1, x2 = xf[..., :half], xf[..., half:]
    return jnp.concatenate([x1 * cos - x2 * sin, x2 * cos + x1 * sin], axis=-1)

def retention_chunkwise(q, k, v):
    B, S, H, d = q.shape
    C = RET_CHUNK
    N = S // C
    log_g = jnp.log(1.0 - 2.0 ** (-5.0 - jnp.arange(H, dtype=jnp.float32)))

    def chunks(t):
        return t.reshape(B, N, C, H, d).transpose(0, 3, 1, 2, 4)

    qc, kc, vc = chunks(q), chunks(k * (d ** -0.5)), chunks(v)
    i = jnp.arange(C, dtype=jnp.float32)
    diff = i[:, None] - i[None, :]
    decay = jnp.exp(jnp.maximum(diff, 0.0)[None] * log_g[:, None, None]) * (diff >= 0)[None]
    inner = jnp.einsum('bhncd,bhnmd->bhncm', qc, kc) * decay[None, :, None]
    inner = jnp.einsum('bhncm,bhnme->bhnce', inner, vc)
    zeta = jnp.exp((C - 1.0 - i)[None, :] * log_g[:, None])
    xi = jnp.exp((i + 1.0)[None, :] * log_g[:, None])
    kv = jnp.einsum('bhnmd,bhnme->nbhde', kc * zeta[None, :, None, :, None], vc)
    g_chunk = jnp.exp(C * log_g)[None, :, None, None]

    def step(state, kv_n):
        return g_chunk * state + kv_n, state

    _, state_prev = lax.scan(step, jnp.zeros((B, H, d, d), jnp.float32), kv)
    cross = jnp.einsum('bhncd,nbhde->bhnce', qc, state_prev) * xi[None, :, None, :, None]
    o = inner + cross
    return o.transpose(0, 2, 3, 1, 4).reshape(B, S, H, d)

def retention_mixer(cols, norm_w, pos):
    B, S, _ = cols.shape
    q, k, v, g = jnp.split(cols, 4, axis=-1)
    shp = (B, S, RET_HEADS, HEAD_DIM)
    o = retention_chunkwise(rotary(q.reshape(shp), pos), rotary(k.reshape(shp), pos),
                            v.reshape(shp).astype(jnp.float32))
    mu = jnp.mean(o, axis=-1, keepdims=True)
    var = jnp.mean(jnp.square(o - mu), axis=-1, keepdims=True)
    o = (o - mu) * lax.rsqrt(var + NORM_EPS) * norm_w.astype(jnp.float32)
    o = o.reshape(B, S, RET_W)
    return (jax.nn.silu(g.astype(jnp.float32)) * o).astype(cols.dtype)

def dsa_mixer(cols, kv_norm_w, w_uk, w_uv):
    B, S, _ = cols.shape
    q, c_kv, q_idx, k_idx, w_idx = jnp.split(cols, _offsets(DSA_SIZES), axis=-1)
    q = q.reshape(B, S, DSA_HEADS, HEAD_DIM)
    c_kv = rms_norm(c_kv, kv_norm_w)
    k = (c_kv @ w_uk).reshape(B, S, DSA_HEADS, HEAD_DIM)
    v = (c_kv @ w_uv).reshape(B, S, DSA_HEADS, HEAD_DIM)
    q_idx = q_idx.reshape(B, S, IDX_HEADS, IDX_DIM)
    w_idx = w_idx * (IDX_HEADS ** -0.5 * IDX_DIM ** -0.5)
    n_sel = min(TOPK_MAX, S // 4)
    nblk = S // QUERY_BLOCK
    key_pos = jnp.arange(S)

    def to_blocks(t):
        return jnp.moveaxis(t.reshape((B, nblk, QUERY_BLOCK) + t.shape[2:]), 1, 0)

    def block(args):
        qb, qib, wb, start = args
        qpos = start + jnp.arange(QUERY_BLOCK)
        logits = jnp.einsum('bqhd,bsd->bqhs', qib, k_idx)
        score = jnp.einsum('bqhs,bqh->bqs', jax.nn.relu(logits), wb).astype(jnp.float32)
        causal = key_pos[None, :] <= qpos[:, None]
        score = jnp.where(causal[None], score, -jnp.inf)
        _, idx = lax.top_k(score, n_sel)
        k_sel = jax.vmap(lambda kb, ib: kb[ib])(k, idx)
        v_sel = jax.vmap(lambda vb, ib: vb[ib])(v, idx)
        s = jnp.einsum('bqhd,bqnhd->bhqn', qb, k_sel).astype(jnp.float32) * (HEAD_DIM ** -0.5)
        valid = (idx <= qpos[None, :, None])[:, None]
        p = jax.nn.softmax(jnp.where(valid, s, -jnp.inf), axis=-1).astype(v.dtype)
        return jnp.einsum('bhqn,bqnhd->bqhd', p, v_sel)

    starts = jnp.arange(nblk) * QUERY_BLOCK
    o = lax.map(block, (to_blocks(q), to_blocks(q_idx), to_blocks(w_idx), starts))
    return jnp.moveaxis(o, 0, 1).reshape(B, S, DSA_W).astype(cols.dtype)

def dilated_branch(q, k, v, window, dilation):
    B, S, H, d = q.shape
    steps = window // dilation
    n = S // dilation
    lb = min(steps, n)
    nb = -(-n // lb)
    pad = nb * lb - n

    def to_sub(t):
        t = t.reshape(B, n, dilation, H, d).transpose(0, 2, 3, 1, 4)
        t = jnp.pad(t, ((0, 0), (0, 0), (0, 0), (0, pad), (0, 0)))
        return t.reshape(B, dilation, H, nb, lb, d)

    def with_prev(t):
        prev = jnp.pad(t, ((0, 0), (0, 0), (0, 0), (1, 0), (0, 0), (0, 0)))[:, :, :, :-1]
        return jnp.concatenate([prev, t], axis=4)

    qs = to_sub(q)
    kk = with_prev(to_sub(k))
    vv = with_prev(to_sub(v)).astype(jnp.float32)
    qi = jnp.arange(lb)[:, None]
    kj = jnp.arange(2 * lb)[None, :]
    dist = lb + qi - kj
    key_idx = jnp.arange(nb)[:, None, None] * lb - lb + kj[None]
    mask = (dist >= 0) & (dist <= steps) & (key_idx >= 0)
    s = jnp.einsum('brhnqd,brhnkd->brhnqk', qs, kk).astype(jnp.float32) * (d ** -0.5)
    s = jnp.where(mask, s, -jnp.inf)
    m = jnp.max(s, axis=-1, keepdims=True)
    p = jnp.exp(s - m)
    den = jnp.sum(p, axis=-1, keepdims=True)
    o = jnp.einsum('brhnqk,brhnkd->brhnqd', p, vv) / den
    lse = (m + jnp.log(den))[..., 0]
    o = o.reshape(B, dilation, H, nb * lb, d)[:, :, :, :n].transpose(0, 3, 1, 2, 4).reshape(B, S, H, d)
    lse = lse.reshape(B, dilation, H, nb * lb)[:, :, :, :n].transpose(0, 3, 1, 2).reshape(B, S, H)
    return o, lse

def dilated_mixer(cols):
    B, S, _ = cols.shape
    q, k, v = jnp.split(cols, 3, axis=-1)
    shp = (B, S, DIL_HEADS, HEAD_DIM)
    q, k, v = q.reshape(shp), k.reshape(shp), v.reshape(shp)
    outs = []
    lses = []
    for window, dilation in DIL_PATTERNS:
        o, lse = dilated_branch(q, k, v, window, dilation)
        outs.append(o)
        lses.append(lse)
    alpha = jax.nn.softmax(jnp.stack(lses, axis=0), axis=0)
    o = jnp.sum(alpha[..., None] * jnp.stack(outs, axis=0), axis=0)
    return o.reshape(B, S, DIL_W).astype(cols.dtype)

def hybrid_layer(x, attn_norm_w, w_in, ret_norm_w, kv_norm_w, w_uk, w_uv, w_out, mlp_norm_w, w_up, w_down, pos):
    h = rms_norm(x, attn_norm_w)
    proj = h @ w_in
    ret_cols, dsa_cols, dil_cols = jnp.split(proj, _offsets((RET_COLS, DSA_COLS, DIL_COLS)), axis=-1)
    mixed = jnp.concatenate([retention_mixer(ret_cols, ret_norm_w, pos),
                             dsa_mixer(dsa_cols, kv_norm_w, w_uk, w_uv),
                             dilated_mixer(dil_cols)], axis=-1)
    x = x + mixed @ w_out
    h = rms_norm(x, mlp_norm_w)
    return x + jnp.square(jax.nn.relu(h @ w_up)) @ w_down

def second_inputs(seed: int = 0) -> dict:
    key = jax.random.key(seed)
    ks = jax.random.split(key, 12)
    f32 = jnp.float32

    def nrm(k, shape, scale):
        return jax.random.normal(k, shape, f32) * scale

    return {
        'x': nrm(ks[0], (BATCH, SEQ, D_MODEL), 1.0),
        'attn_norm_w': 1.0 + nrm(ks[1], (DEPTH_2, D_MODEL), 0.02),
        'w_in': nrm(ks[2], (DEPTH_2, D_MODEL, N_IN), D_MODEL ** -0.5),
        'ret_norm_w': 1.0 + nrm(ks[3], (DEPTH_2, RET_HEADS, HEAD_DIM), 0.02),
        'dsa_kv_norm_w': 1.0 + nrm(ks[4], (DEPTH_2, KV_LATENT), 0.02),
        'dsa_w_uk': nrm(ks[5], (DEPTH_2, KV_LATENT, DSA_W), KV_LATENT ** -0.5),
        'dsa_w_uv': nrm(ks[6], (DEPTH_2, KV_LATENT, DSA_W), KV_LATENT ** -0.5),
        'w_out': nrm(ks[7], (DEPTH_2, D_MIX, D_MODEL), D_MIX ** -0.5),
        'mlp_norm_w': 1.0 + nrm(ks[8], (DEPTH_2, D_MODEL), 0.02),
        'w_up': nrm(ks[9], (DEPTH_2, D_MODEL, D_FF), D_MODEL ** -0.5),
        'w_down': nrm(ks[10], (DEPTH_2, D_FF, D_MODEL), D_FF ** -0.5),
        'final_norm_w': 1.0 + nrm(ks[11], (D_MODEL,), 0.02),
    }

def second_block(x, attn_norm_w, w_in, ret_norm_w, dsa_kv_norm_w, dsa_w_uk, dsa_w_uv, w_out, mlp_norm_w, w_up, w_down, final_norm_w):
    pos = jnp.arange(x.shape[1])
    for layer in range(DEPTH_2):
        x = hybrid_layer(x, attn_norm_w[layer], w_in[layer], ret_norm_w[layer], dsa_kv_norm_w[layer],
                         dsa_w_uk[layer], dsa_w_uv[layer], w_out[layer], mlp_norm_w[layer],
                         w_up[layer], w_down[layer], pos)
    return rms_norm(x, final_norm_w)


def setup_inputs(seed=0):
    out = dict(first_inputs(seed))
    for name, value in second_inputs(seed + 1).items():
        if name != "x":
            out[name + "_2"] = value
    return out


def reference(
    x, norm1_w, w_in, b_branch_gate, ssm_conv_w, ssm_conv_b, ssm_dt_bias, ssm_a_log, ssm_d,
    ssm_norm_w, w_out_ssm, lru_conv_w, lru_conv_b, lru_w_r, lru_b_r, lru_w_i, lru_b_i,
    lru_lambda, w_out_lru, w_out, norm2_w, w_ffn_in, w_ffn_out, norm_f_w, attn_norm_w_2, w_in_2,
    ret_norm_w_2, dsa_kv_norm_w_2, dsa_w_uk_2, dsa_w_uv_2, w_out_2, mlp_norm_w_2, w_up_2,
    w_down_2, final_norm_w_2,
):
    x = first_block(
        x, norm1_w, w_in, b_branch_gate, ssm_conv_w, ssm_conv_b, ssm_dt_bias, ssm_a_log, ssm_d,
        ssm_norm_w, w_out_ssm, lru_conv_w, lru_conv_b, lru_w_r, lru_b_r, lru_w_i, lru_b_i,
        lru_lambda, w_out_lru, w_out, norm2_w, w_ffn_in, w_ffn_out, norm_f_w,
    )
    return second_block(
        x, attn_norm_w_2, w_in_2, ret_norm_w_2, dsa_kv_norm_w_2, dsa_w_uk_2, dsa_w_uv_2,
        w_out_2, mlp_norm_w_2, w_up_2, w_down_2, final_norm_w_2,
    )


_drawn_inputs = setup_inputs


def setup_inputs(seed=0):
    import zlib

    import numpy as np

    out = dict(_drawn_inputs(seed))
    spreads = {}
    factors = {'lru_b_r': 8.0, 'lru_b_i': 8.0, 'ret_norm_w_2': 6.601, 'dsa_kv_norm_w_2': 8.0}
    for name, (base, spread) in spreads.items():
        noise = np.random.default_rng([zlib.crc32(name.encode()), seed]).standard_normal(out[name].shape)
        drawn = base * np.exp(spread * noise) if base else spread * noise
        out[name] = jnp.asarray(drawn.astype(out[name].dtype))
    for name, factor in factors.items():
        out[name] = (out[name] * factor).astype(out[name].dtype)
    return out
```

```python
from contextlib import ExitStack

import numpy as np

import concourse.bass as bass
from concourse import mybir

F32 = mybir.dt.float32
F32R = mybir.dt.float32r
ACT = mybir.ActivationFunctionType
ALU = mybir.AluOpType
AX_X = mybir.AxisListType.X

P = 128
SEQ = 256
TT = SEQ // P
D = 1024
DC = D // P
EPS = 1e-6

D_INNER = 2048
HEADS = 32
HD = 64
GROUPS = 4
HPG = HEADS // GROUPS
STATE = 128
CONV = 4
XBC = D_INNER + 2 * GROUPS * STATE
LRU = 1280
LC = LRU // P
LRU_C = 8.0
FFN = 2816
COL_GATE = 0
COL_Z = 2 * D
COL_XBC = COL_Z + D_INNER
COL_B = COL_XBC + D_INNER
COL_C = COL_B + GROUPS * STATE
COL_DT = COL_XBC + XBC
COL_LX = COL_DT + HEADS
COL_LY = COL_LX + LRU
GC = D_INNER // GROUPS // P

DEPTH_2 = 2
RET_H, DSA_H, DIL_H = 4, 4, 8
RET_W, DSA_W, DIL_W = RET_H * HD, DSA_H * HD, DIL_H * HD
LATENT = 128
IDX_H = 8
TOPK = min(256, SEQ // 4)
FF2 = 4 * D
C_RET = 0
C_DSA = 4 * RET_W
C_CKV = C_DSA + DSA_W
C_QI = C_CKV + LATENT
C_KI = C_QI + IDX_H * HD
C_DIL = C_KI + HD + IDX_H
IDX_SCALE = float(IDX_H ** -0.5 * HD ** -0.5)
SCALE = float(HD) ** -0.5
MASKED = -3.0e38
TAKEN = -3.4e38

RAW_SLOTS, SPLIT_SLOTS = 3, 3
TILE = 2048
KQ = 3 * P

PARAMS = [
    ("norm1", DC), ("conv_w", CONV * XBC // P), ("conv_b", XBC // P), ("lconv_w", CONV * LC), ("lconv_b", LC),
    ("b_r", LC), ("b_i", LC), ("lam", LC), ("b_gate", 2 * DC), ("norm_w", D_INNER // P), ("d_skip", D_INNER // P),
    ("norm2", DC), ("dt_bias", 1), ("a_log", 1), ("attn", DC * DEPTH_2), ("mlp", DC * DEPTH_2),
    ("ret", RET_W // P * DEPTH_2), ("kvn", DEPTH_2), ("norm_f", DC), ("final", DC),
]
PARAM_AT, _n = {}, 0
for _name, _w in PARAMS:
    PARAM_AT[_name] = (_n, _w)
    _n += _w
N_PARAMS = _n

CONSTS = [("ident", P), ("mean_d", P), ("mean_group", P), ("mean_latent", P), ("mean_head", P), ("tri", KQ), ("eps", 1)]
CONSTS_2 = [("rotate", P), ("cos", SEQ), ("sin", SEQ), ("cos_k", SEQ), ("sin_k", SEQ), ("decay", RET_H * SEQ),
            ("causal", KQ), ("union", KQ), ("count", KQ)]


class Engine:

    def __init__(self, ops, sem):
        self.ops, self.sem, self.count, self.seen = ops, sem, 0, {}

    def wait(self, *tokens):
        for t in tokens:
            if t is None:
                continue
            if isinstance(t, list):
                self.wait(*t)
                continue
            sem, value = t
            if self.seen.get(sem.name, 0) < value:
                self.ops.wait_ge(sem, value)
                self.seen[sem.name] = value

    def count_up(self, inst):
        self.count += 1
        inst.then_inc(self.sem, 1)
        return (self.sem, self.count)

    def last(self):
        return (self.sem, self.count) if self.count else None


class Slot:
    def __init__(self, ap):
        self.ap, self.users = ap, []


class Ring:

    def __init__(self, aps):
        self.slots, self.n = [Slot(a) for a in aps], 0

    def take(self, writer):
        slot = self.slots[self.n % len(self.slots)]
        self.n += 1
        assert slot.users is not None, "still in use"
        writer.wait(slot.users)
        slot.users = None
        return slot


class Split:

    def __init__(self, hi, lo):
        self.hi, self.lo = hi, lo

    def __getitem__(self, key):
        return Split(self.hi[key], self.lo[key])


def weight_plan(w):
    plan = []

    def cols(name, mat, c0, n):
        src = mat[:, c0:c0 + n].rearrange("(k p) c -> p k c", p=P)
        plan.append((name, True, (DC, n), [((0, n), src)]))

    def rows(name, mat, k0, n=2):
        src = mat[k0 * P:(k0 + n) * P, :].rearrange("(k p) c -> p k c", p=P)
        plan.append((name, True, (n, D), [((0, D), src)]))

    w_in = w["w_in"]
    cols("dt", w_in, COL_DT, P)
    for i in range(4):
        cols("bc", w_in, COL_B + 256 * i, 256)
    for i in range(LC // 2):
        cols("lx", w_in, COL_LX + 256 * i, 256)
    for name in ("lru_w_r", "lru_w_i"):
        plan.append((name, False, (LC, P), [((0, P), w[name].rearrange("h i j -> i h j"))]))
    for i in range(8):
        cols("xs", w_in, COL_XBC + 256 * i, 256)
    for i in range(LC // 2):
        cols("ly", w_in, COL_LY + 256 * i, 256)
    for i in range(8):
        cols("gate", w_in, COL_GATE + 256 * i, 256)
    for g in range(GROUPS + 1):
        if g < GROUPS:
            for i in range(2):
                cols("z", w_in, COL_Z + 512 * g + 256 * i, 256)
        if g:
            for i in range(2):
                rows("out_ssm", w["w_out_ssm"], GC * (g - 1) + 2 * i)
    for i in range(LC // 2):
        rows("out_lru", w["w_out_lru"], 2 * i)
    for i in range(DC // 2):
        rows("out", w["w_out"], 2 * i)
    nf = FFN // 256
    for i in range(nf + 1):
        if i < nf:
            cols("ffn_gate", w["w_ffn_in"], 256 * i, 256)
            cols("ffn_up", w["w_ffn_in"], FFN + 256 * i, 256)
        if i:
            rows("ffn_out", w["w_ffn_out"], 2 * (i - 1))
    for l in range(DEPTH_2):
        w2 = w["w_in_2"][l]
        cols("ckv", w2, C_CKV, LATENT)
        ki = w2[:, C_KI:C_KI + HD].rearrange("(k p) c -> p k c", p=P)
        kiw = w2[:, C_KI:C_KI + HD + IDX_H].rearrange("(k p) c -> p k c", p=P)
        plan.append(("ki", True, (DC, 2 * HD + IDX_H), [((0, HD), ki), ((HD, 2 * HD + IDX_H), kiw)]))
        for i in range(2):
            cols("qi", w2, C_QI + 256 * i, 256)
        plan.append(("ukv", False, (2, DSA_W), [((0, DSA_W), w["dsa_w_uk_2"][l]), ((0, DSA_W), w["dsa_w_uv_2"][l])]))
        cols("dsa_q", w2, C_DSA, 256)
        for name, c in (("ret_k", 1), ("ret_q", 0), ("ret_v", 2), ("ret_g", 3)):
            cols(name, w2, C_RET + RET_W * c, 256)
        for name, c in (("dil_k", 1), ("dil_q", 0), ("dil_v", 2)):
            for i in range(2):
                cols(name, w2, C_DIL + DIL_W * c + 256 * i, 256)
        for i in range(DC // 2):
            rows("out_2", w["w_out_2"][l], 2 * i)
        nf = FF2 // 256
        for i in range(nf + 2):
            if i < nf:
                cols("up", w["w_up_2"][l], 256 * i, 256)
            if i >= 2:
                rows("down", w["w_down_2"][l], 2 * (i - 2))
    return plan


def build(nc, w, x_t, params, consts, consts_2, out_t, debug=None):
    ctx = ExitStack()
    with ctx:
        def sem(name):
            return ctx.enter_context(nc.semaphore(name))

        def sb(name, shape, dt=F32, stack=ctx):
            return stack.enter_context(nc.sbuf_tensor(name, shape, dt))

        pe = Engine(nc.tensor, sem("pe_done"))
        act = Engine(nc.scalar, sem("act_done"))
        vec = Engine(nc.vector, sem("vec_done"))
        pool = Engine(nc.gpsimd, sem("pool_done"))
        sp = Engine(nc.sync, sem("sp_unused"))
        dma_sems = [sem(f"tile_arrived_{i}") for i in range(RAW_SLOTS)]
        s_misc = sem("small_load_arrived")
        s_spill = sem("cs_spilled")
        s_bcast = sem("cs_broadcast")
        s_consts_2 = sem("consts_2_arrived")
        s_store = sem("output_stored")

        res = sb("residual", [P, DC, SEQ])
        act_hi = sb("act_hi", [P, 16, SEQ], F32R)
        act_lo = sb("act_lo", [P, 16, SEQ], F32R)
        acts = Split(act_hi, act_lo)
        raw = [sb(f"raw_{i}", [P, TILE]) for i in range(RAW_SLOTS)]
        w_hi = [sb(f"w_hi_{i}", [P, TILE], F32R) for i in range(SPLIT_SLOTS)]
        w_lo = [sb(f"w_lo_{i}", [P, TILE], F32R) for i in range(SPLIT_SLOTS)]
        par = sb("params", [P, N_PARAMS])
        n_consts = sum(n for _, n in CONSTS)
        con = sb("consts", [P, n_consts])
        tmps = Ring([sb(f"tmp_{i}", [P, 512])[:, :] for i in range(5)])
        rstd = sb("rstd", [P, SEQ])
        small = sb("small", [P, 96])

        banks = [ctx.enter_context(nc.psum_tensor(f"bank_{i}", [P, 512], F32)) for i in range(8)]
        low, high = Ring([b[:, :] for b in banks[:4]]), Ring([b[:, :] for b in banks[4:]])

        c, at = {}, 0
        for name, n in CONSTS:
            c[name] = con[:, at:at + n]
            at += n

        def param(name, i=0, n=1):
            a, width = PARAM_AT[name]
            assert i + n <= width
            return par[:, a + i:a + i + n]

        def tt(out, a, b, op, after=(), on=vec):
            on.wait(*after)
            return on.count_up(on.ops.tensor_tensor(out, a, b, op))

        def ts(out, a, s1, op0, s2=None, op1=None, after=(), on=vec):
            on.wait(*after)
            if op1 is None:
                return on.count_up(on.ops.tensor_scalar(out, a, s1, None, op0))
            return on.count_up(on.ops.tensor_scalar(out, a, s1, s2, op0, op1))

        def stt(out, a, s, b, op0, op1, after=(), accum=None):
            vec.wait(*after)
            return vec.count_up(nc.vector.scalar_tensor_tensor(out=out, in0=a, scalar=s, in1=b, op0=op0, op1=op1,
                                                             accum_out=accum))

        def fn(out, a, func, after=(), scale=1.0, bias=0.0, accum=None):
            act.wait(*after)
            return act.count_up(nc.scalar.activation(out, a, func, bias=bias, scale=scale, accum_out=accum))

        def copy(out, a, after=(), on=vec):
            if on is act:
                return fn(out, a, ACT.Copy, after)
            on.wait(*after)
            return on.count_up(on.ops.tensor_copy(out, a))

        def recip(out, a, after=()):
            vec.wait(*after)
            return vec.count_up(nc.vector.reciprocal(out, a))

        def mm(out, lhs, rhs, start=True, stop=True, after=()):
            pe.wait(*after)
            return nc.tensor.matmul(out, lhs, rhs, start=start, stop=stop, skip_group_check=True)

        def product(out, lhs, rhs, start, stop, after=()):
            pe.wait(*after)
            nc.tensor.matmul(out, lhs.hi, rhs.hi, start=start, stop=False, skip_group_check=True)
            nc.tensor.matmul(out, lhs.hi, rhs.lo, start=False, stop=False, skip_group_check=True)
            return nc.tensor.matmul(out, lhs.lo, rhs.hi, start=False, stop=stop, skip_group_check=True)

        def transpose(out, a, k=P, after=()):
            pe.wait(*after)
            return nc.tensor.transpose(out, a, c["ident"][0:k, 0:k])

        def split_into(k, n, src, after=(), lo_on=pool):
            hi, lo = act_hi[:, k:k + n, :], act_lo[:, k:k + n, :]
            used = [chunk_users[j] for j in range(k, k + n)]
            a = copy(hi, src, after=[*after, used], on=act)
            b = tt(lo, src, hi.bitcast(F32), ALU.subtract, after=[*after, used, a], on=lo_on)
            for j in range(k, k + n):
                chunk_users[j] = None
                chunk_ready[j] = [a, b]
            return [a, b]

        chunk_users = [None] * 16
        chunk_ready = [None] * 16

        nc.scalar.dma_start(par[:, :], params).then_inc(s_misc, 16)
        nc.scalar.dma_start(con[:, :], consts).then_inc(s_misc, 16)
        nc.scalar.dma_start(res[:, :, :], x_t).then_inc(s_misc, 16)
        loaded = (s_misc, 48)

        plan = weight_plan(w)
        dma_count = [0] * RAW_SLOTS
        arrived, tiles, raw_users = [None] * len(plan), [None] * len(plan), [None] * len(plan)
        split_users = [None] * len(plan)
        state = {"next_load": 0, "next_split": 0, "next_take": 0}

        def load_tile():
            i = state["next_load"]
            if i >= len(plan) or (i >= RAW_SLOTS and raw_users[i - RAW_SLOTS] is None):
                return
            state["next_load"] = i + 1
            slot = i % RAW_SLOTS
            _, _, (k, n), parts = plan[i]
            if i >= RAW_SLOTS:
                sp.wait(raw_users[i - RAW_SLOTS])
            tile = raw[slot][:, 0:k * n].rearrange("p (k c) -> p k c", k=k)
            for j, ((a, b), src) in enumerate(parts):
                dst = tile[:, j, :] if len(src.shape) == 2 else tile[:, :, a:b]
                nc.sync.dma_start(dst, src).then_inc(dma_sems[slot], 16)
                dma_count[slot] += 16
            arrived[i] = (dma_sems[slot], dma_count[slot])
            load_tile()

        def split_tile():
            i = state["next_split"]
            state["next_split"] = i + 1
            assert arrived[i] is not None
            _, is_split, (k, n), _ = plan[i]
            src = raw[i % RAW_SLOTS][:, 0:k * n]
            if not is_split:
                tiles[i] = (src.rearrange("p (k c) -> p k c", k=k), arrived[i])
                return
            slot = i % SPLIT_SLOTS
            free = split_users[i - SPLIT_SLOTS] if i >= SPLIT_SLOTS else None
            hi, lo = w_hi[slot][:, 0:k * n], w_lo[slot][:, 0:k * n]
            a = copy(hi, src, after=[arrived[i], free], on=act)
            b = tt(lo, src, hi.bitcast(F32), ALU.subtract, after=[arrived[i], free, a], on=vec)
            raw_users[i] = [a, b]
            tiles[i] = (Split(hi.rearrange("p (k c) -> p k c", k=k), lo.rearrange("p (k c) -> p k c", k=k)), [a, b])
            load_tile()

        def take(name):
            i = state["next_take"]
            state["next_take"] = i + 1
            assert plan[i][0] == name, (plan[i][0], name)
            while state["next_split"] < min(i + SPLIT_SLOTS, state["next_load"]):
                split_tile()
            return (i, *tiles[i])

        def used(i, token):
            split_users[i] = token
            if not plan[i][1]:
                raw_users[i] = token
                load_tile()

        load_tile()

        background = []

        def advance(n=1):
            for _ in range(n):
                for g in list(background):
                    if next(g, "end") == "end":
                        background.remove(g)

        def finish(*gens):
            while any(g in background for g in gens):
                advance()

        def up(name, base, ring, evacuate, width=256):
            i, tile, ready = take(name)
            bank = ring.take(pe)
            pe.wait(ready)
            for m in range(width // P):
                for k in range(DC):
                    inst = product(bank.ap[:, m * SEQ:(m + 1) * SEQ], tile[:, k, m * P:(m + 1) * P],
                                   acts[:, base + k, :], k == 0, k == DC - 1, after=[chunk_ready[base + k]])
            token = pe.count_up(inst)
            for k in range(DC):
                chunk_users[base + k] = token
            used(i, token)
            evacuate(bank, token)
            advance()

        def up_tokens(name, base, ring, evacuate, lo=0, width=256):
            i, tile, ready = take(name)
            bank = ring.take(pe)
            pe.wait(ready)
            for t in range(TT):
                for k in range(DC):
                    inst = product(bank.ap[:, t * width:(t + 1) * width], acts[:, base + k, t * P:(t + 1) * P],
                                   tile[:, k, lo:lo + width], k == 0, k == DC - 1, after=[chunk_ready[base + k]])
            token = pe.count_up(inst)
            for k in range(DC):
                chunk_users[base + k] = token
            used(i, token)
            evacuate(bank, token)
            advance()

        def down(name, chunks, ring_banks, first, last):
            i, tile, ready = take(name)
            pe.wait(ready)
            tokens = []
            for b, bank in enumerate(ring_banks):
                for j, k in enumerate(chunks):
                    for m in range(2):
                        inst = product(bank.ap[:, m * SEQ:(m + 1) * SEQ],
                                       tile[:, j, (2 * b + m) * P:(2 * b + m + 1) * P], acts[:, k, :],
                                       first and j == 0 and m == 0, last and j == 1, after=[chunk_ready[k]])
                tokens.append(pe.count_up(inst) if last or b == len(ring_banks) - 1 else None)
            for k in chunks:
                chunk_users[k] = tokens[-1]
            used(i, tokens[-1])
            advance()
            return tokens

        def feature_mean(bank_ap, square, matrix, start, stop, after):
            return mm(bank_ap, matrix, square, start, stop, after=after)

        def rms_scale(mean, out, after):
            a = fn(out, mean, ACT.Sqrt, after=after, bias=c["eps"])
            return recip(out, out, after=[a]), a

        res_ready = [loaded] * DC

        def norm_to(base, weight, w0, ring, write=None):
            bank = ring.take(pe)
            for j in range(DC // 2):
                sq = tmps.take(act)
                a = fn(sq.ap, res[:, 2 * j:2 * j + 2, :], ACT.Square, after=[res_ready[2 * j], res_ready[2 * j + 1]])
                for m in range(2):
                    inst = feature_mean(bank.ap[:, 0:SEQ], sq.ap[:, m * SEQ:(m + 1) * SEQ], c["mean_d"],
                                        j == 0 and m == 0, j == DC // 2 - 1 and m == 1, after=[a, loaded])
                sq.users = [pe.count_up(inst)]
            scale_ready, read = rms_scale(bank.ap[:, 0:SEQ], rstd[:, :], after=[*sq.users, *norm_users])
            bank.users = [read]
            norm_users.clear()
            for j in range(DC // 2):
                n = tmps.take(vec) if write is None else None
                for m in range(2):
                    k = 2 * j + m
                    dst = n.ap[:, m * SEQ:(m + 1) * SEQ] if n else write[:, k, :]
                    t = stt(dst, res[:, k, :], param(weight, w0 + k), rstd[:, :], ALU.mult, ALU.mult,
                            after=[scale_ready])
                if n:
                    n.users = split_into(base + 2 * j, 2, n.ap.rearrange("p (k t) -> p k t", k=2), after=[t])
            norm_users.append(t)
            return t

        norm_users = []

        one = ExitStack()
        xbc = sb("xbc", [P, XBC // P, SEQ], stack=one)
        lru_u = sb("lru_u", [P, LC, SEQ], stack=one)
        lru_ab = sb("lru_ab", [P, 2 * LC, SEQ], stack=one)
        lru_a, lru_b = lru_ab[:, 0:LC, :], lru_ab[:, LC:2 * LC, :]
        gates = lru_ab[:, 0:2 * DC, :]
        cs_all = sb("cs_all", [P, HPG, SEQ], stack=one)
        xdt = sb("xdt", [P, TT, GC * P], stack=one)
        z_silu = sb("z_silu", [P, GC, SEQ], stack=one)
        cb_mask = sb("cb_mask", [P, KQ], stack=one)
        cs_dram = nc.dram_tensor("cs_scratch", (HEADS, SEQ), F32, kind="Internal").ap()

        a0, wd = PARAM_AT["conv_w"]
        half = ts(par[:, a0:a0 + wd + XBC // P], par[:, a0:a0 + wd + XBC // P], 0.5, ALU.mult, after=[loaded])
        a0 = PARAM_AT["b_r"][0]
        half_b = ts(par[:, a0:a0 + 2 * LC], par[:, a0:a0 + 2 * LC], 0.5, ALU.mult, after=[loaded])
        a0 = PARAM_AT["b_gate"][0]
        half_g = ts(par[:, a0:a0 + 2 * DC], par[:, a0:a0 + 2 * DC], 0.5, ALU.mult, after=[loaded])

        def softplus(out, x, s1, s2, sign, after):
            t = ts(s1, x, -1.0, ALU.mult, after=after)
            t = tt(s1, s1, x, ALU.min, after=[t])
            t = fn(s1, s1, ACT.Exp, after=[t])
            t = ts(s2, s1, 1.0, ALU.add, after=[t])
            l = fn(out, s2, ACT.Ln, after=[t, *after])
            u = stt(s1, s2, -1.0, s1, ALU.add, ALU.subtract, after=[t])
            r = recip(s2, s2, after=[l, u])
            t = tt(s1, s1, s2, ALU.mult, after=[r])
            t = tt(out, out, s1, ALU.subtract, after=[t, l])
            t = ts(s1, x, sign, ALU.mult, 0.0, ALU.max, after=[t])
            return tt(out, out, s1, ALU.add, after=[t])

        sp_lam = small[:, 0:LC]
        lam_ready = softplus(sp_lam, param("lam", 0, LC), small[:, 16:16 + LC], small[:, 32:32 + LC], -1.0, [loaded])
        lam_ready = ts(sp_lam, sp_lam, -LRU_C / 2, ALU.mult, after=[lam_ready])
        neg_a = small[0:HEADS, 48:49]
        t = fn(neg_a, param("a_log")[0:HEADS], ACT.Exp, after=[loaded])
        neg_a_ready = ts(neg_a, neg_a, -1.0, ALU.mult, after=[t])

        norm_to(0, "norm1", 0, high)

        dt = sb("dt", [HEADS, SEQ], stack=one)
        cs = sb("cs", [HEADS, SEQ], stack=one)
        dt_tok = sb("dt_tok", [P, TT, HEADS], stack=one)
        neg_cs = sb("neg_cs", [P, TT, HEADS], stack=one)
        ssd_ready = {}

        def evacuate_dt(bank, token):
            x, s1, s2 = tmps.take(vec), tmps.take(vec), tmps.take(vec)
            x_, s1_, s2_ = (s.ap[0:HEADS, 0:SEQ] for s in (x, s1, s2))
            t = ts(x_, bank.ap[0:HEADS, 0:SEQ], param("dt_bias")[0:HEADS], ALU.add, after=[token, loaded])
            bank.users = [t]
            t = softplus(dt[:, :], x_, s1_, s2_, 1.0, [t, act.last()])
            u = ts(s1_, dt[:, :], neg_a, ALU.mult, after=[t, neg_a_ready])
            v = nc.vector.memset(s2_, 1.0)
            v = vec.count_up(v)
            vec.wait(u, v)
            t = vec.count_up(nc.vector.tensor_tensor_scan(cs[:, :], s2_, s1_, 0.0, ALU.mult, ALU.add))
            for s in (x, s1, s2):
                s.users = [t]
            act.wait(t)
            nc.scalar.dma_start(cs_dram, cs[:, :]).then_inc(s_spill, 16)
            bank = high.take(pe)
            for i, src in enumerate((dt, cs)):
                for tile in range(TT):
                    j = (i * TT + tile) * HEADS
                    inst = transpose(bank.ap[:, j:j + HEADS], src[:, tile * P:(tile + 1) * P], HEADS, after=[t])
            token = pe.count_up(inst)
            view = bank.ap[:, 0:4 * HEADS].rearrange("p (i t h) -> p i t h", i=2, t=TT)
            a = copy(dt_tok[:, :, :], view[:, 0], after=[token])
            b = ts(neg_cs[:, :, :], view[:, 1], -1.0, ALU.mult, after=[token])
            bank.users = [b]
            ssd_ready["dt"] = [a, b]

        up("dt", 0, low, evacuate_dt, width=P)

        def conv(bank, token, out, w_name, w_stride, b_name, k0):
            for m in range(2):
                t = fn(out[:, m, :], bank.ap[:, m * SEQ:(m + 1) * SEQ], ACT.Identity, after=[token, half, loaded],
                       scale=param(w_name, 3 * w_stride + k0 + m), bias=param(b_name, k0 + m))
            tokens = [t, t]
            for j in (2, 1, 0):
                d = 3 - j
                for m in range(2):
                    u = bank.ap[:, m * SEQ:(m + 1) * SEQ]
                    tokens[m] = stt(out[:, m, d:SEQ], u[:, 0:SEQ - d], param(w_name, j * w_stride + k0 + m),
                                    out[:, m, d:SEQ], ALU.mult, ALU.add, after=[tokens[m]])
            bank.users = [tokens[1]]
            return tokens[1]

        xbc_ready = [None] * (XBC // P)

        def evacuate_xbc(k0):
            def go(bank, token):
                t = conv(bank, token, xbc[:, k0:k0 + 2, :], "conv_w", XBC // P, "conv_b", k0)
                th = tmps.take(act)
                a = fn(th.ap, xbc[:, k0:k0 + 2, :], ACT.Tanh, after=[t])
                b = stt(xbc[:, k0:k0 + 2, :], th.ap.rearrange("p (k t) -> p k t", k=2), 1.0, xbc[:, k0:k0 + 2, :],
                        ALU.add, ALU.mult, after=[a])
                th.users = [b]
                xbc_ready[k0] = xbc_ready[k0 + 1] = b
            return go

        for i in range(4):
            up("bc", 0, low, evacuate_xbc(16 + 2 * i))

        u_ready = [None] * LC

        def evacuate_lx(k0):
            def go(bank, token):
                u_ready[k0] = u_ready[k0 + 1] = conv(bank, token, lru_u[:, k0:k0 + 2, :], "lconv_w", LC, "lconv_b", k0)
            return go

        for i in range(LC // 2):
            up("lx", 0, low, evacuate_lx(2 * i))

        i_r, w_r, r_ready = take("lru_w_r")
        i_i, w_i, i_ready = take("lru_w_i")
        ab_ready = [None] * LC
        for h in range(LC):
            bank = high.take(pe)
            mm(bank.ap[:, 0:SEQ], w_r[:, h, :], lru_u[:, h, :], after=[r_ready, u_ready[h]])
            token = pe.count_up(mm(bank.ap[:, SEQ:512], w_i[:, h, :], lru_u[:, h, :], after=[i_ready]))
            th = tmps.take(act)
            r, g = th.ap[:, 0:SEQ], th.ap[:, SEQ:512]
            a1 = fn(r, bank.ap[:, 0:SEQ], ACT.Tanh, after=[token, half_b], scale=0.5, bias=param("b_r", h))
            a2 = fn(g, bank.ap[:, SEQ:512], ACT.Tanh, scale=0.5, bias=param("b_i", h))
            bank.users = [a2]
            la = ts(r, r, 1.0, ALU.add, sp_lam[:, h:h + 1], ALU.mult, after=[a1, lam_ready])
            e = fn(lru_a[:, h, :], r, ACT.Exp, after=[la])
            tl = fn(r, r, ACT.Tanh, after=[la, e])
            sq = tmps.take(vec)
            s = sq.ap[:, 0:SEQ]
            v = tt(s, lru_a[:, h, :], lru_a[:, h, :], ALU.mult, after=[e])
            v = stt(s, s, 1.0, r, ALU.add, ALU.mult, after=[v, tl])
            v2 = ts(lru_b[:, h, :], s, -1.0, ALU.mult, after=[v])
            v3 = stt(g, g, 1.0, lru_u[:, h, :], ALU.add, ALU.mult, after=[a2])
            v4 = ts(lru_u[:, h, :], g, 0.5, ALU.mult, after=[v3])
            th.users, sq.users = [v4], [v2]
            ab_ready[h] = v4
        used(i_r, token)
        used(i_i, token)

        lru_done = [None] * LC

        def lru_scan():
            root = fn(lru_b, lru_b, ACT.Sqrt, after=[ab_ready[-1]])
            yield
            for h in range(LC):
                t = tt(lru_b[:, h, :], lru_b[:, h, :], lru_u[:, h, :], ALU.mult, after=[root])
                vec.wait(t)
                lru_done[h] = vec.count_up(nc.vector.tensor_tensor_scan(lru_u[:, h, :], lru_a[:, h, :], lru_b[:, h, :],
                                                                      0.0, ALU.mult, ALU.add))
                if h % 2:
                    yield

        scan = lru_scan()
        background.append(scan)

        y_ready = [None] * GROUPS
        cs_read, xdt_read, cb_read = [], [], []

        def ssd(g):
            act.wait((s_spill, 16), cs_read)
            nc.scalar.dma_start(cs_all[:, :, :], cs_dram[g * HPG:(g + 1) * HPG, :].partition_broadcast(P)).then_inc(s_bcast, 16)
            cs_here = (s_bcast, 16 * (g + 1))
            bm, cm = xbc[:, 16 + g, :], xbc[:, 20 + g, :]
            bank = high.take(pe)
            mm(bank.ap[:, 0:SEQ], bm[:, 0:P], cm, after=[xbc_ready[16 + g], xbc_ready[20 + g]])
            token = pe.count_up(mm(bank.ap[:, SEQ:KQ], bm[:, P:SEQ], cm[:, P:SEQ]))
            cb = tt(cb_mask[:, :], bank.ap[:, 0:KQ], c["tri"], ALU.mult, after=[token, cb_read])
            bank.users = [cb]
            cb_read.clear()
            x_ready = [xbc_ready[GC * g + k] for k in range(GC)]
            xdt_ready = []
            for t in range(TT):
                bank = high.take(pe)
                for k in range(GC):
                    inst = transpose(bank.ap[:, k * P:(k + 1) * P], xbc[:, GC * g + k, t * P:(t + 1) * P],
                                     after=[x_ready[k]])
                token = pe.count_up(inst)
                v = tt(xdt[:, t, :].rearrange("p (h e) -> p h e", e=HD), bank.ap.rearrange("p (h e) -> p h e", e=HD),
                       dt_tok[:, t, g * HPG:(g + 1) * HPG].unsqueeze(2).broadcast_to([P, HPG, HD]), ALU.mult,
                       after=[token, xdt_read, ssd_ready["dt"]])
                bank.users = [v]
                xdt_ready.append(v)
            xdt_read.clear()
            yield
            m_ready = {}

            def decays(h):
                e = tmps.take(vec)
                hh = g * HPG + h
                ts(e.ap[:, 0:SEQ], cs_all[:, h, :], neg_cs[:, 0, hh:hh + 1], ALU.add, 0.0, ALU.min,
                   after=[cs_here, ssd_ready["dt"]])
                d = ts(e.ap[:, SEQ:KQ], cs_all[:, h, P:SEQ], neg_cs[:, 1, hh:hh + 1], ALU.add, 0.0, ALU.min)
                a = fn(e.ap[:, 0:KQ], e.ap[:, 0:KQ], ACT.Exp, after=[d])
                v = tt(e.ap[:, 0:KQ], e.ap[:, 0:KQ], cb_mask[:, :], ALU.mult, after=[a, cb])
                m_ready[h] = (e, v)
                return d, v

            for pair in range(0, HPG, 2):
                for h in (pair, pair + 1):
                    a, v = decays(h)
                if pair == HPG - 2:
                    cs_read.append(a)
                    cb_read.append(v)
                yield
                bank = high.take(pe)
                for h in (pair, pair + 1):
                    e, v = m_ready[h]
                    rows = slice((h % 2) * HD, (h % 2 + 1) * HD)
                    mm(bank.ap[rows, 0:SEQ], xdt[:, 0, h * HD:(h + 1) * HD], e.ap[:, 0:SEQ], True, False,
                       after=[v, xdt_ready])
                    inst = mm(bank.ap[rows, P:SEQ], xdt[:, 1, h * HD:(h + 1) * HD], e.ap[:, SEQ:KQ], False, True)
                    e.users = [pe.count_up(inst)]
                token = e.users[0]
                k = GC * g + pair // 2
                xbc_y = stt(xbc[:, k, :], xbc[:, k, :], param("d_skip", k), bank.ap[:, 0:SEQ], ALU.mult, ALU.add,
                            after=[token])
                bank.users = [xbc_y]
            xdt_read.append(token)
            y_ready[g] = xbc_y
            yield

        def all_ssd():
            for g in range(GROUPS):
                yield from ssd(g)

        for i in range(8):
            up("xs", 0, low, evacuate_xbc(2 * i))
            if i == 3:
                ssd_work = all_ssd()
                background.append(ssd_work)

        finish(scan)
        lru_out = [None] * LC

        def evacuate_ly(k0):
            def go(bank, token):
                q = tmps.take(act)
                x2 = bank.ap
                a = fn(q.ap, x2, ACT.Square, after=[token])
                v = ts(q.ap, q.ap, 0.044715, ALU.mult, 1.0, ALU.add, after=[a])
                v = tt(q.ap, q.ap, x2, ALU.mult, after=[v])
                a = fn(q.ap, q.ap, ACT.Tanh, after=[v], scale=float(np.sqrt(2 / np.pi)))
                v = stt(q.ap, q.ap, 1.0, x2, ALU.add, ALU.mult, after=[a])
                bank.users = [v]
                hs = lru_u[:, k0:k0 + 2, :]
                v = stt(hs, q.ap.rearrange("p (k t) -> p k t", k=2), 0.5, hs, ALU.mult, ALU.mult,
                        after=[v, lru_done[k0], lru_done[k0 + 1]])
                q.users = [v]
                lru_out[k0] = lru_out[k0 + 1] = v
            return go

        for i in range(LC // 2):
            up("ly", 0, low, evacuate_ly(2 * i))

        gate_ready = [None] * (2 * DC)

        def evacuate_gate(k0):
            def go(bank, token):
                for m in range(2):
                    a = fn(gates[:, k0 + m, :], bank.ap[:, m * SEQ:(m + 1) * SEQ], ACT.Tanh,
                           after=[token, half_g, lru_done], scale=0.5, bias=param("b_gate", k0 + m))
                bank.users = [a]
                g = gates[:, k0:k0 + 2, :]
                gate_ready[k0] = gate_ready[k0 + 1] = ts(g, g, 0.5, ALU.mult, 0.5, ALU.add, after=[a])
            return go

        for i in range(8):
            up("gate", 0, low, evacuate_gate(2 * i))
        finish(ssd_work)

        z_ready = [None] * GC
        z_read = []

        def evacuate_z(k0):
            def go(bank, token):
                th = tmps.take(act)
                a = fn(th.ap, bank.ap, ACT.Tanh, after=[token], scale=0.5)
                j = k0 % GC
                v = stt(th.ap, th.ap, 1.0, bank.ap, ALU.add, ALU.mult, after=[a])
                bank.users = [v]
                v = stt(z_silu[:, j:j + 2, :], th.ap.rearrange("p (k t) -> p k t", k=2), 0.5, xbc[:, k0:k0 + 2, :],
                        ALU.mult, ALU.mult, after=[v, y_ready[k0 // GC], z_read])
                th.users = [v]
                z_ready[j] = z_ready[j + 1] = v
            return go

        g_rstd = [sb(f"g_rstd_{i}", [P, SEQ], stack=one) for i in range(2)]

        def group_norm(g):
            bank = low.take(pe)
            for j in range(GC // 2):
                sq = tmps.take(act)
                a = fn(sq.ap, z_silu[:, 2 * j:2 * j + 2, :], ACT.Square, after=[z_ready[2 * j]])
                for m in range(2):
                    inst = feature_mean(bank.ap[:, 0:SEQ], sq.ap[:, m * SEQ:(m + 1) * SEQ], c["mean_group"],
                                        j == 0 and m == 0, j == 1 and m == 1, after=[a])
                sq.users = [pe.count_up(inst)]
            scale, read = rms_scale(bank.ap[:, 0:SEQ], g_rstd[g % 2][:, :], after=[*sq.users, vec.last()])
            bank.users = [read]
            z_read.clear()
            for j in range(GC // 2):
                n = tmps.take(vec)
                for m in range(2):
                    k = GC * g + 2 * j + m
                    t = stt(n.ap[:, m * SEQ:(m + 1) * SEQ], z_silu[:, 2 * j + m, :], param("norm_w", k),
                            g_rstd[g % 2][:, :], ALU.mult, ALU.mult, after=[scale])
                n.users = split_into(8 + GC * (g % 2) + 2 * j, 2, n.ap.rearrange("p (k t) -> p k t", k=2), after=[t])
            z_read.append(t)

        ssm_acc = None
        for g in range(GROUPS + 1):
            if g < GROUPS:
                for i in range(2):
                    up("z", 0, low, evacuate_z(GC * g + 2 * i))
                group_norm(g)
            if g:
                if g == 1:
                    ssm_acc = [high.take(pe) for _ in range(4)]
                for i in range(2):
                    k = 8 + GC * ((g - 1) % 2) + 2 * i
                    tokens = down("out_ssm", (k, k + 1), ssm_acc, g == 1 and i == 0, g == GROUPS and i == 1)
            if g == GROUPS - 1:
                for k in range(0, 8, 2):
                    split_into(k, 2, lru_u[:, k:k + 2, :], after=[lru_out[k]])
            if g == GROUPS:
                split_into(8, 2, lru_u[:, 8:10, :], after=[lru_out[8]])
        for b in range(4):
            g = gates[:, 2 * b:2 * b + 2, :]
            t = tt(g, g, ssm_acc[b].ap.rearrange("p (k t) -> p k t", k=2), ALU.mult, after=[tokens[b], gate_ready[2 * b]])
            ssm_acc[b].users = [t]
            gate_ready[2 * b] = t
        acc = [low.take(pe) for _ in range(4)]
        for i in range(LC // 2):
            tokens = down("out_lru", (2 * i, 2 * i + 1), acc, i == 0, i == LC // 2 - 1)
        for b in range(4):
            g = gates[:, DC + 2 * b:DC + 2 * b + 2, :]
            t = tt(g, g, acc[b].ap.rearrange("p (k t) -> p k t", k=2), ALU.mult, after=[tokens[b], gate_ready[DC + 2 * b]])
            acc[b].users = [t]
            t = tt(g, g, gates[:, 2 * b:2 * b + 2, :], ALU.add, after=[t, gate_ready[2 * b]])
            split_into(2 * b, 2, g, after=[t])

        def project_to_residual(name, chunks_of, n, ring, before=None):
            banks_ = [ring.take(pe) for _ in range(4)]
            for i in range(n):
                if before:
                    before(i)
                tokens = down(name, chunks_of(i), banks_, i == 0, i == n - 1)
            add_residual(banks_, tokens)

        def add_residual(banks_, tokens):
            for b in range(4):
                r = res[:, 2 * b:2 * b + 2, :]
                t = tt(r, r, banks_[b].ap.rearrange("p (k t) -> p k t", k=2), ALU.add,
                       after=[tokens[b], res_ready[2 * b], norm_users, act.last() if b == 0 else None])
                banks_[b].users = [t]
                res_ready[2 * b] = res_ready[2 * b + 1] = t

        project_to_residual("out", lambda i: (2 * i, 2 * i + 1), DC // 2, high)

        norm_to(8, "norm2", 0, low)
        acc = [high.take(pe) for _ in range(4)]
        silu_gate = {}

        def evacuate_ffn_gate(bank, token):
            th, s = tmps.take(act), tmps.take(vec)
            a = fn(th.ap, bank.ap, ACT.Tanh, after=[token], scale=0.5)
            v = stt(s.ap, th.ap, 1.0, bank.ap, ALU.add, ALU.mult, after=[a])
            th.users, bank.users = [v], [v]
            silu_gate["s"], silu_gate["v"] = s, v

        def evacuate_ffn_up(k):
            def go(bank, token):
                s = silu_gate["s"]
                v = stt(s.ap, s.ap, 0.5, bank.ap, ALU.mult, ALU.mult, after=[token, silu_gate["v"]])
                bank.users = [v]
                s.users = split_into(k, 2, s.ap.rearrange("p (k t) -> p k t", k=2), after=[v])
            return go

        nf = FFN // 256
        for i in range(nf + 1):
            if i < nf:
                up("ffn_gate", 8, low, evacuate_ffn_gate)
                up("ffn_up", 8, low, evacuate_ffn_up(2 * (i % 4)))
            if i:
                k = 2 * ((i - 1) % 4)
                tokens = down("ffn_out", (k, k + 1), acc, i == 1, i == nf)
        add_residual(acc, tokens)
        t = norm_to(0, "norm_f", 0, low, write=res)
        res_ready[:] = [t] * DC
        one_done = [vec.last(), act.last(), pe.last(), pool.last()]
        one.close()

        two = ExitStack()
        ctx.enter_context(two)
        con2 = sb("consts_2", [P, sum(n for _, n in CONSTS_2)], stack=two)
        sp.wait(one_done)
        nc.sync.dma_start(con2[:, :], consts_2).then_inc(s_consts_2, 16)
        loaded2 = (s_consts_2, 16)
        at = 0
        for name, n in CONSTS_2:
            c[name] = con2[:, at:at + n]
            at += n
        for e in (vec, act, pe, pool):
            e.wait(one_done)
        ckv_t = sb("ckv_t", [P, SEQ], stack=two)
        ki_t = sb("ki_t", [P, SEQ], stack=two)
        w_idx = sb("w_idx", [P, TT, IDX_H], stack=two)
        qi_t = sb("qi_t", [P, IDX_H * HD // P, SEQ], stack=two)
        dq_t = sb("dq_t", [P, 2, SEQ], stack=two)
        dk_t = sb("dk_t", [P, 2, SEQ], stack=two)
        dv = sb("dv", [P, TT, DSA_W], stack=two)
        relu = Ring([sb(f"relu_{i}", [P, 512], stack=two)[:, :] for i in range(2)])
        score = sb("score", [P, KQ], stack=two)
        work = [sb(f"work_{i}", [P, KQ], stack=two) for i in range(2)]
        keep = sb("keep", [P, KQ], stack=two)
        top8 = sb("top8", [P, 2, 8], stack=two)
        rq_t = sb("rq_t", [P, 2, SEQ], stack=two)
        rk_t = sb("rk_t", [P, 2, SEQ], stack=two)
        rv = sb("rv", [P, TT, RET_W], stack=two)
        rg_t = sb("rg_t", [P, 2, SEQ], stack=two)
        ro_t = sb("ro_t", [P, 2, SEQ], stack=two)
        lq_t = sb("lq_t", [P, 4, SEQ], stack=two)
        lk_t = sb("lk_t", [P, 4, SEQ], stack=two)
        lv = sb("lv", [P, TT, DIL_W], stack=two)
        probs = Ring([sb(f"probs_{i}", [P, KQ], stack=two)[:, :] for i in range(6)])
        probs_t = Ring([sb(f"probs_t_{i}", [P, KQ], stack=two)[:, :] for i in range(4)])
        stats = Ring([sb(f"stats_{i}", [P, 8], stack=two)[:, :] for i in range(6)])
        PAIRS = ((0, 0, P), (1, P, KQ))

        def value_product(o, pt, v0, v1, after):
            mm(o, v0, pt[:, 0:SEQ], True, False, after=after)
            return mm(o[:, P:SEQ], v1, pt[:, SEQ:KQ], False, True)

        def head_rows(t, h):
            return t[(h % 2) * HD:(h % 2 + 1) * HD, h // 2, :]

        def attention(n_heads, q, k, v, additive, count, ready, out_chunk):
            for h0 in range(0, n_heads, 2):
                work_ = []
                for h in (h0, h0 + 1):
                    bank = high.take(pe)
                    qh, kh = head_rows(q, h), head_rows(k, h)
                    mm(bank.ap[:, 0:P], qh[:, 0:P], kh[:, 0:P], after=ready)
                    token = pe.count_up(mm(bank.ap[:, P:KQ], qh[:, P:SEQ], kh[:, :]))
                    p, st = probs.take(vec), stats.take(vec)
                    t = stt(p.ap, bank.ap[:, 0:KQ], SCALE, additive, ALU.mult, ALU.add, after=[token, *ready, loaded2])
                    bank.users = [t]
                    vec.wait(t)
                    for i, a, b in PAIRS:
                        t = vec.count_up(nc.vector.tensor_reduce(st.ap[:, i:i + 1], p.ap[:, a:b], AX_X, ALU.max, negate=True))
                    work_.append((p, st, t))
                yield
                normed = []
                for p, st, t in work_:
                    for i, a, b in PAIRS:
                        e = fn(p.ap[:, a:b], p.ap[:, a:b], ACT.Exp, after=[t], bias=st.ap[:, i:i + 1],
                               accum=st.ap[:, 2 + i:3 + i] if count is None else None)
                    if count is not None:
                        for i, a, b in PAIRS:
                            e = stt(p.ap[:, a:b], p.ap[:, a:b], 1.0, count[:, a:b], ALU.mult, ALU.mult, after=[e],
                                    accum=st.ap[:, 2 + i:3 + i])
                    r_ = recip(st.ap[:, 4:6], st.ap[:, 2:4], after=[e])
                    for i, a, b in PAIRS:
                        n = ts(p.ap[:, a:b], p.ap[:, a:b], st.ap[:, 4 + i:5 + i], ALU.mult, after=[r_])
                    st.users = [n]
                    normed.append(n)
                yield
                turned = []
                for (p, _, _), n in zip(work_, normed):
                    bank = high.take(pe)
                    for j in range(3):
                        inst = transpose(bank.ap[:, j * P:(j + 1) * P], p.ap[:, j * P:(j + 1) * P], after=[n])
                    token = pe.count_up(inst)
                    p.users = [token]
                    pt = probs_t.take(act)
                    cp = fn(pt.ap, bank.ap[:, 0:KQ], ACT.Copy, after=[token])
                    bank.users = [cp]
                    turned.append((pt, cp))
                yield
                bank = high.take(pe)
                for h, (pt, cp) in zip((h0, h0 + 1), turned):
                    o = bank.ap[(h % 2) * HD:(h % 2 + 1) * HD, 0:SEQ]
                    token = pe.count_up(value_product(o, pt.ap, v[:, 0, h * HD:(h + 1) * HD],
                                                    v[:, 1, h * HD:(h + 1) * HD], [cp, ready]))
                    pt.users = [token]
                o = tmps.take(vec)
                t = copy(o.ap[:, 0:SEQ], bank.ap[:, 0:SEQ], after=[token])
                bank.users = [t]
                o.users = split_into(out_chunk + h0 // 2, 1, o.ap[:, 0:SEQ].unsqueeze(1), after=[t])

        def plain(dst, after=(), scale=None, on=act):
            def go(bank, token):
                src = bank.ap.rearrange("p (k t) -> p k t", k=2)
                bank.users = [copy(dst, src, after=[token, *after], on=on)]
                ready_of[0] = bank.users[0]
            return go

        ready_of = [None]

        for l in range(DEPTH_2):
            base = 8
            prev = [vec.last(), act.last(), pe.last(), pool.last()]
            for e in (vec, act, pe, pool):
                e.wait(prev)
            norm_to(base, "attn", DC * l, high)
            r = {}

            def evacuate_ckv(bank, token):
                sq = tmps.take(act)
                cp = fn(ckv_t[:, :], bank.ap[:, 0:SEQ], ACT.Copy, after=[token])
                a = fn(sq.ap[:, 0:SEQ], bank.ap[:, 0:SEQ], ACT.Square)
                bank.users = [a]
                r["sq"], r["a"], r["cp"] = sq, a, cp

            up("ckv", base, low, evacuate_ckv, width=LATENT)

            def finish_ckv():
                sq = r["sq"]
                bank = high.take(pe)
                token = pe.count_up(feature_mean(bank.ap[:, 0:SEQ], sq.ap[:, 0:SEQ], c["mean_latent"], True, True, after=[r["a"]]))
                scale, read = rms_scale(bank.ap[:, 0:SEQ], sq.ap[:, SEQ:512], after=[token])
                bank.users = [read]
                r["ckv"] = stt(ckv_t[:, :], ckv_t[:, :], param("kvn", l), sq.ap[:, SEQ:512], ALU.mult, ALU.mult,
                               after=[scale, r["cp"]])
                sq.users = [r["ckv"]]

            i, tile, ready = take("ki")
            bank = low.take(pe)
            pe.wait(ready)
            for k in range(DC):
                product(bank.ap[:, 0:SEQ], tile[:, k, 0:2 * HD], acts[:, base + k, :], k == 0, k == DC - 1)
            for t in range(TT):
                for k in range(DC):
                    inst = product(bank.ap[:, SEQ + t * IDX_H:SEQ + (t + 1) * IDX_H],
                                   acts[:, base + k, t * P:(t + 1) * P], tile[:, k, 2 * HD:2 * HD + IDX_H],
                                   k == 0, k == DC - 1)
            token = pe.count_up(inst)
            used(i, token)
            a = fn(ki_t[:, :], bank.ap[:, 0:SEQ], ACT.Copy, after=[token])
            b = fn(w_idx[:, :, :], bank.ap[:, SEQ:SEQ + TT * IDX_H].rearrange("p (t h) -> p t h", t=TT), ACT.Copy,
                   scale=IDX_SCALE)
            bank.users = [b]
            idx_ready = [a, b]
            advance()
            finish_ckv()

            for j in range(2):
                up("qi", base, low, plain(qi_t[:, 2 * j:2 * j + 2, :]))
                idx_ready.append(ready_of[0])

            i, ukv, ready = take("ukv")
            bank, bank2 = high.take(pe), high.take(pe)
            for m in range(2):
                inst = mm(bank.ap[:, m * SEQ:(m + 1) * SEQ], ukv[:, 0, m * P:(m + 1) * P], ckv_t[:, :],
                          after=[ready, r["ckv"]])
            t1 = pe.count_up(inst)
            for t in range(TT):
                inst = mm(bank2.ap[:, t * DSA_W:(t + 1) * DSA_W], ckv_t[:, t * P:(t + 1) * P], ukv[:, 1, :])
            t2 = pe.count_up(inst)
            used(i, t2)
            a = copy(dk_t[:, :, :], bank.ap.rearrange("p (k t) -> p k t", k=2), after=[t1])
            b = copy(dv[:, :, :], bank2.ap.rearrange("p (k t) -> p k t", k=2), after=[t2])
            bank.users, bank2.users = [a], [b]
            dsa_ready = [a, b]

            def select():
                acc_t = None
                for q, a, b in PAIRS:
                    n = b - a
                    per = 512 // n
                    halves = [h for half in (0, 1) for h in range(half, IDX_H, 2)]
                    for h0 in range(0, IDX_H, per):
                        bank = high.take(pe)
                        for j, h in enumerate(halves[h0:h0 + per]):
                            inst = mm(bank.ap[:, j * n:(j + 1) * n], head_rows(qi_t, h)[:, q * P:(q + 1) * P],
                                      ki_t[(h % 2) * HD:(h % 2 + 1) * HD, 0:n], after=idx_ready)
                        token = pe.count_up(inst)
                        rl = relu.take(act)
                        x = fn(rl.ap, bank.ap, ACT.Relu, after=[token])
                        bank.users = [x]
                        for j, h in enumerate(halves[h0:h0 + per]):
                            src = rl.ap[:, j * n:(j + 1) * n]
                            wt = w_idx[:, q, h:h + 1]
                            if h == 0:
                                t = ts(score[:, a:b], src, wt, ALU.mult, after=[x, idx_ready])
                            else:
                                t = stt(score[:, a:b], src, wt, score[:, a:b], ALU.mult, ALU.add, after=[x, t])
                        rl.users = [t]
                        yield
                    t = tt(score[:, a:b], score[:, a:b], c["causal"][:, a:b], ALU.add, after=[t, loaded2])
                yield
                src = score
                for step in range(TOPK // 8):
                    for q, a, b in PAIRS:
                        vec.wait(vec.last())
                        m = vec.count_up(nc.vector.max(top8[:, q, :], src[:, a:b]))
                        if step < TOPK // 8 - 1:
                            vec.wait(m)
                            vec.count_up(nc.vector.match_replace(work[step % 2][:, a:b], top8[:, q, :], src[:, a:b], TAKEN))
                    src = work[step % 2]
                    if step % 2:
                        yield
                more, eq, need = work[0], work[1], top8
                for q, a, b in PAIRS:
                    kth = top8[:, q, 7:8]
                    t1 = ts(more[:, a:b], score[:, a:b], kth, ALU.is_gt, after=[vec.last()])
                    t2 = ts(eq[:, a:b], score[:, a:b], kth, ALU.is_equal, after=[vec.last()])
                    vec.wait(t1, t2)
                    t3 = vec.count_up(nc.vector.tensor_reduce(need[:, q, 0:1], more[:, a:b], AX_X, ALU.add))
                    t3 = ts(need[:, q, 1:2], need[:, q, 0:1], -1.0, ALU.mult, float(TOPK), ALU.add, after=[t3])
                    vec.wait(t3)
                    t4 = vec.count_up(nc.vector.tensor_tensor_scan(keep[:, a:b], eq[:, a:b], eq[:, a:b], 0.0,
                                                                 ALU.add, ALU.max))
                    t5 = stt(eq[:, a:b], keep[:, a:b], need[:, q, 1:2], eq[:, a:b], ALU.is_le, ALU.mult, after=[t4])
                    t6 = tt(more[:, a:b], more[:, a:b], eq[:, a:b], ALU.add, after=[t5])
                    t7 = ts(more[:, a:b], more[:, a:b], -1.0, ALU.add, -MASKED, ALU.mult, after=[t6])
                    r["keep"] = tt(keep[:, a:b], more[:, a:b], c["causal"][:, a:b], ALU.min, after=[t7])
                yield

            sel = select()
            background.append(sel)
            up("dsa_q", base, low, plain(dq_t[:, :, :]))
            dsa_ready.append(ready_of[0])

            def rotary(dst, cos, sin):
                def go(bank, token):
                    raw_ = tmps.take(act)
                    a = fn(raw_.ap, bank.ap, ACT.Copy, after=[token])
                    bank.users = [a]
                    r["rot"] = (raw_, a, dst, cos, sin)
                return go

            def finish_rotary():
                raw_, a, dst, cos, sin = r["rot"]
                bank = high.take(pe)
                token = pe.count_up(mm(bank.ap, c["rotate"], raw_.ap, after=[a, loaded2]))
                two_ = lambda x: x.unsqueeze(1).broadcast_to([P, 2, SEQ])
                s = tmps.take(vec)
                v = lambda x: x.rearrange("p (k t) -> p k t", k=2)
                t1 = tt(v(s.ap), v(bank.ap), two_(sin), ALU.mult, after=[token])
                bank.users = [t1]
                t2 = tt(v(raw_.ap), v(raw_.ap), two_(cos), ALU.mult, after=[a, token])
                t3 = tt(dst, v(raw_.ap), v(s.ap), ALU.add, after=[t1, t2])
                raw_.users, s.users = [t3], [t3]
                return t3

            up("ret_k", base, low, rotary(rk_t[:, :, :], c["cos_k"], c["sin_k"]))
            rk_ready = finish_rotary()
            up("ret_q", base, low, rotary(rq_t[:, :, :], c["cos"], c["sin"]))
            rq_ready = finish_rotary()
            up_tokens("ret_v", base, low, plain(rv[:, :, :]))
            rv_ready = ready_of[0]

            def evacuate_rg(bank, token):
                th = tmps.take(act)
                a = fn(th.ap, bank.ap, ACT.Tanh, after=[token], scale=0.5)
                v = stt(rg_t[:, :, :], th.ap.rearrange("p (k t) -> p k t", k=2), 1.0,
                        bank.ap.rearrange("p (k t) -> p k t", k=2), ALU.add, ALU.mult, after=[a])
                th.users, bank.users = [v], [v]
                r["rg"] = v

            up("ret_g", base, low, evacuate_rg)

            def retention():
                for ch in range(2):
                    ms = []
                    for h in (2 * ch, 2 * ch + 1):
                        bank = high.take(pe)
                        q, k = head_rows(rq_t, h), head_rows(rk_t, h)
                        mm(bank.ap[:, 0:SEQ], k[:, 0:P], q, after=[rk_ready, rq_ready])
                        token = pe.count_up(mm(bank.ap[:, SEQ:KQ], k[:, P:SEQ], q[:, P:SEQ]))
                        m = tmps.take(vec)
                        dec = c["decay"][:, h * SEQ:(h + 1) * SEQ]
                        tt(m.ap[:, 0:SEQ], bank.ap[:, 0:SEQ], dec, ALU.mult, after=[token])
                        t = tt(m.ap[:, SEQ:KQ], bank.ap[:, SEQ:KQ], dec[:, 0:P], ALU.mult)
                        bank.users = [t]
                        ms.append((m, t))
                    yield
                    bank = high.take(pe)
                    for h, (m, t) in zip((2 * ch, 2 * ch + 1), ms):
                        o = bank.ap[(h % 2) * HD:(h % 2 + 1) * HD, 0:SEQ]
                        token = pe.count_up(value_product(o, m.ap, rv[:, 0, h * HD:(h + 1) * HD],
                                                        rv[:, 1, h * HD:(h + 1) * HD], [t, rv_ready]))
                        m.users = [token]
                    cp = copy(ro_t[:, ch, :], bank.ap[:, 0:SEQ], after=[token])
                    bank.users = [cp]
                    yield
                    bank = high.take(pe)
                    token = pe.count_up(mm(bank.ap[:, 0:SEQ], c["mean_head"], ro_t[:, ch, :], after=[cp]))
                    t = tt(ro_t[:, ch, :], ro_t[:, ch, :], bank.ap[:, 0:SEQ], ALU.subtract, after=[token])
                    bank.users = [t]
                    sq = tmps.take(act)
                    a = fn(sq.ap[:, 0:SEQ], ro_t[:, ch, :], ACT.Square, after=[t])
                    bank = high.take(pe)
                    token = pe.count_up(mm(bank.ap[:, 0:SEQ], c["mean_head"], sq.ap[:, 0:SEQ], after=[a]))
                    scale, read = rms_scale(bank.ap[:, 0:SEQ], sq.ap[:, SEQ:512], after=[token])
                    bank.users = [read]
                    t = stt(sq.ap[:, SEQ:512], sq.ap[:, SEQ:512], param("ret", 2 * l + ch), rg_t[:, ch, :],
                            ALU.mult, ALU.mult, after=[scale, r["rg"]])
                    t = stt(sq.ap[:, 0:SEQ], sq.ap[:, SEQ:512], 0.5, ro_t[:, ch, :], ALU.mult, ALU.mult,
                            after=[t, token])
                    sq.users = split_into(ch, 1, sq.ap[:, 0:SEQ].unsqueeze(1), after=[t])
                    yield

            ret = retention()
            background.append(ret)

            dil_ready = []
            for name, dst in (("dil_k", lk_t), ("dil_q", lq_t)):
                for j in range(2):
                    up(name, base, low, plain(dst[:, 2 * j:2 * j + 2, :]))
                    dil_ready.append(ready_of[0])
            for j in range(2):
                up_tokens("dil_v", base, low, plain(lv[:, :, j * 256:(j + 1) * 256]))
                dil_ready.append(ready_of[0])
            finish(sel, ret)
            dsa = attention(DSA_H, dq_t, dk_t, dv, keep[:, :], None, [dsa_ready, r["keep"]], 2)
            dil = attention(DIL_H, lq_t, lk_t, lv, c["union"], c["count"], dil_ready, 4)
            background.extend([dsa, dil])
            finish(dsa, dil)
            project_to_residual("out_2", lambda i: (2 * i, 2 * i + 1), DC // 2, low)

            norm_to(8, "mlp", DC * l, high)

            def evacuate_up(k):
                def go(bank, token):
                    s = tmps.take(act)
                    a = fn(s.ap, bank.ap, ACT.Relu, after=[token])
                    v = tt(s.ap, s.ap, bank.ap, ALU.mult, after=[a])
                    bank.users = [v]
                    s.users = split_into(k, 2, s.ap.rearrange("p (k t) -> p k t", k=2), after=[v])
                return go

            acc = [low.take(pe) for _ in range(4)]
            nf = FF2 // 256
            for i in range(nf + 2):
                if i < nf:
                    up("up", 8, high, evacuate_up(2 * (i % 4)))
                if i >= 2:
                    k = 2 * ((i - 2) % 4)
                    tokens = down("down", (k, k + 1), acc, i == 2, i == nf + 1)
            add_residual(acc, tokens)

        done = norm_to(0, "final", 0, high, write=res)
        sp.wait(done)
        nc.sync.dma_start(out_t, res[:, :, :]).then_inc(s_store, 16)
        nc.sync.wait_ge(s_store, 16)
        nc.sync.wait_ge(s_spill, 16)
        assert state["next_take"] == len(plan)


def shape_constants():
    ident = np.eye(P)
    tri = np.triu(np.ones((P, P)))
    block = np.kron(np.eye(2), np.ones((HD, HD)) / HD)
    first = {
        "ident": ident, "mean_d": np.full((P, P), 1 / D), "mean_group": np.full((P, P), GROUPS / D_INNER),
        "mean_latent": np.full((P, P), 1 / LATENT), "mean_head": block,
        "tri": np.concatenate([tri, np.ones((P, P)), tri], 1), "eps": np.full((P, 1), EPS),
    }
    rot = np.zeros((P, P))
    half = HD // 2
    for h in range(P // HD):
        for i in range(half):
            rot[h * HD + half + i, h * HD + i] = -1.0
            rot[h * HD + i, h * HD + half + i] = 1.0
    inv = np.float32(10000.0) ** (-np.arange(half, dtype=np.float32) / half)
    ang = (np.arange(SEQ, dtype=np.float32)[None, :] * inv.astype(np.float32)[:, None]).astype(np.float32)
    ang = np.tile(ang, (P // half, 1)).astype(np.float64)
    pos = np.arange(SEQ)
    gamma = np.log(1.0 - 2.0 ** (-5.0 - np.arange(RET_H)))
    diff = pos[None, :] - np.arange(P)[:, None]
    decay = np.concatenate([np.exp(np.maximum(diff, 0) * g) * (diff >= 0) for g in gamma], 1)
    q, k = pos[:, None], pos[None, :]
    dist = q - k
    cnt = ((dist >= 0) & (dist <= 128)).astype(int)
    for dil in (4, 16):
        cnt += (dist >= 0) & (dist % dil == 0)
    pairs = lambda m: np.concatenate([m[0:P, 0:P], m[P:SEQ, :]], 1)
    second = {
        "rotate": rot, "cos": np.cos(ang), "sin": np.sin(ang), "cos_k": np.cos(ang) * SCALE, "sin_k": np.sin(ang) * SCALE,
        "decay": decay, "causal": pairs(np.where(dist >= 0, 0.0, MASKED)),
        "union": pairs(np.where(cnt > 0, 0.0, MASKED)), "count": pairs(cnt),
    }
    pack = lambda names, d: np.concatenate([d[n] for n, _ in names], 1).astype(np.float32)
    return pack(CONSTS, first), pack(CONSTS_2, second)


def pack_params(a):
    def chunks(v):
        return np.ascontiguousarray(v.reshape(-1, P).T)

    def padded(v):
        return np.concatenate([v, np.zeros(P - len(v), v.dtype)])[:, None]

    cols = {
        "norm1": chunks(a["norm1_w"]), "conv_w": chunks(a["ssm_conv_w"]), "conv_b": chunks(a["ssm_conv_b"]),
        "lconv_w": chunks(a["lru_conv_w"]), "lconv_b": chunks(a["lru_conv_b"]), "b_r": chunks(a["lru_b_r"]),
        "b_i": chunks(a["lru_b_i"]), "lam": chunks(a["lru_lambda"]), "b_gate": chunks(a["b_branch_gate"]),
        "norm_w": chunks(a["ssm_norm_w"]), "d_skip": chunks(np.repeat(a["ssm_d"].reshape(-1), HD)),
        "norm2": chunks(a["norm2_w"]), "dt_bias": padded(a["ssm_dt_bias"].reshape(-1)),
        "a_log": padded(a["ssm_a_log"].reshape(-1)), "attn": chunks(a["attn_norm_w_2"]), "mlp": chunks(a["mlp_norm_w_2"]),
        "ret": chunks(a["ret_norm_w_2"]), "kvn": chunks(a["dsa_kv_norm_w_2"]), "norm_f": chunks(a["norm_f_w"]), "final": chunks(a["final_norm_w_2"]),
    }
    return np.ascontiguousarray(np.concatenate([cols[n] for n, _ in PARAMS], 1))


WEIGHTS = ["w_in", "w_out_ssm", "lru_w_r", "lru_w_i", "w_out_lru", "w_out", "w_ffn_in", "w_ffn_out",
           "w_in_2", "dsa_w_uk_2", "dsa_w_uv_2", "w_out_2", "w_up_2", "w_down_2"]


def kernel(**inputs):
    import concourse.bacc as bacc
    from concourse.bass_utils import run_bass_kernel_spmd

    a = {k: np.asarray(v) for k, v in inputs.items()}
    consts, consts_2 = shape_constants()
    arrays = {k: (np.ascontiguousarray(a[k]) if k.endswith("_2") else np.ascontiguousarray(a[k][0])) for k in WEIGHTS}
    arrays["x_t"] = np.ascontiguousarray(a["x"][0].T.reshape(DC, P, SEQ).transpose(1, 0, 2))
    arrays["params"], arrays["consts"], arrays["consts_2"] = pack_params(a), consts, consts_2
    nc = bacc.Bacc("TRN2", target_bir_lowering=False, num_devices=1)
    aps = {k: nc.dram_tensor(f"in_{k}", v.shape, F32, kind="ExternalInput").ap() for k, v in arrays.items()}
    out = nc.dram_tensor("out_t", (P, DC, SEQ), F32, kind="ExternalOutput").ap()
    build(nc, {k: aps[k] for k in WEIGHTS}, aps["x_t"], aps["params"], aps["consts"], aps["consts_2"], out)
    r = run_bass_kernel_spmd(nc, [{f"in_{k}": v for k, v in arrays.items()}], core_ids=[0])
    got = r.results[0]["out_t"]
    return np.ascontiguousarray(got.transpose(1, 0, 2).reshape(D, SEQ).T)[None]
```

```python
from contextlib import ExitStack

import numpy as np

import concourse.bass as bass
from concourse import mybir

F32 = mybir.dt.float32
F32R = mybir.dt.float32r
ACT = mybir.ActivationFunctionType
ALU = mybir.AluOpType
AX_X = mybir.AxisListType.X

P = 128
SEQ = 256
TT = SEQ // P
D = 1024
DC = D // P
EPS = 1e-6

D_INNER = 2048
HEADS = 32
HD = 64
GROUPS = 4
HPG = HEADS // GROUPS
STATE = 128
CONV = 4
XBC = D_INNER + 2 * GROUPS * STATE
LRU = 1280
LC = LRU // P
LRU_C = 8.0
FFN = 2816
COL_GATE = 0
COL_Z = 2 * D
COL_XBC = COL_Z + D_INNER
COL_B = COL_XBC + D_INNER
COL_C = COL_B + GROUPS * STATE
COL_DT = COL_XBC + XBC
COL_LX = COL_DT + HEADS
COL_LY = COL_LX + LRU
GC = D_INNER // GROUPS // P

DEPTH_2 = 2
RET_H, DSA_H, DIL_H = 4, 4, 8
RET_W, DSA_W, DIL_W = RET_H * HD, DSA_H * HD, DIL_H * HD
LATENT = 128
IDX_H = 8
TOPK = min(256, SEQ // 4)
FF2 = 4 * D
C_RET = 0
C_DSA = 4 * RET_W
C_CKV = C_DSA + DSA_W
C_QI = C_CKV + LATENT
C_KI = C_QI + IDX_H * HD
C_DIL = C_KI + HD + IDX_H
IDX_SCALE = float(IDX_H ** -0.5 * HD ** -0.5)
SCALE = float(HD) ** -0.5
MASKED = -3.0e38
TAKEN = -3.4e38

XS_AND_GATES = [("xs", 0), ("xs", 1)] + [t for i in range(6) for t in (("gate", i), ("xs", 2 + i))] + [("gate", 6), ("gate", 7)]

RAW_SLOTS, SPLIT_SLOTS = 3, 3
OUT_ORDER = (2, 3, 0, 1)
POOL_TILES = {"dt": 1, "lx": 2, "bc": 2, "xs": 1, "gate": 1, "ly": 2,
              "dsa_q": 1, "dil_k": 2, "dil_q": 2, "dil_v": 2, "ret_k": 2, "ret_q": 2, "ret_v": 2, "ret_g": 2, "out_2": 2}
TILE = 2048
KQ = 3 * P

PARAMS = [
    ("norm1", DC), ("conv_w", CONV * XBC // P), ("conv_b", XBC // P), ("lconv_w", CONV * LC), ("lconv_b", LC),
    ("b_r", LC), ("b_i", LC), ("lam", LC), ("b_gate", 2 * DC), ("norm_w", D_INNER // P), ("d_skip", D_INNER // P),
    ("norm2", DC), ("dt_bias", 1), ("a_log", 1), ("attn", DC * DEPTH_2), ("mlp", DC * DEPTH_2),
    ("ret", RET_W // P * DEPTH_2), ("kvn", DEPTH_2), ("norm_f", DC), ("final", DC),
]
PARAM_AT, _n = {}, 0
for _name, _w in PARAMS:
    PARAM_AT[_name] = (_n, _w)
    _n += _w
N_PARAMS = _n

CONSTS = [("ident", P), ("mean_d", P), ("mean_group", P), ("mean_latent", P), ("mean_head", P), ("tri", KQ), ("eps", 1)]
CONSTS_2 = [("rotate", P), ("cos", SEQ), ("sin", SEQ), ("cos_k", SEQ), ("sin_k", SEQ), ("decay", RET_H * SEQ),
            ("causal", KQ), ("union", KQ), ("count", KQ)]


class Engine:

    def __init__(self, ops, sem):
        self.ops, self.sem, self.count, self.seen = ops, sem, 0, {}

    def wait(self, *tokens):
        for t in tokens:
            if t is None:
                continue
            if isinstance(t, list):
                self.wait(*t)
                continue
            sem, value = t
            if self.seen.get(sem.name, 0) < value:
                self.ops.wait_ge(sem, value)
                self.seen[sem.name] = value

    def count_up(self, inst):
        self.count += 1
        inst.then_inc(self.sem, 1)
        return (self.sem, self.count)

    def last(self):
        return (self.sem, self.count) if self.count else None


class Slot:
    def __init__(self, ap):
        self.ap, self.users = ap, []


class Ring:

    def __init__(self, aps):
        self.slots, self.n = [Slot(a) for a in aps], 0

    def take(self, writer):
        slot = self.slots[self.n % len(self.slots)]
        self.n += 1
        assert slot.users is not None, "still in use"
        writer.wait(slot.users)
        slot.users = None
        return slot


class Split:

    def __init__(self, hi, lo):
        self.hi, self.lo = hi, lo

    def __getitem__(self, key):
        return Split(self.hi[key], self.lo[key])


def weight_plan(w):
    plan = []

    def cols(name, mat, c0, n):
        src = mat[:, c0:c0 + n].rearrange("(k p) c -> p k c", p=P)
        plan.append((name, True, (DC, n), [((0, n), src)]))

    def rows(name, mat, k0, n=2):
        src = mat[k0 * P:(k0 + n) * P, :].rearrange("(k p) c -> p k c", p=P)
        plan.append((name, True, (n, D), [((0, D), src)]))

    w_in = w["w_in"]
    cols("dt", w_in, COL_DT, P)
    for i in range(LC // 2):
        cols("lx", w_in, COL_LX + 256 * i, 256)
    for i in range(4):
        cols("bc", w_in, COL_B + 256 * i, 256)
    for kind, i in XS_AND_GATES:
        cols(kind, w_in, (COL_XBC if kind == "xs" else COL_GATE) + 256 * i, 256)
    for i in range(LC // 2):
        cols("ly", w_in, COL_LY + 256 * i, 256)
    def out_ssm(g):
        for i in range(2):
            rows("out_ssm", w["w_out_ssm"], GC * g + 2 * i)

    for g in range(GROUPS):
        for i in range(2):
            cols("z", w_in, COL_Z + 512 * g + 256 * i, 256)
        if g:
            out_ssm(g - 1)
    for i in range(LC // 2 - 1):
        rows("out_lru", w["w_out_lru"], 2 * i)
    out_ssm(GROUPS - 1)
    rows("out_lru", w["w_out_lru"], LC - 2)
    for i in range(DC // 2):
        rows("out", w["w_out"], 2 * i)
    nf = FFN // 256
    for i in range(nf + 1):
        if i < nf:
            cols("ffn_gate", w["w_ffn_in"], 256 * i, 256)
            cols("ffn_up", w["w_ffn_in"], FFN + 256 * i, 256)
        if i:
            rows("ffn_out", w["w_ffn_out"], 2 * (i - 1))
    for l in range(DEPTH_2):
        w2 = w["w_in_2"][l]
        cols("ckv", w2, C_CKV, LATENT)
        ki = w2[:, C_KI:C_KI + HD].rearrange("(k p) c -> p k c", p=P)
        kiw = w2[:, C_KI:C_KI + HD + IDX_H].rearrange("(k p) c -> p k c", p=P)
        plan.append(("ki", True, (DC, 2 * HD + IDX_H), [((0, HD), ki), ((HD, 2 * HD + IDX_H), kiw)]))
        for i in range(2):
            cols("qi", w2, C_QI + 256 * i, 256)
        cols("dsa_q", w2, C_DSA, 256)
        for name, c in (("dil_k", 1), ("dil_q", 0), ("dil_v", 2)):
            for i in range(2):
                cols(name, w2, C_DIL + DIL_W * c + 256 * i, 256)
        for name, c in (("ret_k", 1), ("ret_q", 0), ("ret_v", 2), ("ret_g", 3)):
            cols(name, w2, C_RET + RET_W * c, 256)
        for i in OUT_ORDER:
            rows("out_2", w["w_out_2"][l], 2 * i)
        nf = FF2 // 256
        for i in range(nf + 2):
            if i < nf:
                cols("up", w["w_up_2"][l], 256 * i, 256)
            if i >= 2:
                rows("down", w["w_down_2"][l], 2 * (i - 2))
    return plan


def build(nc, w, x_t, params, consts, consts_2, out_t, debug=None):
    ctx = ExitStack()
    with ctx:
        def sem(name):
            return ctx.enter_context(nc.semaphore(name))

        def sb(name, shape, dt=F32, stack=ctx):
            return stack.enter_context(nc.sbuf_tensor(name, shape, dt))

        pe = Engine(nc.tensor, sem("pe_done"))
        act = Engine(nc.scalar, sem("act_done"))
        vec = Engine(nc.vector, sem("vec_done"))
        pool = Engine(nc.gpsimd, sem("pool_done"))
        sp = Engine(nc.sync, sem("sp_unused"))
        dma_sems = [sem(f"tile_arrived_{i}") for i in range(RAW_SLOTS)]
        s_x = sem("x_arrived")
        s_misc = sem("small_loads_arrived")
        s_lru = sem("lru_weights_arrived")
        s_spill = sem("cs_spilled")
        s_bcast = sem("cs_broadcast")
        s_ukv = sem("ukv_arrived")
        s_consts_2 = sem("consts_2_arrived")
        s_store = sem("output_stored")

        res = sb("residual", [P, DC, SEQ])
        act_hi = sb("act_hi", [P, 16, SEQ], F32R)
        act_lo = sb("act_lo", [P, 16, SEQ], F32R)
        acts = Split(act_hi, act_lo)
        raw = [sb(f"raw_{i}", [P, TILE]) for i in range(RAW_SLOTS)]
        w_hi = [sb(f"w_hi_{i}", [P, TILE], F32R) for i in range(SPLIT_SLOTS)]
        w_lo = [sb(f"w_lo_{i}", [P, TILE], F32R) for i in range(SPLIT_SLOTS)]
        par = sb("params", [P, N_PARAMS])
        n_consts = sum(n for _, n in CONSTS)
        con = sb("consts", [P, n_consts])
        tmps = Ring([sb(f"tmp_{i}", [P, 512])[:, :] for i in range(5)])
        rstd = sb("rstd", [P, SEQ])
        rstd_sq = sb("rstd_sq", [P, SEQ])
        small = sb("small", [P, 96])

        banks = [ctx.enter_context(nc.psum_tensor(f"bank_{i}", [P, 512], F32)) for i in range(8)]
        low, high = Ring([b[:, :] for b in banks[:4]]), Ring([b[:, :] for b in banks[4:]])

        c, at = {}, 0
        for name, n in CONSTS:
            c[name] = con[:, at:at + n]
            at += n

        def param(name, i=0, n=1):
            a, width = PARAM_AT[name]
            assert i + n <= width
            return par[:, a + i:a + i + n]

        def tt(out, a, b, op, after=(), on=vec):
            on.wait(*after)
            return on.count_up(on.ops.tensor_tensor(out, a, b, op))

        def ts(out, a, s1, op0, s2=None, op1=None, after=(), on=vec):
            on.wait(*after)
            if op1 is None:
                return on.count_up(on.ops.tensor_scalar(out, a, s1, None, op0))
            return on.count_up(on.ops.tensor_scalar(out, a, s1, s2, op0, op1))

        def stt(out, a, s, b, op0, op1, after=(), accum=None):
            vec.wait(*after)
            return vec.count_up(nc.vector.scalar_tensor_tensor(out=out, in0=a, scalar=s, in1=b, op0=op0, op1=op1,
                                                             accum_out=accum))

        def fn(out, a, func, after=(), scale=1.0, bias=0.0, accum=None):
            act.wait(*after)
            return act.count_up(nc.scalar.activation(out, a, func, bias=bias, scale=scale, accum_out=accum))

        def copy(out, a, after=(), on=vec):
            if on is act:
                return fn(out, a, ACT.Copy, after)
            on.wait(*after)
            return on.count_up(on.ops.tensor_copy(out, a))

        def recip(out, a, after=()):
            vec.wait(*after)
            return vec.count_up(nc.vector.reciprocal(out, a))

        def mm(out, lhs, rhs, start=True, stop=True, after=()):
            pe.wait(*after)
            return nc.tensor.matmul(out, lhs, rhs, start=start, stop=stop, skip_group_check=True)

        def product(out, lhs, rhs, start, stop, after=()):
            pe.wait(*after)
            nc.tensor.matmul(out, lhs.hi, rhs.hi, start=start, stop=False, skip_group_check=True)
            nc.tensor.matmul(out, lhs.hi, rhs.lo, start=False, stop=False, skip_group_check=True)
            return nc.tensor.matmul(out, lhs.lo, rhs.hi, start=False, stop=stop, skip_group_check=True)

        def transpose(out, a, k=P, after=()):
            pe.wait(*after)
            return nc.tensor.transpose(out, a, c["ident"][0:k, 0:k])

        def split_into(k, n, src, after=(), lo_on=pool):
            hi, lo = act_hi[:, k:k + n, :], act_lo[:, k:k + n, :]
            used = [chunk_users[j] for j in range(k, k + n)]
            a = copy(hi, src, after=[*after, used], on=act)
            b = tt(lo, src, hi.bitcast(F32), ALU.subtract, after=[*after, used, a], on=lo_on)
            for j in range(k, k + n):
                chunk_users[j] = None
                chunk_ready[j] = [a, b]
            return [a, b]

        chunk_users = [None] * 16
        chunk_ready = [None] * 16

        nc.sync.dma_start(res[:, :, :], x_t).then_inc(s_x, 16)
        nc.sync.dma_start(con[:, :], consts).then_inc(s_misc, 16)
        nc.sync.dma_start(par[:, :], params).then_inc(s_misc, 16)
        x_loaded, loaded = (s_x, 16), (s_misc, 32)

        plan = weight_plan(w)
        dma_count = [0] * RAW_SLOTS
        arrived, tiles, raw_users = [None] * len(plan), [None] * len(plan), [None] * len(plan)
        split_users = [None] * len(plan)
        state = {"next_load": 0, "next_split": 0, "next_take": 0}

        def load_tile():
            i = state["next_load"]
            if i >= len(plan) or (i >= RAW_SLOTS and raw_users[i - RAW_SLOTS] is None):
                return
            state["next_load"] = i + 1
            slot = i % RAW_SLOTS
            _, _, (k, n), parts = plan[i]
            if i >= RAW_SLOTS:
                sp.wait(raw_users[i - RAW_SLOTS])
            tile = raw[slot][:, 0:k * n].rearrange("p (k c) -> p k c", k=k)
            for j, ((a, b), src) in enumerate(parts):
                dst = tile[:, j, :] if len(src.shape) == 2 else tile[:, :, a:b]
                nc.sync.dma_start(dst, src).then_inc(dma_sems[slot], 16)
                dma_count[slot] += 16
            arrived[i] = (dma_sems[slot], dma_count[slot])
            load_tile()

        def split_tile():
            i = state["next_split"]
            state["next_split"] = i + 1
            assert arrived[i] is not None
            _, is_split, (k, n), _ = plan[i]
            src = raw[i % RAW_SLOTS][:, 0:k * n]
            if not is_split:
                tiles[i] = (src.rearrange("p (k c) -> p k c", k=k), arrived[i])
                return
            slot = i % SPLIT_SLOTS
            free = split_users[i - SPLIT_SLOTS] if i >= SPLIT_SLOTS else None
            hi, lo = w_hi[slot][:, 0:k * n], w_lo[slot][:, 0:k * n]
            a = copy(hi, src, after=[arrived[i], free], on=act)
            every = POOL_TILES.get(plan[i][0], 0)
            state["light"] = state.get("light", 0) + 1
            b = tt(lo, src, hi.bitcast(F32), ALU.subtract, after=[arrived[i], free, a],
                   on=pool if every and state["light"] % every == 0 else vec)
            raw_users[i] = [a, b]
            tiles[i] = (Split(hi.rearrange("p (k c) -> p k c", k=k), lo.rearrange("p (k c) -> p k c", k=k)), [a, b])
            load_tile()

        def take(name):
            i = state["next_take"]
            state["next_take"] = i + 1
            assert plan[i][0] == name, (plan[i][0], name)
            while state["next_split"] < min(i + SPLIT_SLOTS, state["next_load"]):
                split_tile()
            return (i, *tiles[i])

        def used(i, token):
            split_users[i] = token
            if not plan[i][1]:
                raw_users[i] = token
                load_tile()

        load_tile()

        background = []

        def advance(n=1):
            for _ in range(n):
                for g in list(background):
                    if next(g, "end") == "end":
                        background.remove(g)

        def finish(*gens):
            while any(g in background for g in gens):
                advance()

        def up(name, base, ring, evacuate, width=256):
            i, tile, ready = take(name)
            bank = ring.take(pe)
            pe.wait(ready)
            for m in range(width // P):
                for k in range(DC):
                    inst = product(bank.ap[:, m * SEQ:(m + 1) * SEQ], tile[:, k, m * P:(m + 1) * P],
                                   acts[:, base + k, :], k == 0, k == DC - 1, after=[chunk_ready[base + k]])
            token = pe.count_up(inst)
            for k in range(DC):
                chunk_users[base + k] = token
            used(i, token)
            run_late()
            evacuate_when_scaled(evacuate, bank, token)
            advance()

        def up_tokens(name, base, ring, evacuate, lo=0, width=256):
            i, tile, ready = take(name)
            bank = ring.take(pe)
            pe.wait(ready)
            for t in range(TT):
                for k in range(DC):
                    inst = product(bank.ap[:, t * width:(t + 1) * width], acts[:, base + k, t * P:(t + 1) * P],
                                   tile[:, k, lo:lo + width], k == 0, k == DC - 1, after=[chunk_ready[base + k]])
            token = pe.count_up(inst)
            for k in range(DC):
                chunk_users[base + k] = token
            used(i, token)
            run_late()
            evacuate_when_scaled(evacuate, bank, token)
            advance()

        def down(name, chunks, ring_banks, first, last):
            i, tile, ready = take(name)
            pe.wait(ready)
            tokens = []
            for b, bank in enumerate(ring_banks):
                for j, k in enumerate(chunks):
                    for m in range(2):
                        inst = product(bank.ap[:, m * SEQ:(m + 1) * SEQ],
                                       tile[:, j, (2 * b + m) * P:(2 * b + m + 1) * P], acts[:, k, :],
                                       first and j == 0 and m == 0, last and j == 1, after=[chunk_ready[k]])
                tokens.append(pe.count_up(inst) if last or b == len(ring_banks) - 1 else None)
            for k in chunks:
                chunk_users[k] = tokens[-1]
            used(i, tokens[-1])
            advance()
            return tokens

        def feature_mean(bank_ap, square, matrix, start, stop, after):
            return mm(bank_ap, matrix, square, start, stop, after=after)

        def rms_scale(mean, out, after):
            a = fn(out, mean, ACT.Sqrt, after=after, bias=c["eps"])
            return recip(out, out, after=[a]), a

        res_ready = [x_loaded] * DC

        def norm_to(base, weight, w0, ring, write=None, meanwhile=None):
            bank = ring.take(pe)
            for j in range(DC // 2):
                sq = tmps.take(act)
                a = fn(sq.ap, res[:, 2 * j:2 * j + 2, :], ACT.Square, after=[res_ready[2 * j], res_ready[2 * j + 1]])
                for m in range(2):
                    inst = feature_mean(bank.ap[:, 0:SEQ], sq.ap[:, m * SEQ:(m + 1) * SEQ], c["mean_d"],
                                        j == 0 and m == 0, j == DC // 2 - 1 and m == 1, after=[a, loaded])
                sq.users = [pe.count_up(inst)]
            if meanwhile:
                meanwhile()
            scale_ready, read = rms_scale(bank.ap[:, 0:SEQ], rstd[:, :], after=[*sq.users, *norm_users])
            bank.users = [read]
            norm_users.clear()
            for j in range(DC // 2):
                n = tmps.take(vec) if write is None else None
                for m in range(2):
                    k = 2 * j + m
                    dst = n.ap[:, m * SEQ:(m + 1) * SEQ] if n else write[:, k, :]
                    t = stt(dst, res[:, k, :], param(weight, w0 + k), rstd[:, :], ALU.mult, ALU.mult,
                            after=[scale_ready, loaded])
                if n:
                    n.users = split_into(base + 2 * j, 2, n.ap.rearrange("p (k t) -> p k t", k=2), after=[t])
            norm_users.append(t)
            return t

        norm_users = []
        late = {"work": None, "evacuations": [], "ready": None}

        def run_late():
            if late["work"] is not None and next(late["work"], "end") == "end":
                late["work"] = None
                for go in late["evacuations"]:
                    go()
                late["evacuations"] = []

        def evacuate_when_scaled(go, bank, token):
            if late["work"] is None:
                go(bank, token)
            else:
                late["evacuations"].append(lambda: go(bank, token))

        def begin_norm(base, weight, work):
            for k in range(DC):
                hi, lo = act_hi[:, base + k, :], act_lo[:, base + k, :]
                a = fn(hi, res[:, k, :], ACT.Copy, after=[res_ready[k], chunk_users[base + k], loaded],
                       scale=weight[:, k:k + 1])
                b = stt(lo, res[:, k, :], weight[:, k:k + 1], hi.bitcast(F32), ALU.mult, ALU.subtract,
                        after=[a, res_ready[k], chunk_users[base + k]])
                chunk_users[base + k] = None
                chunk_ready[base + k] = [a, b]
            late["work"] = work
            late["split"] = [a, b]

        def mean_square(ring):
            squares = []
            for j in range(DC // 2):
                sq = tmps.take(act)
                a = fn(sq.ap, res[:, 2 * j:2 * j + 2, :], ACT.Square, after=[res_ready[2 * j], res_ready[2 * j + 1]])
                squares.append((sq, a))
            bank = ring.take(pe)
            for j, (sq, a) in enumerate(squares):
                for m in range(2):
                    inst = mm(bank.ap[:, 0:SEQ], c["mean_d"], sq.ap[:, m * SEQ:(m + 1) * SEQ],
                              j == 0 and m == 0, j == DC // 2 - 1 and m == 1, after=[a])
                sq.users = [pe.count_up(inst)]
            return bank, sq.users

        def scale_of(bank, after):
            ready, read = rms_scale(bank.ap[:, 0:SEQ], rstd[:, :], after=[after, norm_users])
            bank.users = [read]
            norm_users.clear()
            return ready

        def by_scale(out, src, after, n=2):
            return tt(out, src, rstd[:, :].unsqueeze(1).broadcast_to([P, n, SEQ]), ALU.mult,
                      after=[late["ready"], *after])

        def pair(x):
            return x.rearrange("p (k t) -> p k t", k=2)

        one = ExitStack()
        xbc = sb("xbc", [P, XBC // P, SEQ], stack=one)
        lru_u = sb("lru_u", [P, LC, SEQ], stack=one)
        lru_ab = sb("lru_ab", [P, 2 * LC, SEQ], stack=one)
        lru_a, lru_b = lru_ab[:, 0:LC, :], lru_ab[:, LC:2 * LC, :]
        gates = lru_ab[:, 0:2 * DC, :]
        cs_all = sb("cs_all", [P, HPG, SEQ], stack=one)
        xdt = sb("xdt", [P, TT, GC * P], stack=one)
        z_silu = sb("z_silu", [P, 2 * GC, SEQ], stack=one)
        cb_mask = sb("cb_mask", [P, KQ], stack=one)
        lru_w = xbc[:, 0:2 * LC * P // SEQ, :].rearrange("p k (a j) -> p (k a) j", j=P).rearrange(
            "p (g h) j -> p g h j", g=2)
        lru_w_used = []
        cs_dram = nc.dram_tensor("cs_scratch", (HEADS, SEQ), F32, kind="Internal").ap()

        def first_splits():
            for _ in range(2):
                split_tile()

        norm_to(0, "norm1", 0, high, meanwhile=first_splits)

        a0, wd = PARAM_AT["conv_w"]
        half = ts(par[:, a0:a0 + wd + XBC // P], par[:, a0:a0 + wd + XBC // P], 0.5, ALU.mult, after=[loaded])
        a0 = PARAM_AT["b_r"][0]
        half_b = ts(par[:, a0:a0 + 2 * LC], par[:, a0:a0 + 2 * LC], 0.5, ALU.mult, after=[loaded])
        a0 = PARAM_AT["b_gate"][0]
        half_g = ts(par[:, a0:a0 + 2 * DC], par[:, a0:a0 + 2 * DC], 0.5, ALU.mult, after=[loaded])

        def softplus(out, x, s1, s2, sign, after):
            t = ts(s1, x, -1.0, ALU.mult, after=after)
            t = tt(s1, s1, x, ALU.min, after=[t])
            t = fn(s1, s1, ACT.Exp, after=[t])
            t = ts(s2, s1, 1.0, ALU.add, after=[t])
            l = fn(out, s2, ACT.Ln, after=[t, *after])
            u = stt(s1, s2, -1.0, s1, ALU.add, ALU.subtract, after=[t])
            r = recip(s2, s2, after=[l, u])
            t = tt(s1, s1, s2, ALU.mult, after=[r])
            t = tt(out, out, s1, ALU.subtract, after=[t, l])
            t = ts(s1, x, sign, ALU.mult, 0.0, ALU.max, after=[t])
            return tt(out, out, s1, ALU.add, after=[t])

        sp_lam = small[:, 0:LC]
        neg_a = small[0:HEADS, 48:49]

        dt = sb("dt", [HEADS, SEQ], stack=one)
        cs = sb("cs", [HEADS, SEQ], stack=one)
        dt_tok = sb("dt_tok", [P, TT, HEADS], stack=one)
        neg_cs = sb("neg_cs", [P, TT, HEADS], stack=one)
        ssd_ready = {}

        def evacuate_dt(bank, token):
            lam_ready = softplus(sp_lam, param("lam", 0, LC), small[:, 16:16 + LC], small[:, 32:32 + LC], -1.0, [loaded])
            lam_ready = ts(sp_lam, sp_lam, -LRU_C / 2, ALU.mult, after=[lam_ready])
            t = fn(neg_a, param("a_log")[0:HEADS], ACT.Exp, after=[loaded])
            for i, name in enumerate(("lru_w_r", "lru_w_i")):
                nc.scalar.dma_start(lru_w[:, i], w[name].rearrange("h i j -> i h j")).then_inc(s_lru, 16)
            neg_a_ready = ts(neg_a, neg_a, -1.0, ALU.mult, after=[t])

            x, s1, s2 = tmps.take(vec), tmps.take(vec), tmps.take(vec)
            x_, s1_, s2_ = (s.ap[0:HEADS, 0:SEQ] for s in (x, s1, s2))
            t = ts(x_, bank.ap[0:HEADS, 0:SEQ], param("dt_bias")[0:HEADS], ALU.add, after=[token, loaded])
            bank.users = [t]
            ssd_ready["lam"] = lam_ready
            t = softplus(dt[:, :], x_, s1_, s2_, 1.0, [t, act.last()])
            u = ts(s1_, dt[:, :], neg_a, ALU.mult, after=[t, neg_a_ready])
            v = nc.vector.memset(s2_, 1.0)
            v = vec.count_up(v)
            vec.wait(u, v)
            t = vec.count_up(nc.vector.tensor_tensor_scan(cs[:, :], s2_, s1_, 0.0, ALU.mult, ALU.add))
            for s in (x, s1, s2):
                s.users = [t]
            act.wait(t)
            nc.scalar.dma_start(cs_dram, cs[:, :]).then_inc(s_spill, 16)
            ssd_ready["cs"] = t

        def turn_dt():
            yield
            yield
            t = ssd_ready["cs"]
            bank = high.take(pe)
            for i, src in enumerate((dt, cs)):
                for tile in range(TT):
                    j = (i * TT + tile) * HEADS
                    inst = transpose(bank.ap[:, j:j + HEADS], src[:, tile * P:(tile + 1) * P], HEADS, after=[t])
            token = pe.count_up(inst)
            view = bank.ap[:, 0:4 * HEADS].rearrange("p (i t h) -> p i t h", i=2, t=TT)
            a = copy(dt_tok[:, :, :], view[:, 0], after=[token])
            b = ts(neg_cs[:, :, :], view[:, 1], -1.0, ALU.mult, after=[token])
            bank.users = [b]
            ssd_ready["dt"] = [a, b]
            yield

        up("dt", 0, low, evacuate_dt, width=P)
        background.append(turn_dt())

        def conv(bank, token, out, w_name, w_stride, b_name, k0):
            for m in range(2):
                t = fn(out[:, m, :], bank.ap[:, m * SEQ:(m + 1) * SEQ], ACT.Identity, after=[token, half, loaded],
                       scale=param(w_name, 3 * w_stride + k0 + m), bias=param(b_name, k0 + m))
            tokens = [t, t]
            for j in (2, 1, 0):
                d = 3 - j
                for m in range(2):
                    u = bank.ap[:, m * SEQ:(m + 1) * SEQ]
                    tokens[m] = stt(out[:, m, d:SEQ], u[:, 0:SEQ - d], param(w_name, j * w_stride + k0 + m),
                                    out[:, m, d:SEQ], ALU.mult, ALU.add, after=[tokens[m]])
            bank.users = [tokens[1]]
            return tokens[1]

        xbc_ready = [None] * (XBC // P)

        def evacuate_xbc(k0):
            def go(bank, token):
                act.wait(lru_w_used)
                t = conv(bank, token, xbc[:, k0:k0 + 2, :], "conv_w", XBC // P, "conv_b", k0)
                th = tmps.take(act)
                a = fn(th.ap, xbc[:, k0:k0 + 2, :], ACT.Tanh, after=[t])
                b = stt(xbc[:, k0:k0 + 2, :], th.ap.rearrange("p (k t) -> p k t", k=2), 1.0, xbc[:, k0:k0 + 2, :],
                        ALU.add, ALU.mult, after=[a])
                th.users = [b]
                xbc_ready[k0] = xbc_ready[k0 + 1] = b
            return go

        u_ready = [None] * LC

        def evacuate_lx(k0):
            def go(bank, token):
                u_ready[k0] = u_ready[k0 + 1] = conv(bank, token, lru_u[:, k0:k0 + 2, :], "lconv_w", LC, "lconv_b", k0)
            return go

        lru_done = [None] * LC

        def lru_work():
            for h in range(LC):
                bank = high.take(pe)
                mm(bank.ap[:, 0:SEQ], lru_w[:, 0, h, :], lru_u[:, h, :], after=[(s_lru, 32), u_ready[h]])
                token = pe.count_up(mm(bank.ap[:, SEQ:512], lru_w[:, 1, h, :], lru_u[:, h, :]))
                th, sq = tmps.take(act), tmps.take(act)
                r, g, s = th.ap[:, 0:SEQ], th.ap[:, SEQ:512], sq.ap[:, 0:SEQ]
                fn(r, bank.ap[:, 0:SEQ], ACT.Tanh, after=[token, half_b], scale=0.5, bias=param("b_r", h))
                a2 = fn(g, bank.ap[:, SEQ:512], ACT.Tanh, scale=0.5, bias=param("b_i", h))
                bank.users = [a2]
                lam = sp_lam[:, h:h + 1]
                e = fn(lru_a[:, h, :], r, ACT.Exp, after=[a2, ssd_ready["lam"]], scale=lam, bias=lam)
                tl = fn(r, r, ACT.Tanh, after=[e], scale=lam, bias=lam)
                a3 = fn(s, lru_a[:, h, :], ACT.Square, after=[e])
                v = stt(lru_b[:, h, :], s, 1.0, r, ALU.add, ALU.mult, after=[a3, tl])
                v3 = stt(lru_u[:, h, :], g, 1.0, lru_u[:, h, :], ALU.add, ALU.mult, after=[a2])
                th.users, sq.users = [v3], [v]
                if h % 2:
                    yield
            lru_w_used.append(token)
            root = fn(lru_b, lru_b, ACT.Sqrt, after=[v], scale=-0.25)
            yield
            for h in range(LC):
                t = tt(lru_b[:, h, :], lru_b[:, h, :], lru_u[:, h, :], ALU.mult, after=[root, v3])
                vec.wait(t)
                lru_done[h] = vec.count_up(nc.vector.tensor_tensor_scan(lru_u[:, h, :], lru_a[:, h, :], lru_b[:, h, :],
                                                                        0.0, ALU.mult, ALU.add))
                if h % 4 == 3:
                    yield

        scan = lru_work()
        for i in range(LC // 2):
            if i == 1:
                background.append(scan)
            up("lx", 0, low, evacuate_lx(2 * i))
        for i in range(4):
            up("bc", 0, low, evacuate_xbc(16 + 2 * i))

        y_ready = [None] * GROUPS
        cs_read, xdt_read, cb_read = [], [], []

        def load_cs(g):
            act.wait((s_spill, 16), cs_read)
            nc.scalar.dma_start(cs_all[:, :, :], cs_dram[g * HPG:(g + 1) * HPG, :].partition_broadcast(P)).then_inc(s_bcast, 16)

        def ssd(g):
            if g == 0:
                load_cs(0)
            cs_here = (s_bcast, 16 * (g + 1))
            bm, cm = xbc[:, 16 + g, :], xbc[:, 20 + g, :]
            bank = high.take(pe)
            mm(bank.ap[:, 0:SEQ], bm[:, 0:P], cm, after=[xbc_ready[16 + g], xbc_ready[20 + g]])
            token = pe.count_up(mm(bank.ap[:, SEQ:KQ], bm[:, P:SEQ], cm[:, P:SEQ]))
            cb = tt(cb_mask[:, :], bank.ap[:, 0:KQ], c["tri"], ALU.mult, after=[token, cb_read])
            bank.users = [cb]
            cb_read.clear()
            x_ready = [xbc_ready[GC * g + k] for k in range(GC)]
            xdt_ready = []
            for t in range(TT):
                bank = high.take(pe)
                for k in range(GC):
                    inst = transpose(bank.ap[:, k * P:(k + 1) * P], xbc[:, GC * g + k, t * P:(t + 1) * P],
                                     after=[x_ready[k]])
                token = pe.count_up(inst)
                v = tt(xdt[:, t, :].rearrange("p (h e) -> p h e", e=HD), bank.ap.rearrange("p (h e) -> p h e", e=HD),
                       dt_tok[:, t, g * HPG:(g + 1) * HPG].unsqueeze(2).broadcast_to([P, HPG, HD]), ALU.mult,
                       after=[token, xdt_read, ssd_ready["dt"]])
                bank.users = [v]
                xdt_ready.append(v)
            xdt_read.clear()
            yield
            m_ready = {}

            def decays(h):
                e = tmps.take(vec)
                hh = g * HPG + h
                ts(e.ap[:, 0:SEQ], cs_all[:, h, :], neg_cs[:, 0, hh:hh + 1], ALU.add, 0.0, ALU.min,
                   after=[cs_here, ssd_ready["dt"]])
                d = ts(e.ap[:, SEQ:KQ], cs_all[:, h, P:SEQ], neg_cs[:, 1, hh:hh + 1], ALU.add, 0.0, ALU.min)
                a = fn(e.ap[:, 0:KQ], e.ap[:, 0:KQ], ACT.Exp, after=[d])
                v = tt(e.ap[:, 0:KQ], e.ap[:, 0:KQ], cb_mask[:, :], ALU.mult, after=[a, cb])
                m_ready[h] = (e, v)
                return d, v

            for pair in range(0, HPG, 2):
                for h in (pair, pair + 1):
                    a, v = decays(h)
                if pair == HPG - 2:
                    cs_read.append(a)
                    cb_read.append(v)
                    if g + 1 < GROUPS:
                        load_cs(g + 1)
                yield
                bank = high.take(pe)
                for h in (pair, pair + 1):
                    e, v = m_ready[h]
                    rows = slice((h % 2) * HD, (h % 2 + 1) * HD)
                    mm(bank.ap[rows, 0:SEQ], xdt[:, 0, h * HD:(h + 1) * HD], e.ap[:, 0:SEQ], True, False,
                       after=[v, xdt_ready])
                    inst = mm(bank.ap[rows, P:SEQ], xdt[:, 1, h * HD:(h + 1) * HD], e.ap[:, SEQ:KQ], False, True)
                    e.users = [pe.count_up(inst)]
                token = e.users[0]
                k = GC * g + pair // 2
                xbc_y = stt(xbc[:, k, :], xbc[:, k, :], param("d_skip", k), bank.ap[:, 0:SEQ], ALU.mult, ALU.add,
                            after=[token])
                bank.users = [xbc_y]
            xdt_read.append(token)
            y_ready[g] = xbc_y
            yield

        def all_ssd():
            for g in range(GROUPS):
                yield from ssd(g)

        gate_ready = [None] * (2 * DC)

        def evacuate_gate(k0):
            def go(bank, token):
                for m in range(2):
                    a = fn(gates[:, k0 + m, :], bank.ap[:, m * SEQ:(m + 1) * SEQ], ACT.Tanh,
                           after=[token, half_g, lru_done], scale=0.5, bias=param("b_gate", k0 + m))
                bank.users = [a]
                g = gates[:, k0:k0 + 2, :]
                gate_ready[k0] = gate_ready[k0 + 1] = ts(g, g, 0.5, ALU.mult, 0.5, ALU.add, after=[a])
            return go

        ssd_work = all_ssd()
        for n, (kind, i) in enumerate(XS_AND_GATES):
            if n == 2:
                finish(scan)
                background.append(ssd_work)
            up(kind, 0, low, evacuate_xbc(2 * i) if kind == "xs" else evacuate_gate(2 * i))

        lru_out = [None] * LC

        def evacuate_ly(k0):
            def go(bank, token):
                q = tmps.take(act)
                x2 = bank.ap
                a = fn(q.ap, x2, ACT.Square, after=[token], scale=float(np.sqrt(0.044715)))
                v = stt(q.ap, q.ap, 1.0, x2, ALU.add, ALU.mult, after=[a])
                a = fn(q.ap, q.ap, ACT.Tanh, after=[v], scale=float(np.sqrt(2 / np.pi)))
                v = stt(q.ap, q.ap, 1.0, x2, ALU.add, ALU.mult, after=[a])
                bank.users = [v]
                hs = lru_u[:, k0:k0 + 2, :]
                v = stt(hs, q.ap.rearrange("p (k t) -> p k t", k=2), 0.5, hs, ALU.mult, ALU.mult,
                        after=[v, lru_done[k0], lru_done[k0 + 1]])
                q.users = [v]
                lru_out[k0] = lru_out[k0 + 1] = v
            return go

        for i in range(LC // 2):
            up("ly", 0, low, evacuate_ly(2 * i))

        z_ready = [None] * (2 * GC)
        z_read = [None, None]

        def evacuate_z(k0):
            def go(bank, token):
                th = tmps.take(act)
                a = fn(th.ap, bank.ap, ACT.Tanh, after=[token], scale=0.5)
                j = k0 % (2 * GC)
                assert y_ready[k0 // GC]
                v = stt(th.ap, th.ap, 1.0, bank.ap, ALU.add, ALU.mult, after=[a])
                bank.users = [v]
                v = stt(z_silu[:, j:j + 2, :], th.ap.rearrange("p (k t) -> p k t", k=2), 0.5, xbc[:, k0:k0 + 2, :],
                        ALU.mult, ALU.mult, after=[v, y_ready[k0 // GC], z_read[j // GC]])
                th.users = [v]
                z_ready[j] = z_ready[j + 1] = v
            return go

        def group_norm(g):
            z0 = GC * (g % 2)
            squares = []
            for j in range(GC // 2):
                sq = tmps.take(act)
                a = fn(sq.ap, z_silu[:, z0 + 2 * j:z0 + 2 * j + 2, :], ACT.Square, after=[z_ready[z0 + 2 * j]])
                squares.append((sq, a))
            yield
            bank = low.take(pe)
            for j, (sq, a) in enumerate(squares):
                for m in range(2):
                    inst = feature_mean(bank.ap[:, 0:SEQ], sq.ap[:, m * SEQ:(m + 1) * SEQ], c["mean_group"],
                                        j == 0 and m == 0, j == 1 and m == 1, after=[a])
                sq.users = [pe.count_up(inst)]
            scale, read = rms_scale(bank.ap[:, 0:SEQ], rstd[:, :], after=[*sq.users, *norm_users])
            norm_users.clear()
            bank.users = [read]
            yield
            for j in range(GC // 2):
                n = tmps.take(vec)
                for m in range(2):
                    k = GC * g + 2 * j + m
                    t = stt(n.ap[:, m * SEQ:(m + 1) * SEQ], z_silu[:, z0 + 2 * j + m, :], param("norm_w", k),
                            rstd[:, :], ALU.mult, ALU.mult, after=[scale])
                n.users = split_into(8 + GC * (g % 2) + 2 * j, 2, n.ap.rearrange("p (k t) -> p k t", k=2), after=[t])
            z_read[g % 2] = t
            norm_users.append(t)
            yield

        norms = []
        def down_ssm(g):
            for i in range(2):
                k = 8 + GC * (g % 2) + 2 * i
                tokens = down("out_ssm", (k, k + 1), ssm_acc, g == 0 and i == 0, g == GROUPS - 1 and i == 1)
            return tokens

        def down_lru(i):
            return down("out_lru", (2 * i, 2 * i + 1), lru_acc, i == 0, i == LC // 2 - 1)

        for g in range(GROUPS):
            for i in range(2):
                up("z", 0, low, evacuate_z(GC * g + 2 * i))
            norms.append(group_norm(g))
            background.append(norms[g])
            if g == 1:
                finish(ssd_work)
                ssm_acc = [high.take(pe) for _ in range(4)]
            if g == GROUPS - 1:
                for k in range(0, 8, 2):
                    split_into(k, 2, lru_u[:, k:k + 2, :], after=[lru_out[k]])
            if g:
                finish(norms[g - 1])
                down_ssm(g - 1)
        finish(norms[GROUPS - 1])
        split_into(8, 2, lru_u[:, 8:10, :], after=[lru_out[8]])
        lru_acc = [low.take(pe) for _ in range(4)]
        for i in range(LC // 2 - 1):
            down_lru(i)
        tokens = down_ssm(GROUPS - 1)
        for b in range(4):
            g = gates[:, 2 * b:2 * b + 2, :]
            t = tt(g, g, ssm_acc[b].ap.rearrange("p (k t) -> p k t", k=2), ALU.mult, after=[tokens[b], gate_ready[2 * b]])
            ssm_acc[b].users = [t]
            gate_ready[2 * b] = t
        tokens = down_lru(LC // 2 - 1)
        for b in range(4):
            g = gates[:, DC + 2 * b:DC + 2 * b + 2, :]
            t = tt(g, g, lru_acc[b].ap.rearrange("p (k t) -> p k t", k=2), ALU.mult, after=[tokens[b], gate_ready[DC + 2 * b]])
            lru_acc[b].users = [t]
            t = tt(g, g, gates[:, 2 * b:2 * b + 2, :], ALU.add, after=[t, gate_ready[2 * b]])
            split_into(2 * b, 2, g, after=[t], lo_on=vec)

        def project_to_residual(name, chunks_of, n, ring, before=None):
            banks_ = [ring.take(pe) for _ in range(4)]
            for i in range(n):
                if before:
                    before(i)
                tokens = down(name, chunks_of(i), banks_, i == 0, i == n - 1)
            add_residual(banks_, tokens)

        def add_residual(banks_, tokens):
            for b in range(4):
                r = res[:, 2 * b:2 * b + 2, :]
                t = tt(r, r, banks_[b].ap.rearrange("p (k t) -> p k t", k=2), ALU.add,
                       after=[tokens[b], res_ready[2 * b], norm_users, act.last() if b == 0 else None])
                banks_[b].users = [t]
                res_ready[2 * b] = res_ready[2 * b + 1] = t

        project_to_residual("out", lambda i: (2 * i, 2 * i + 1), DC // 2, high)

        one_done = [vec.last(), act.last(), pe.last(), pool.last()]
        one.close()

        two = ExitStack()
        ctx.enter_context(two)
        con2 = sb("consts_2", [P, sum(n for _, n in CONSTS_2)], stack=two)
        sp.wait(one_done)
        nc.sync.dma_start(con2[:, :], consts_2).then_inc(s_consts_2, 16)
        loaded2 = (s_consts_2, 16)
        at = 0
        for name, n in CONSTS_2:
            c[name] = con2[:, at:at + n]
            at += n
        ckv_t = sb("ckv_t", [P, SEQ], stack=two)
        ukv = sb("ukv", [P, 2, DSA_W], stack=two)
        rstd_tok = sb("rstd_tok", [P, 2 * TT], stack=two)
        w_norms = sb("w_norms", [P, DC], stack=two)
        ki_t = sb("ki_t", [P, SEQ], stack=two)
        w_idx = sb("w_idx", [P, TT, IDX_H], stack=two)
        qi_t = sb("qi_t", [P, IDX_H * HD // P, SEQ], stack=two)
        dq_t = sb("dq_t", [P, 2, SEQ], stack=two)
        dk_t = sb("dk_t", [P, 2, SEQ], stack=two)
        dv = sb("dv", [P, TT, DSA_W], stack=two)
        relu = Ring([sb(f"relu_{i}", [P, 512], stack=two)[:, :] for i in range(2)])
        score = sb("score", [P, KQ], stack=two)
        work = [sb(f"work_{i}", [P, KQ], stack=two) for i in range(2)]
        keep = sb("keep", [P, KQ], stack=two)
        top8 = sb("top8", [P, 2, 8], stack=two)
        rq_t = sb("rq_t", [P, 2, SEQ], stack=two)
        rk_t = sb("rk_t", [P, 2, SEQ], stack=two)
        rv = sb("rv", [P, TT, RET_W], stack=two)
        rg_t = sb("rg_t", [P, 2, SEQ], stack=two)
        ro_t = sb("ro_t", [P, 2, SEQ], stack=two)
        lq_t = sb("lq_t", [P, 4, SEQ], stack=two)
        lk_t = sb("lk_t", [P, 4, SEQ], stack=two)
        lv = sb("lv", [P, TT, DIL_W], stack=two)
        probs = Ring([sb(f"probs_{i}", [P, KQ], stack=two)[:, :] for i in range(6)])
        probs_t = Ring([sb(f"probs_t_{i}", [P, KQ], stack=two)[:, :] for i in range(4)])
        stats = Ring([sb(f"stats_{i}", [P, 8], stack=two)[:, :] for i in range(6)])

        def ffn_scale():
            bank, after = mean_square(low)
            late["ready"] = scale_of(bank, after)
            return
            yield

        begin_norm(8, param("norm2", 0, DC), ffn_scale())
        acc = [high.take(pe) for _ in range(4)]
        silu_gate = {}

        def evacuate_ffn_gate(bank, token):
            th, s = tmps.take(act), tmps.take(vec)
            g = by_scale(pair(s.ap), pair(bank.ap), [token])
            bank.users = [g]
            a = fn(th.ap, s.ap, ACT.Tanh, after=[g], scale=0.5)
            v = stt(s.ap, th.ap, 1.0, s.ap, ALU.add, ALU.mult, after=[a, g])
            th.users = [v]
            v = by_scale(pair(s.ap), pair(s.ap), [v])
            norm_users.append(v)
            silu_gate["s"], silu_gate["v"] = s, v

        def evacuate_ffn_up(k):
            def go(bank, token):
                s = silu_gate["s"]
                v = stt(s.ap, s.ap, 0.5, bank.ap, ALU.mult, ALU.mult, after=[token, silu_gate["v"]])
                bank.users = [v]
                s.users = split_into(k, 2, pair(s.ap), after=[v])
            return go

        nf = FFN // 256
        for i in range(nf + 1):
            if i < nf:
                up("ffn_gate", 8, low, evacuate_ffn_gate)
                up("ffn_up", 8, low, evacuate_ffn_up(2 * (i % 4)))
            if i:
                k = 2 * ((i - 1) % 4)
                tokens = down("ffn_out", (k, k + 1), acc, i == 1, i == nf)
        add_residual(acc, tokens)

        PAIRS = ((0, 0, P), (1, P, KQ))

        def value_product(o, pt, v0, v1, after):
            mm(o, v0, pt[:, 0:SEQ], True, False, after=after)
            return mm(o[:, P:SEQ], v1, pt[:, SEQ:KQ], False, True)

        def head_rows(t, h):
            return t[(h % 2) * HD:(h % 2 + 1) * HD, h // 2, :]

        def attention(n_heads, q, k, v, additive, count, ready, out_chunk):

            def scores(h):
                bank = high.take(pe)
                qh, kh = head_rows(q, h), head_rows(k, h)
                mm(bank.ap[:, 0:P], qh[:, 0:P], kh[:, 0:P], after=ready)
                token = pe.count_up(mm(bank.ap[:, P:KQ], qh[:, P:SEQ], kh[:, :]))
                p, st = probs.take(vec), stats.take(vec)
                t = stt(p.ap, bank.ap[:, 0:KQ], SCALE, additive, ALU.mult, ALU.add, after=[token, *ready, loaded2])
                bank.users = [t]
                vec.wait(t)
                for i, a, b in PAIRS:
                    t = vec.count_up(nc.vector.tensor_reduce(st.ap[:, i:i + 1], p.ap[:, a:b], AX_X, ALU.max, negate=True))
                for i, a, b in PAIRS:
                    e = fn(p.ap[:, a:b], p.ap[:, a:b], ACT.Exp, after=[t], bias=st.ap[:, i:i + 1],
                           accum=st.ap[:, 2 + i:3 + i] if count is None else None)
                return p, st, e

            def normalise(p, st, e):
                if count is not None:
                    for i, a, b in PAIRS:
                        e = stt(p.ap[:, a:b], p.ap[:, a:b], 1.0, count[:, a:b], ALU.mult, ALU.mult, after=[e],
                                accum=st.ap[:, 2 + i:3 + i])
                r_ = recip(st.ap[:, 4:6], st.ap[:, 2:4], after=[e])
                for i, a, b in PAIRS:
                    n = ts(p.ap[:, a:b], p.ap[:, a:b], st.ap[:, 4 + i:5 + i], ALU.mult, after=[r_])
                st.users = [n]
                return p, n

            def turn(p, n):
                bank = high.take(pe)
                for j in range(3):
                    inst = transpose(bank.ap[:, j * P:(j + 1) * P], p.ap[:, j * P:(j + 1) * P], after=[n])
                token = pe.count_up(inst)
                p.users = [token]
                pt = probs_t.take(act)
                cp = fn(pt.ap, bank.ap[:, 0:KQ], ACT.Copy, after=[token])
                bank.users = [cp]
                return pt, cp

            def values(h0, turned):
                bank = high.take(pe)
                for h, (pt, cp) in zip((h0, h0 + 1), turned):
                    o = bank.ap[(h % 2) * HD:(h % 2 + 1) * HD, 0:SEQ]
                    token = pe.count_up(value_product(o, pt.ap, v[:, 0, h * HD:(h + 1) * HD],
                                                      v[:, 1, h * HD:(h + 1) * HD], [cp, ready]))
                    pt.users = [token]
                split_from_psum(out_chunk + h0 // 2, bank, token)

            pair_n, turned = None, None
            for h0 in range(0, n_heads + 2, 2):
                scored = [scores(h) for h in (h0, h0 + 1)] if h0 < n_heads else None
                if pair_n:
                    turned = [turn(*x) for x in pair_n]
                yield
                pair_n = [normalise(*x) for x in scored] if scored else None
                if turned:
                    values(h0 - 2, turned)
                    turned = None
                    yield
                elif h0 == 0:
                    yield

        def split_from_psum(k, bank, token):
            hi, lo = act_hi[:, k, :], act_lo[:, k, :]
            a = fn(hi, bank.ap[:, 0:SEQ], ACT.Copy, after=[token, chunk_users[k]])
            b = tt(lo, bank.ap[:, 0:SEQ], hi.bitcast(F32), ALU.subtract, after=[a, token, chunk_users[k]])
            bank.users = [b]
            chunk_users[k] = None
            chunk_ready[k] = [a, b]

        def plain(dst, ready):
            def go(bank, token):
                t = by_scale(dst, pair(bank.ap), [token])
                bank.users = [t]
                norm_users.append(t)
                ready.append(t)
            return go

        def plain_tokens(dst, ready):
            def go(bank, token):
                for t in range(TT):
                    a = fn(dst[:, t, :], bank.ap[:, t * 256:(t + 1) * 256], ACT.Copy, after=[token, late["ready"]],
                           scale=rstd_tok[:, t:t + 1])
                bank.users = [a]
                ready.append(a)
            return go

        for e in (vec, act, pe, pool):
            e.wait(one_done)
        prev = []
        for l in range(DEPTH_2):
            base = 8
            for e in (vec, act, pe, pool):
                e.wait(prev)
            r = {}
            idx_ready, dsa_ready = [], []
            sp.wait(prev)
            for i, name in enumerate(("dsa_w_uk_2", "dsa_w_uv_2")):
                nc.sync.dma_start(ukv[:, i, :], w[name][l]).then_inc(s_ukv, 16)

            def layer_scale(first=l == 0):
                bank, after = mean_square(high)
                ready = scale_of(bank, after)
                if first:
                    copy(rstd_sq[:, :], rstd[:, :], after=[ready])
                    for k in range(DC):
                        t = stt(res[:, k, :], res[:, k, :], param("norm_f", k), rstd[:, :], ALU.mult, ALU.mult,
                                after=[ready, late["split"], act.last()])
                        res_ready[k] = t
                    norm_users.append(t)
                    yield
                    bank, after = mean_square(high)
                    ready = scale_of(bank, after)
                    ready = tt(rstd[:, :], rstd[:, :], rstd_sq[:, :], ALU.mult, after=[ready])
                yield
                bank = high.take(pe)
                for t in range(TT):
                    inst = transpose(bank.ap[:, t * P:(t + 1) * P], rstd[:, t * P:(t + 1) * P], after=[ready])
                token = pe.count_up(inst)
                src = bank.ap[:, 0:SEQ].rearrange("p (t j) -> p t j", t=TT)[:, :, 0]
                a = copy(rstd_tok[:, 0:TT], src, after=[token])
                b = ts(rstd_tok[:, TT:2 * TT], src, IDX_SCALE, ALU.mult, after=[token])
                bank.users = [b]
                late["ready"] = [ready, a, b]

            if l == 0:
                t = tt(w_norms[:, :], param("norm_f", 0, DC), param("attn", 0, DC), ALU.mult, after=[loaded])
                act.wait(t)
                begin_norm(base, w_norms, layer_scale())
            else:
                begin_norm(base, param("attn", DC * l, DC), layer_scale())

            def evacuate_ckv(bank, token):
                t = by_scale(ckv_t[:, :].unsqueeze(1), bank.ap[:, 0:SEQ].unsqueeze(1), [token], n=1)
                bank.users = [t]
                norm_users.append(t)
                r["ckv_raw"] = t

            up("ckv", base, low, evacuate_ckv, width=LATENT)

            def latent():
                sq = tmps.take(act)
                a = fn(sq.ap[:, 0:SEQ], ckv_t[:, :], ACT.Square, after=[r["ckv_raw"]])
                yield
                bank = high.take(pe)
                token = pe.count_up(mm(bank.ap[:, 0:SEQ], c["mean_latent"], sq.ap[:, 0:SEQ], after=[a]))
                scale, read = rms_scale(bank.ap[:, 0:SEQ], sq.ap[:, SEQ:512], after=[token])
                bank.users = [read]
                ckv = stt(ckv_t[:, :], ckv_t[:, :], param("kvn", l), sq.ap[:, SEQ:512], ALU.mult, ALU.mult,
                          after=[scale, r["ckv_raw"]])
                sq.users = [ckv]
                yield
                bank, bank2 = high.take(pe), high.take(pe)
                for m in range(2):
                    inst = mm(bank.ap[:, m * SEQ:(m + 1) * SEQ], ukv[:, 0, m * P:(m + 1) * P], ckv_t[:, :],
                              after=[(s_ukv, 32 * (l + 1)), ckv])
                t1 = pe.count_up(inst)
                for t in range(TT):
                    inst = mm(bank2.ap[:, t * DSA_W:(t + 1) * DSA_W], ckv_t[:, t * P:(t + 1) * P], ukv[:, 1, :])
                t2 = pe.count_up(inst)
                a = copy(dk_t[:, :, :], pair(bank.ap), after=[t1], on=act)
                b = copy(dv[:, :, :], pair(bank2.ap), after=[t2], on=act)
                bank.users, bank2.users = [a], [b]
                dsa_ready.extend([a, b])

            i, tile, ready = take("ki")
            bank = low.take(pe)
            pe.wait(ready)
            for k in range(DC):
                product(bank.ap[:, 0:SEQ], tile[:, k, 0:2 * HD], acts[:, base + k, :], k == 0, k == DC - 1)
            for t in range(TT):
                for k in range(DC):
                    inst = product(bank.ap[:, SEQ + t * IDX_H:SEQ + (t + 1) * IDX_H],
                                   acts[:, base + k, t * P:(t + 1) * P], tile[:, k, 2 * HD:2 * HD + IDX_H],
                                   k == 0, k == DC - 1)
            token = pe.count_up(inst)
            used(i, token)

            def evacuate_ki(bank, token):
                for t in range(TT):
                    a = fn(w_idx[:, t, :], bank.ap[:, SEQ + t * IDX_H:SEQ + (t + 1) * IDX_H], ACT.Copy,
                           after=[token, late["ready"]], scale=rstd_tok[:, TT + t:TT + t + 1])
                b = by_scale(ki_t[:, :].unsqueeze(1), bank.ap[:, 0:SEQ].unsqueeze(1), [a], n=1)
                bank.users = [b]
                norm_users.append(b)
                idx_ready.extend([a, b])

            run_late()
            evacuate_when_scaled(evacuate_ki, bank, token)
            advance()
            for j in range(2):
                up("qi", base, low, plain(qi_t[:, 2 * j:2 * j + 2, :], idx_ready))
            assert late["work"] is None
            kv = latent()
            background.append(kv)

            def select():
                for q, a, b in PAIRS:
                    n = b - a
                    per = 512 // n
                    halves = [h for half in (0, 1) for h in range(half, IDX_H, 2)]
                    for h0 in range(0, IDX_H, per):
                        bank = high.take(pe)
                        for j, h in enumerate(halves[h0:h0 + per]):
                            inst = mm(bank.ap[:, j * n:(j + 1) * n], head_rows(qi_t, h)[:, q * P:(q + 1) * P],
                                      ki_t[(h % 2) * HD:(h % 2 + 1) * HD, 0:n], after=idx_ready)
                        token = pe.count_up(inst)
                        rl = relu.take(act)
                        x = fn(rl.ap, bank.ap, ACT.Relu, after=[token])
                        bank.users = [x]
                        for j, h in enumerate(halves[h0:h0 + per]):
                            src = rl.ap[:, j * n:(j + 1) * n]
                            wt = w_idx[:, q, h:h + 1]
                            if h == 0:
                                t = ts(score[:, a:b], src, wt, ALU.mult, after=[x, idx_ready])
                            else:
                                t = stt(score[:, a:b], src, wt, score[:, a:b], ALU.mult, ALU.add, after=[x, t])
                        rl.users = [t]
                        yield
                    t = tt(score[:, a:b], score[:, a:b], c["causal"][:, a:b], ALU.add, after=[t, loaded2])
                yield
                src = score
                for step in range(TOPK // 8):
                    for q, a, b in PAIRS:
                        vec.wait(vec.last())
                        m = vec.count_up(nc.vector.max(top8[:, q, :], src[:, a:b]))
                        if step < TOPK // 8 - 1:
                            vec.wait(m)
                            vec.count_up(nc.vector.match_replace(work[step % 2][:, a:b], top8[:, q, :], src[:, a:b], TAKEN))
                    src = work[step % 2]
                    if step % 2:
                        yield
                more, eq, need = work[0], work[1], top8
                for q, a, b in PAIRS:
                    kth = top8[:, q, 7:8]
                    t1 = ts(more[:, a:b], score[:, a:b], kth, ALU.is_gt, after=[vec.last()])
                    t2 = ts(eq[:, a:b], score[:, a:b], kth, ALU.is_equal, after=[vec.last()])
                    vec.wait(t1, t2)
                    t3 = vec.count_up(nc.vector.tensor_reduce(need[:, q, 0:1], more[:, a:b], AX_X, ALU.add))
                    t3 = ts(need[:, q, 1:2], need[:, q, 0:1], -1.0, ALU.mult, float(TOPK), ALU.add, after=[t3])
                    vec.wait(t3)
                    t4 = vec.count_up(nc.vector.tensor_tensor_scan(keep[:, a:b], eq[:, a:b], eq[:, a:b], 0.0,
                                                                 ALU.add, ALU.max))
                    t5 = stt(eq[:, a:b], keep[:, a:b], need[:, q, 1:2], eq[:, a:b], ALU.is_le, ALU.mult, after=[t4])
                    t6 = tt(more[:, a:b], more[:, a:b], eq[:, a:b], ALU.add, after=[t5])
                    t7 = ts(more[:, a:b], more[:, a:b], -1.0, ALU.add, -MASKED, ALU.mult, after=[t6])
                    r["keep"] = tt(keep[:, a:b], more[:, a:b], c["causal"][:, a:b], ALU.min, after=[t7])
                yield

            sel = select()
            background.append(sel)
            up("dsa_q", base, low, plain(dq_t[:, :, :], dsa_ready))

            dil_ready = []
            for name, dst in (("dil_k", lk_t), ("dil_q", lq_t)):
                for j in range(2):
                    up(name, base, low, plain(dst[:, 2 * j:2 * j + 2, :], dil_ready))
            for j in range(2):
                up_tokens("dil_v", base, low, plain_tokens(lv[:, :, j * 256:(j + 1) * 256], dil_ready))
            dil = attention(DIL_H, lq_t, lk_t, lv, c["union"], c["count"], dil_ready, 4)
            background.append(dil)

            def rotary(name, dst, cos, sin):
                def go(bank, token):
                    raw_ = tmps.take(vec)
                    a = by_scale(pair(raw_.ap), pair(bank.ap), [token])
                    bank.users = [a]
                    norm_users.append(a)
                    r[name] = (raw_, a)
                return go

            def finish_rotary(name, dst, cos, sin):
                raw_, a = r[name]
                bank = high.take(pe)
                token = pe.count_up(mm(bank.ap, c["rotate"], raw_.ap, after=[a, loaded2]))
                both = lambda x: x.unsqueeze(1).broadcast_to([P, 2, SEQ])
                s = tmps.take(vec)
                t1 = tt(pair(s.ap), pair(bank.ap), both(sin), ALU.mult, after=[token])
                bank.users = [t1]
                t2 = tt(pair(raw_.ap), pair(raw_.ap), both(cos), ALU.mult, after=[a, token])
                t3 = tt(dst, pair(raw_.ap), pair(s.ap), ALU.add, after=[t1, t2])
                raw_.users, s.users = [t3], [t3]
                return t3

            k_args = ("k", rk_t[:, :, :], c["cos_k"], c["sin_k"])
            q_args = ("q", rq_t[:, :, :], c["cos"], c["sin"])
            rv_ready = []
            up("ret_k", base, low, rotary(*k_args))
            advance()
            up("ret_q", base, low, rotary(*q_args))
            rk_ready = finish_rotary(*k_args)
            advance()
            up_tokens("ret_v", base, low, plain_tokens(rv[:, :, :], rv_ready))
            rq_ready = finish_rotary(*q_args)
            advance()

            def evacuate_rg(bank, token):
                th = tmps.take(vec)
                g = by_scale(rg_t[:, :, :], pair(bank.ap), [token])
                bank.users = [g]
                norm_users.append(g)
                a = fn(pair(th.ap), rg_t[:, :, :], ACT.Tanh, after=[g, th.users], scale=0.5)
                v = stt(rg_t[:, :, :], pair(th.ap), 1.0, rg_t[:, :, :], ALU.add, ALU.mult, after=[a])
                th.users = [v]
                r["rg"] = v

            up("ret_g", base, low, evacuate_rg)

            def retention():
                for ch in range(2):
                    ms = []
                    for h in (2 * ch, 2 * ch + 1):
                        bank = high.take(pe)
                        q, k = head_rows(rq_t, h), head_rows(rk_t, h)
                        mm(bank.ap[:, 0:SEQ], k[:, 0:P], q, after=[rk_ready, rq_ready])
                        token = pe.count_up(mm(bank.ap[:, SEQ:KQ], k[:, P:SEQ], q[:, P:SEQ]))
                        m = tmps.take(vec)
                        dec = c["decay"][:, h * SEQ:(h + 1) * SEQ]
                        tt(m.ap[:, 0:SEQ], bank.ap[:, 0:SEQ], dec, ALU.mult, after=[token])
                        t = tt(m.ap[:, SEQ:KQ], bank.ap[:, SEQ:KQ], dec[:, 0:P], ALU.mult)
                        bank.users = [t]
                        ms.append((m, t))
                    yield
                    bank = high.take(pe)
                    for h, (m, t) in zip((2 * ch, 2 * ch + 1), ms):
                        o = bank.ap[(h % 2) * HD:(h % 2 + 1) * HD, 0:SEQ]
                        token = pe.count_up(value_product(o, m.ap, rv[:, 0, h * HD:(h + 1) * HD],
                                                        rv[:, 1, h * HD:(h + 1) * HD], [t, rv_ready]))
                        m.users = [token]
                    cp = copy(ro_t[:, ch, :], bank.ap[:, 0:SEQ], after=[token])
                    bank.users = [cp]
                    yield
                    bank = high.take(pe)
                    token = pe.count_up(mm(bank.ap[:, 0:SEQ], c["mean_head"], ro_t[:, ch, :], after=[cp]))
                    t = tt(ro_t[:, ch, :], ro_t[:, ch, :], bank.ap[:, 0:SEQ], ALU.subtract, after=[token])
                    bank.users = [t]
                    sq = tmps.take(act)
                    a = fn(sq.ap[:, 0:SEQ], ro_t[:, ch, :], ACT.Square, after=[t])
                    bank = high.take(pe)
                    token = pe.count_up(mm(bank.ap[:, 0:SEQ], c["mean_head"], sq.ap[:, 0:SEQ], after=[a]))
                    scale, read = rms_scale(bank.ap[:, 0:SEQ], sq.ap[:, SEQ:512], after=[token])
                    bank.users = [read]
                    t = stt(sq.ap[:, SEQ:512], sq.ap[:, SEQ:512], param("ret", 2 * l + ch), rg_t[:, ch, :],
                            ALU.mult, ALU.mult, after=[scale, r["rg"]])
                    t = stt(sq.ap[:, 0:SEQ], sq.ap[:, SEQ:512], 0.5, ro_t[:, ch, :], ALU.mult, ALU.mult,
                            after=[t, token])
                    sq.users = split_into(ch, 1, sq.ap[:, 0:SEQ].unsqueeze(1), after=[t])
                    yield

            ret = retention()
            background.append(ret)
            out_acc = [low.take(pe) for _ in range(4)]
            finish(kv, sel)
            dsa = attention(DSA_H, dq_t, dk_t, dv, keep[:, :], None, [dsa_ready, r["keep"]], 2)
            background.append(dsa)
            for n, i in enumerate(OUT_ORDER):
                finish(*{2: [dil], 3: [dil], 0: [ret], 1: [dsa]}[i])
                tokens = down("out_2", (2 * i, 2 * i + 1), out_acc, n == 0, n == len(OUT_ORDER) - 1)
            prev = [vec.last(), act.last(), pe.last(), pool.last()]
            add_residual(out_acc, tokens)

            def mlp_scale():
                bank, after = mean_square(high)
                ready = scale_of(bank, after)
                late["ready"] = ready
                return
                yield

            begin_norm(8, param("mlp", DC * l, DC), mlp_scale())

            def evacuate_up(k):
                def go(bank, token):
                    s = tmps.take(vec)
                    t = by_scale(pair(s.ap), pair(bank.ap), [token])
                    bank.users = [t]
                    norm_users.append(t)
                    v = stt(s.ap, s.ap, 0.0, s.ap, ALU.max, ALU.mult, after=[t])
                    s.users = split_into(k, 2, pair(s.ap), after=[v])
                return go

            acc = [low.take(pe) for _ in range(4)]
            nf = FF2 // 256
            for i in range(nf + 2):
                if i < nf:
                    up("up", 8, high, evacuate_up(2 * (i % 4)))
                if i >= 2:
                    k = 2 * ((i - 2) % 4)
                    tokens = down("down", (k, k + 1), acc, i == 2, i == nf + 1)
            add_residual(acc, tokens)

        done = norm_to(0, "final", 0, high, write=res)
        sp.wait(done)
        nc.sync.dma_start(out_t, res[:, :, :]).then_inc(s_store, 16)
        nc.sync.wait_ge(s_store, 16)
        nc.sync.wait_ge(s_spill, 16)
        assert state["next_take"] == len(plan)


def shape_constants():
    ident = np.eye(P)
    tri = np.triu(np.ones((P, P)))
    block = np.kron(np.eye(2), np.ones((HD, HD)) / HD)
    first = {
        "ident": ident, "mean_d": np.full((P, P), 1 / D), "mean_group": np.full((P, P), GROUPS / D_INNER),
        "mean_latent": np.full((P, P), 1 / LATENT), "mean_head": block,
        "tri": np.concatenate([tri, np.ones((P, P)), tri], 1), "eps": np.full((P, 1), EPS),
    }
    rot = np.zeros((P, P))
    half = HD // 2
    for h in range(P // HD):
        for i in range(half):
            rot[h * HD + half + i, h * HD + i] = -1.0
            rot[h * HD + i, h * HD + half + i] = 1.0
    inv = np.float32(10000.0) ** (-np.arange(half, dtype=np.float32) / half)
    ang = (np.arange(SEQ, dtype=np.float32)[None, :] * inv.astype(np.float32)[:, None]).astype(np.float32)
    ang = np.tile(ang, (P // half, 1)).astype(np.float64)
    pos = np.arange(SEQ)
    gamma = np.log(1.0 - 2.0 ** (-5.0 - np.arange(RET_H)))
    diff = pos[None, :] - np.arange(P)[:, None]
    decay = np.concatenate([np.exp(np.maximum(diff, 0) * g) * (diff >= 0) for g in gamma], 1)
    q, k = pos[:, None], pos[None, :]
    dist = q - k
    cnt = ((dist >= 0) & (dist <= 128)).astype(int)
    for dil in (4, 16):
        cnt += (dist >= 0) & (dist % dil == 0)
    pairs = lambda m: np.concatenate([m[0:P, 0:P], m[P:SEQ, :]], 1)
    second = {
        "rotate": rot, "cos": np.cos(ang), "sin": np.sin(ang), "cos_k": np.cos(ang) * SCALE, "sin_k": np.sin(ang) * SCALE,
        "decay": decay, "causal": pairs(np.where(dist >= 0, 0.0, MASKED)),
        "union": pairs(np.where(cnt > 0, 0.0, MASKED)), "count": pairs(cnt),
    }
    pack = lambda names, d: np.concatenate([d[n] for n, _ in names], 1).astype(np.float32)
    return pack(CONSTS, first), pack(CONSTS_2, second)


def pack_params(a):
    def chunks(v):
        return np.ascontiguousarray(v.reshape(-1, P).T)

    def padded(v):
        return np.concatenate([v, np.zeros(P - len(v), v.dtype)])[:, None]

    cols = {
        "norm1": chunks(a["norm1_w"]), "conv_w": chunks(a["ssm_conv_w"]), "conv_b": chunks(a["ssm_conv_b"]),
        "lconv_w": chunks(a["lru_conv_w"]), "lconv_b": chunks(a["lru_conv_b"]), "b_r": chunks(a["lru_b_r"]),
        "b_i": chunks(a["lru_b_i"]), "lam": chunks(a["lru_lambda"]), "b_gate": chunks(a["b_branch_gate"]),
        "norm_w": chunks(a["ssm_norm_w"]), "d_skip": chunks(np.repeat(a["ssm_d"].reshape(-1), HD)),
        "norm2": chunks(a["norm2_w"]), "dt_bias": padded(a["ssm_dt_bias"].reshape(-1)),
        "a_log": padded(a["ssm_a_log"].reshape(-1)), "attn": chunks(a["attn_norm_w_2"]), "mlp": chunks(a["mlp_norm_w_2"]),
        "ret": chunks(a["ret_norm_w_2"]), "kvn": chunks(a["dsa_kv_norm_w_2"]), "norm_f": chunks(a["norm_f_w"]), "final": chunks(a["final_norm_w_2"]),
    }
    return np.ascontiguousarray(np.concatenate([cols[n] for n, _ in PARAMS], 1))


WEIGHTS = ["w_in", "w_out_ssm", "lru_w_r", "lru_w_i", "w_out_lru", "w_out", "w_ffn_in", "w_ffn_out",
           "w_in_2", "dsa_w_uk_2", "dsa_w_uv_2", "w_out_2", "w_up_2", "w_down_2"]


def kernel(**inputs):
    import concourse.bacc as bacc
    from concourse.bass_utils import run_bass_kernel_spmd

    a = {k: np.asarray(v) for k, v in inputs.items()}
    consts, consts_2 = shape_constants()
    arrays = {k: (np.ascontiguousarray(a[k]) if k.endswith("_2") else np.ascontiguousarray(a[k][0])) for k in WEIGHTS}
    arrays["x_t"] = np.ascontiguousarray(a["x"][0].T.reshape(DC, P, SEQ).transpose(1, 0, 2))
    arrays["params"], arrays["consts"], arrays["consts_2"] = pack_params(a), consts, consts_2
    nc = bacc.Bacc("TRN2", target_bir_lowering=False, num_devices=1)
    aps = {k: nc.dram_tensor(f"in_{k}", v.shape, F32, kind="ExternalInput").ap() for k, v in arrays.items()}
    out = nc.dram_tensor("out_t", (P, DC, SEQ), F32, kind="ExternalOutput").ap()
    build(nc, {k: aps[k] for k in WEIGHTS}, aps["x_t"], aps["params"], aps["consts"], aps["consts_2"], out)
    r = run_bass_kernel_spmd(nc, [{f"in_{k}": v for k, v in arrays.items()}], core_ids=[0])
    got = r.results[0]["out_t"]
    return np.ascontiguousarray(got.transpose(1, 0, 2).reshape(D, SEQ).T)[None]
```

```python
from contextlib import ExitStack

import numpy as np

import concourse.bass as bass
from concourse import mybir

F32 = mybir.dt.float32
F32R = mybir.dt.float32r
ACT = mybir.ActivationFunctionType
ALU = mybir.AluOpType
AX_X = mybir.AxisListType.X

P = 128
SEQ = 256
TT = SEQ // P
D = 1024
DC = D // P
EPS = 1e-6

D_INNER = 2048
HEADS = 32
HD = 64
GROUPS = 4
HPG = HEADS // GROUPS
STATE = 128
CONV = 4
XBC = D_INNER + 2 * GROUPS * STATE
LRU = 1280
LC = LRU // P
LRU_C = 8.0
FFN = 2816
COL_GATE = 0
COL_Z = 2 * D
COL_XBC = COL_Z + D_INNER
COL_B = COL_XBC + D_INNER
COL_C = COL_B + GROUPS * STATE
COL_DT = COL_XBC + XBC
COL_LX = COL_DT + HEADS
COL_LY = COL_LX + LRU
GC = D_INNER // GROUPS // P

DEPTH_2 = 2
RET_H, DSA_H, DIL_H = 4, 4, 8
RET_W, DSA_W, DIL_W = RET_H * HD, DSA_H * HD, DIL_H * HD
LATENT = 128
IDX_H = 8
TOPK = min(256, SEQ // 4)
FF2 = 4 * D
C_RET = 0
C_DSA = 4 * RET_W
C_CKV = C_DSA + DSA_W
C_QI = C_CKV + LATENT
C_KI = C_QI + IDX_H * HD
C_DIL = C_KI + HD + IDX_H
IDX_SCALE = float(IDX_H ** -0.5 * HD ** -0.5)
SCALE = float(HD) ** -0.5
MASKED = -3.0e38
TAKEN = -3.4e38

SCAN_TILES = 5
XS_AND_GATES = ([("xs", i) for i in range(SCAN_TILES)] +
                [t for i in range(8 - SCAN_TILES) for t in (("gate", i), ("xs", SCAN_TILES + i))] +
                [("gate", i) for i in range(8 - SCAN_TILES, 8)])

RAW_SLOTS, SPLIT_SLOTS = 3, 3
OUT_ORDER = (0, 2, 1, 3)
POOL_SHARE = {"lx": 4, "bc": 4, "xs": 5, "gate": 4, "ly": 6, "z": 5, "out_ssm": 4, "out_lru": 4, "out": 5,
              "dsa_q": 5, "ret_k": 5, "ret_q": 5, "ret_v": 5, "ret_g": 5, "dil_k": 7, "dil_q": 7, "dil_v": 8,
              "out_2": 8}
TILE = 2048
KQ = 3 * P

PARAMS = [
    ("norm1", DC), ("conv_w", CONV * XBC // P), ("conv_b", XBC // P), ("lconv_w", CONV * LC), ("lconv_b", LC),
    ("b_r", LC), ("b_i", LC), ("lam", LC), ("b_gate", 2 * DC), ("norm_w", D_INNER // P), ("d_skip", D_INNER // P),
    ("norm2", DC), ("dt_bias", 1), ("a_log", 1), ("attn", DC * DEPTH_2), ("mlp", DC * DEPTH_2),
    ("ret", RET_W // P * DEPTH_2), ("kvn", DEPTH_2), ("norm_f", DC), ("final", DC),
]
PARAM_AT, _n = {}, 0
for _name, _w in PARAMS:
    PARAM_AT[_name] = (_n, _w)
    _n += _w
N_PARAMS = _n

CONSTS = [("ident", P), ("mean_head", P), ("tri", KQ)]
CONSTS_2 = [("rotate", P), ("cos", SEQ), ("sin", SEQ), ("cos_k", SEQ), ("sin_k", SEQ), ("decay", RET_H * SEQ),
            ("causal", KQ), ("union", KQ), ("count", KQ)]


class Engine:

    def __init__(self, ops, sem):
        self.ops, self.sem, self.count, self.seen = ops, sem, 0, {}

    def wait(self, *tokens):
        for t in tokens:
            if t is None:
                continue
            if isinstance(t, list):
                self.wait(*t)
                continue
            sem, value = t
            if self.seen.get(sem.name, 0) < value:
                self.ops.wait_ge(sem, value)
                self.seen[sem.name] = value

    def count_up(self, inst):
        self.count += 1
        inst.then_inc(self.sem, 1)
        return (self.sem, self.count)

    def last(self):
        return (self.sem, self.count) if self.count else None


class Slot:
    def __init__(self, ap):
        self.ap, self.users = ap, []


class Ring:

    def __init__(self, aps):
        self.slots, self.n = [Slot(a) for a in aps], 0

    def take(self, writer):
        slot = self.slots[self.n % len(self.slots)]
        self.n += 1
        assert slot.users is not None, "still in use"
        writer.wait(slot.users)
        slot.users = None
        return slot


class Split:

    def __init__(self, hi, lo):
        self.hi, self.lo = hi, lo

    def __getitem__(self, key):
        return Split(self.hi[key], self.lo[key])


def weight_plan(w):
    plan = []

    def cols(name, mat, c0, n):
        src = mat[:, c0:c0 + n].rearrange("(k p) c -> p k c", p=P)
        plan.append((name, (DC, n), [((0, n), src)]))

    def rows(name, mat, k0, n=2):
        src = mat[k0 * P:(k0 + n) * P, :].rearrange("(k p) c -> p k c", p=P)
        plan.append((name, (n, D), [((0, D), src)]))

    w_in = w["w_in"]
    cols("dt", w_in, COL_DT, P)
    for i in range(LC // 2):
        cols("lx", w_in, COL_LX + 256 * i, 256)
    for i in range(4):
        cols("bc", w_in, COL_B + 256 * i, 256)
    for kind, i in XS_AND_GATES:
        cols(kind, w_in, (COL_XBC if kind == "xs" else COL_GATE) + 256 * i, 256)
    for i in range(LC // 2):
        cols("ly", w_in, COL_LY + 256 * i, 256)
    def out_ssm(g):
        for i in range(2):
            rows("out_ssm", w["w_out_ssm"], GC * g + 2 * i)

    for g in range(GROUPS):
        for i in range(2):
            cols("z", w_in, COL_Z + 512 * g + 256 * i, 256)
        if g >= 2:
            out_ssm(g - 2)
    out_ssm(GROUPS - 2)
    for i in range(LC // 2 - 1):
        rows("out_lru", w["w_out_lru"], 2 * i)
    out_ssm(GROUPS - 1)
    rows("out_lru", w["w_out_lru"], LC - 2)
    for i in range(DC // 2):
        rows("out", w["w_out"], 2 * i)
    nf = FFN // 256
    for i in range(nf + 1):
        if i < nf:
            cols("ffn_gate", w["w_ffn_in"], 256 * i, 256)
            cols("ffn_up", w["w_ffn_in"], FFN + 256 * i, 256)
        if i:
            rows("ffn_out", w["w_ffn_out"], 2 * (i - 1))
    for l in range(DEPTH_2):
        w2 = w["w_in_2"][l]
        cols("qi", w2, C_QI, 256)
        cols("ckv", w2, C_CKV, LATENT)
        ki = w2[:, C_KI:C_KI + HD].rearrange("(k p) c -> p k c", p=P)
        kiw = w2[:, C_KI:C_KI + HD + IDX_H].rearrange("(k p) c -> p k c", p=P)
        plan.append(("ki", (DC, 2 * HD + IDX_H), [((0, HD), ki), ((HD, 2 * HD + IDX_H), kiw)]))
        cols("qi", w2, C_QI + 256, 256)
        cols("dsa_q", w2, C_DSA, 256)
        for name, c in (("ret_k", 1), ("ret_q", 0), ("ret_v", 2), ("ret_g", 3)):
            cols(name, w2, C_RET + RET_W * c, 256)
        for i in range(2):
            for name, c in (("dil_k", 1), ("dil_q", 0), ("dil_v", 2)):
                cols(name, w2, C_DIL + DIL_W * c + 256 * i, 256)
        for i in OUT_ORDER:
            rows("out_2", w["w_out_2"][l], 2 * i)
        nf = FF2 // 256
        for i in range(nf + 2):
            if i < nf:
                cols("up", w["w_up_2"][l], 256 * i, 256)
            if i >= 2:
                rows("down", w["w_down_2"][l], 2 * (i - 2))
    return plan


def pool_shares(plan):
    names = [t[0] for t in plan]
    shares = [POOL_SHARE.get(name, 0) for name in names]
    shares[:2] = [0, 0]
    for i, name in enumerate(names):
        if (name, names[i - 1]) in (("ffn_gate", "out"), ("qi", "ffn_out"), ("qi", "down"), ("up", "out_2")):
            shares[i + 1] = shares[i + 2] = 4
    return shares


def build(nc, w, x_t, params, consts, consts_2, out_t, debug=None):
    ctx = ExitStack()
    with ctx:
        def sem(name):
            return ctx.enter_context(nc.semaphore(name))

        def sb(name, shape, dt=F32, stack=ctx):
            return stack.enter_context(nc.sbuf_tensor(name, shape, dt))

        pe = Engine(nc.tensor, sem("pe_done"))
        act = Engine(nc.scalar, sem("act_done"))
        vec = Engine(nc.vector, sem("vec_done"))
        pool = Engine(nc.gpsimd, sem("pool_done"))
        sp = Engine(nc.sync, sem("sync_engine"))
        dma_sems = [sem(f"tile_arrived_{i}") for i in range(RAW_SLOTS)]
        s_x = [sem(f"x_arrived_{i}") for i in range(DC // 2)]
        s_params = sem("params_arrived")
        s_consts = sem("consts_arrived")
        s_lru = sem("lru_weights_arrived")
        s_spill = sem("cs_spilled")
        s_bcast = sem("cs_broadcast")
        s_ukv = sem("ukv_arrived")
        s_consts_2 = sem("consts_2_arrived")
        s_store = sem("output_stored")

        res = sb("residual", [P, DC, SEQ])
        act_hi = sb("act_hi", [P, 16, SEQ], F32R)
        act_lo = sb("act_lo", [P, 16, SEQ], F32R)
        acts = Split(act_hi, act_lo)
        raw = [sb(f"raw_{i}", [P, TILE]) for i in range(RAW_SLOTS)]
        w_hi = [sb(f"w_hi_{i}", [P, TILE], F32R) for i in range(SPLIT_SLOTS)]
        w_lo = [sb(f"w_lo_{i}", [P, TILE], F32R) for i in range(SPLIT_SLOTS)]
        par = sb("params", [P, N_PARAMS])
        n_consts = sum(n for _, n in CONSTS)
        con = sb("consts", [P, n_consts])
        tmps = Ring([sb(f"tmp_{i}", [P, 512])[:, :] for i in range(5)])
        rstd = sb("rstd", [P, SEQ])
        rstd_sq = sb("rstd_sq", [P, SEQ])
        small = sb("small", [P, 96])

        banks = [ctx.enter_context(nc.psum_tensor(f"bank_{i}", [P, 512], F32)) for i in range(8)]
        low, high = Ring([b[:, :] for b in banks[:4]]), Ring([b[:, :] for b in banks[4:]])

        c, at = {}, 0
        for name, n in CONSTS:
            c[name] = con[:, at:at + n]
            at += n

        def param(name, i=0, n=1):
            a, width = PARAM_AT[name]
            assert i + n <= width
            return par[:, a + i:a + i + n]

        def tt(out, a, b, op, after=(), on=vec):
            on.wait(*after)
            return on.count_up(on.ops.tensor_tensor(out, a, b, op))

        def ts(out, a, s1, op0, s2=None, op1=None, after=(), on=vec):
            on.wait(*after)
            if op1 is None:
                return on.count_up(on.ops.tensor_scalar(out, a, s1, None, op0))
            return on.count_up(on.ops.tensor_scalar(out, a, s1, s2, op0, op1))

        def stt(out, a, s, b, op0, op1, after=(), accum=None):
            vec.wait(*after)
            return vec.count_up(nc.vector.scalar_tensor_tensor(out=out, in0=a, scalar=s, in1=b, op0=op0, op1=op1,
                                                             accum_out=accum))

        def fn(out, a, func, after=(), scale=1.0, bias=0.0, accum=None):
            act.wait(*after)
            return act.count_up(nc.scalar.activation(out, a, func, bias=bias, scale=scale, accum_out=accum))

        def copy(out, a, after=(), on=vec):
            if on is act:
                return fn(out, a, ACT.Copy, after)
            on.wait(*after)
            return on.count_up(on.ops.tensor_copy(out, a))

        def recip(out, a, after=()):
            vec.wait(*after)
            return vec.count_up(nc.vector.reciprocal(out, a))

        def mm(out, lhs, rhs, start=True, stop=True, after=()):
            pe.wait(*after)
            return nc.tensor.matmul(out, lhs, rhs, start=start, stop=stop, skip_group_check=True)

        def product(out, lhs, rhs, start, stop, after=()):
            pe.wait(*after)
            nc.tensor.matmul(out, lhs.hi, rhs.hi, start=start, stop=False, skip_group_check=True)
            nc.tensor.matmul(out, lhs.hi, rhs.lo, start=False, stop=False, skip_group_check=True)
            return nc.tensor.matmul(out, lhs.lo, rhs.hi, start=False, stop=stop, skip_group_check=True)

        def transpose(out, a, k=P, after=()):
            pe.wait(*after, consts_here)
            return nc.tensor.transpose(out, a, c["ident"][0:k, 0:k])

        def split_into(k, n, src, after=(), lo_on=pool):
            hi, lo = act_hi[:, k:k + n, :], act_lo[:, k:k + n, :]
            used = [chunk_users[j] for j in range(k, k + n)]
            a = copy(hi, src, after=[*after, used], on=act)
            b = tt(lo, src, hi.bitcast(F32), ALU.subtract, after=[*after, used, a], on=lo_on)
            for j in range(k, k + n):
                chunk_users[j] = None
                chunk_ready[j] = [a, b]
            return [a, b]

        chunk_users = [None] * 16
        chunk_ready = [None] * 16

        for name, n in (("mean_d", D), ("mean_group", D_INNER // GROUPS), ("mean_latent", LATENT)):
            c[name] = sb(name, [P, P])[:, :]
            filled = vec.count_up(nc.vector.memset(c[name], 1 / n))
        c["eps"] = sb("eps", [P, 1])[:, :]
        filled = vec.count_up(nc.vector.memset(c["eps"], EPS))
        act.wait(filled)
        pe.wait(filled)
        for k in range(0, DC, 2):
            nc.sync.dma_start(res[:, k:k + 2, :], x_t[:, k:k + 2, :]).then_inc(s_x[k // 2], 16)
        nc.scalar.dma_start(par[:, :], params).then_inc(s_params, 16)
        loaded, consts_here = (s_params, 16), (s_consts, 16)

        plan = weight_plan(w)
        dma_count = [0] * RAW_SLOTS
        shares = pool_shares(plan)
        arrived, tiles, raw_users = [None] * len(plan), [None] * len(plan), [None] * len(plan)
        split_users = [None] * len(plan)
        state = {"next_load": 0, "next_split": 0, "next_take": 0}

        def load_tile():
            i = state["next_load"]
            if i >= len(plan) or (i >= RAW_SLOTS and raw_users[i - RAW_SLOTS] is None):
                return
            state["next_load"] = i + 1
            slot = i % RAW_SLOTS
            _, (k, n), parts = plan[i]
            if i >= RAW_SLOTS:
                sp.wait(raw_users[i - RAW_SLOTS])
            tile = raw[slot][:, 0:k * n].rearrange("p (k c) -> p k c", k=k)
            for (a, b), src in parts:
                nc.sync.dma_start(tile[:, :, a:b], src).then_inc(dma_sems[slot], 16)
                dma_count[slot] += 16
            arrived[i] = (dma_sems[slot], dma_count[slot])
            load_tile()

        def split_tile():
            i = state["next_split"]
            state["next_split"] = i + 1
            assert arrived[i] is not None
            _, (k, n), _ = plan[i]
            src = raw[i % RAW_SLOTS][:, 0:k * n]
            slot = i % SPLIT_SLOTS
            free = split_users[i - SPLIT_SLOTS] if i >= SPLIT_SLOTS else None
            hi, lo = w_hi[slot][:, 0:k * n], w_lo[slot][:, 0:k * n]
            a = copy(hi, src, after=[arrived[i], free], on=act)
            cut = k * n * shares[i] // 8
            b = [tt(lo[:, p:q], src[:, p:q], hi[:, p:q].bitcast(F32), ALU.subtract, after=[arrived[i], free, a], on=on)
                 for on, p, q in ((pool, 0, cut), (vec, cut, k * n)) if q > p]
            raw_users[i] = [a, b]
            tiles[i] = (Split(hi.rearrange("p (k c) -> p k c", k=k), lo.rearrange("p (k c) -> p k c", k=k)), [a, b])
            load_tile()

        def take(name):
            i = state["next_take"]
            state["next_take"] = i + 1
            assert plan[i][0] == name, (plan[i][0], name)
            while state["next_split"] < min(i + SPLIT_SLOTS, state["next_load"]):
                split_tile()
            while rests:
                rests.pop(0)()
            return (i, *tiles[i])

        def used(i, token):
            split_users[i] = token

        load_tile()

        background = []
        rests = []

        def advance():
            for g in list(background):
                if next(g, "end") == "end":
                    background.remove(g)

        def finish(*gens):
            for g in gens:
                if g in background:
                    background.remove(g)
                    for _ in g:
                        pass

        def up(name, base, ring, evacuate, width=2 * P):
            i, tile, ready = take(name)
            bank = ring.take(pe)
            pe.wait(ready)
            early = DC - 2
            order = [(m, k) for ks in (range(early), range(early, DC)) for m in range(width // P) for k in ks]
            for n, (m, k) in enumerate(order):
                if n == len(order) // 2:
                    advance()
                inst = product(bank.ap[:, m * SEQ:(m + 1) * SEQ], tile[:, k, m * P:(m + 1) * P],
                               acts[:, base + k, :], n == 0, k == DC - 1, after=[chunk_ready[base + k]])
            token = pe.count_up(inst)
            for k in range(DC):
                chunk_users[base + k] = token
            used(i, token)
            run_late()
            evacuate_when_scaled(evacuate, bank, token)

        def up_tokens(name, base, ring, evacuate, width=2 * P):
            i, tile, ready = take(name)
            bank = ring.take(pe)
            pe.wait(ready)
            for t in range(TT):
                if t:
                    advance()
                for k in range(DC):
                    inst = product(bank.ap[:, t * width:(t + 1) * width], acts[:, base + k, t * P:(t + 1) * P],
                                   tile[:, k, :], k == 0, k == DC - 1, after=[chunk_ready[base + k]])
            token = pe.count_up(inst)
            for k in range(DC):
                chunk_users[base + k] = token
            used(i, token)
            run_late()
            evacuate_when_scaled(evacuate, bank, token)

        def down(name, chunks, acc, ring, first, last, advance_inside=False):
            i, tile, ready = take(name)
            pe.wait(ready)
            tokens = []
            for b in range(DC // 2):
                if advance_inside and b == DC // 4:
                    advance()
                if first:
                    acc.append(ring.take(pe))
                bank = acc[b]
                for j, k in enumerate(chunks):
                    for m in range(2):
                        inst = product(bank.ap[:, m * SEQ:(m + 1) * SEQ],
                                       tile[:, j, (2 * b + m) * P:(2 * b + m + 1) * P], acts[:, k, :],
                                       first and j == 0 and m == 0, last and j == 1, after=[chunk_ready[k]])
                tokens.append(pe.count_up(inst) if last or b == DC // 2 - 1 else None)
            for k in chunks:
                chunk_users[k] = tokens[-1]
            used(i, tokens[-1])
            advance()
            return tokens

        def rms_scale(mean, out, after):
            a = fn(out, mean, ACT.Sqrt, after=after, bias=c["eps"])
            return recip(out, out, after=[a]), a

        res_ready = [(s_x[k // 2], 16) for k in range(DC)]

        def add_up(pairs_of_squares):
            total, ready = pairs_of_squares[0]
            for sq, a in pairs_of_squares[1:]:
                ready = tt(total.ap, total.ap, sq.ap, ALU.add, after=[ready, a])
                sq.users = [ready]
            return total, ready

        def mean_of(total, ready, matrix, ring):
            bank = ring.take(pe)
            for m in range(2):
                inst = mm(bank.ap[:, 0:SEQ], matrix, total.ap[:, m * SEQ:(m + 1) * SEQ], m == 0, m == 1,
                          after=[ready])
            total.users = [pe.count_up(inst)]
            return bank, total.users

        def squares_of(chunks, after):
            out = []
            for j in range(chunks.shape[1] // 2):
                sq = tmps.take(act)
                out.append((sq, fn(sq.ap, chunks[:, 2 * j:2 * j + 2, :], ACT.Square, after=[after[2 * j:2 * j + 2]])))
            res_readers.append(out[-1][1])
            return out

        def mean_square(ring):
            return mean_of(*add_up(squares_of(res, res_ready)), c["mean_d"], ring)

        def norm_to(base, weight, w0, ring, meanwhile):
            bank, summed = mean_square(ring)
            meanwhile()
            scale_ready, read = rms_scale(bank.ap[:, 0:SEQ], rstd[:, :], after=[summed, norm_users])
            bank.users = [read]
            norm_users.clear()
            made = []
            for j in range(DC // 2):
                n = tmps.take(vec)
                for m in range(2):
                    k = 2 * j + m
                    t = stt(n.ap[:, m * SEQ:(m + 1) * SEQ], res[:, k, :], param(weight, w0 + k), rstd[:, :],
                            ALU.mult, ALU.mult, after=[scale_ready, loaded])
                made.append((j, n, t))
                for j_, n_, t_ in made[:-1] if j < DC // 2 - 1 else made:
                    n_.users = split_into(base + 2 * j_, 2, pair(n_.ap), after=[t_],
                                          lo_on=pool if j_ == DC // 2 - 2 else vec)
                made = made[-1:]
            norm_users.append(t)

        res_readers = []
        norm_users = []
        late = {"work": None, "evacuations": [], "ready": None}

        def run_late():
            if late["work"] is not None and next(late["work"], "end") == "end":
                late["work"] = None
                for go in late["evacuations"]:
                    go()
                late["evacuations"] = []

        def evacuate_when_scaled(go, bank, token):
            def whole():
                rest = go(bank, token)
                if rest:
                    rests.append(rest)

            if late["work"] is None:
                whole()
            else:
                late["evacuations"].append(whole)

        def begin_norm(base, weight, work, banks_, tokens):
            def split(k):
                hi, lo = act_hi[:, base + k, :], act_lo[:, base + k, :]
                a = fn(hi, res[:, k, :], ACT.Copy, after=[res_ready[k], chunk_users[base + k], loaded],
                       scale=weight[:, k:k + 1])
                b = stt(lo, res[:, k, :], weight[:, k:k + 1], hi.bitcast(F32), ALU.mult, ALU.subtract,
                        after=[a, res_ready[k], chunk_users[base + k]])
                chunk_users[base + k] = None
                chunk_ready[base + k] = [a, b]
                late["split"] = [a, b]
                res_readers.extend([a, b])

            last_use = [list(norm_users), list(res_readers)]
            res_readers.clear()
            for b in range(4):
                add_residual(b, banks_[b], tokens[b], last_use)
                if b in (1, 2):
                    split(2 * b - 2)
                    split(2 * b - 1)
                if b >= 2:
                    split(2 * b)
                    split(2 * b + 1)
            late["total"] = add_up(squares_of(res, res_ready))
            late["work"] = work

        def add_residual(b, bank, token, last_use):
            r = res[:, 2 * b:2 * b + 2, :]
            t = tt(r, r, pair(bank.ap), ALU.add, after=[token, res_ready[2 * b], last_use])
            bank.users = [t]
            res_ready[2 * b] = res_ready[2 * b + 1] = t

        def scale_of(bank, after):
            ready, read = rms_scale(bank.ap[:, 0:SEQ], rstd[:, :], after=[after, norm_users])
            bank.users = [read]
            norm_users.clear()
            return ready

        def by_scale(out, src, after, n=2):
            return tt(out, src, rstd[:, :].unsqueeze(1).broadcast_to([P, n, SEQ]), ALU.mult,
                      after=[late["ready"], *after])

        def pair(x):
            return x.rearrange("p (k t) -> p k t", k=2)

        one = ExitStack()
        xbc = sb("xbc", [P, XBC // P, SEQ], stack=one)
        lru_u = sb("lru_u", [P, LC, SEQ], stack=one)
        lru_ab = sb("lru_ab", [P, 2 * LC, SEQ], stack=one)
        lru_a, lru_b = lru_ab[:, 0:LC, :], lru_ab[:, LC:2 * LC, :]
        gates = lru_ab[:, 0:2 * DC, :]
        cs_all = sb("cs_all", [P, HPG, SEQ], stack=one)
        xdt = sb("xdt", [P, TT, GC * P], stack=one)
        z_silu = sb("z_silu", [P, 2 * GC, SEQ], stack=one)
        cb_mask = sb("cb_mask", [P, KQ], stack=one)
        lru_w = xbc[:, 0:2 * LC * P // SEQ, :].rearrange("p k (a j) -> p (k a) j", j=P).rearrange(
            "p (g h) j -> p g h j", g=2)
        lru_w_used = []
        cs_dram = nc.dram_tensor("cs_scratch", (HEADS, SEQ), F32, kind="Internal").ap()

        def first_splits():
            split_tile()
            nc.scalar.dma_start(con[:, :], consts).then_inc(s_consts, 16)
            for i, name in enumerate(("lru_w_r", "lru_w_i")):
                nc.scalar.dma_start(lru_w[:, i], w[name].rearrange("h i j -> i h j")).then_inc(s_lru, 16)

        norm_to(0, "norm1", 0, high, meanwhile=first_splits)

        a0, wd = PARAM_AT["conv_w"]
        half = ts(par[:, a0:a0 + wd + XBC // P], par[:, a0:a0 + wd + XBC // P], 0.5, ALU.mult, after=[loaded])
        a0 = PARAM_AT["b_r"][0]
        half_b = ts(par[:, a0:a0 + 2 * LC], par[:, a0:a0 + 2 * LC], 0.5, ALU.mult, after=[loaded])
        a0 = PARAM_AT["b_gate"][0]
        half_g = ts(par[:, a0:a0 + 2 * DC], par[:, a0:a0 + 2 * DC], 0.5, ALU.mult, after=[loaded])

        def softplus(out, x, s1, s2, sign, after):
            t = ts(s1, x, -1.0, ALU.mult, after=after)
            t = tt(s1, s1, x, ALU.min, after=[t])
            t = fn(s1, s1, ACT.Exp, after=[t])
            t = ts(s2, s1, 1.0, ALU.add, after=[t])
            l = fn(out, s2, ACT.Ln, after=[t, *after])
            u = stt(s1, s2, -1.0, s1, ALU.add, ALU.subtract, after=[t])
            r = recip(s2, s2, after=[l, u])
            t = tt(s1, s1, s2, ALU.mult, after=[r])
            t = tt(out, out, s1, ALU.subtract, after=[t, l])
            t = ts(s1, x, sign, ALU.mult, 0.0, ALU.max, after=[t])
            return tt(out, out, s1, ALU.add, after=[t])

        sp_lam = small[:, 0:LC]
        neg_a = small[0:HEADS, 48:49]

        dt = sb("dt", [HEADS, SEQ], stack=one)
        cs = sb("cs", [HEADS, SEQ], stack=one)
        dt_tok = sb("dt_tok", [P, TT, HEADS], stack=one)
        neg_cs = sb("neg_cs", [P, TT, HEADS], stack=one)
        ssd_ready = {}

        def prepare_gates():
            t = softplus(sp_lam, param("lam", 0, LC), small[:, 16:16 + LC], small[:, 32:32 + LC], -1.0, [loaded])
            ssd_ready["lam"] = ts(sp_lam, sp_lam, -LRU_C / 2, ALU.mult, after=[t])
            t = fn(neg_a, param("a_log")[0:HEADS], ACT.Exp, after=[loaded])
            ssd_ready["neg_a"] = ts(neg_a, neg_a, -1.0, ALU.mult, after=[t])

        dt_x, dt_s1, dt_s2 = (cs_all[0:HEADS, i, :] for i in range(3))

        def evacuate_dt(bank, token):
            ssd_ready["dt_x"] = ts(dt_x, bank.ap[0:HEADS, 0:SEQ], param("dt_bias")[0:HEADS], ALU.add,
                                   after=[token, loaded])
            bank.users = [ssd_ready["dt_x"]]

        def make_dt():
            for _ in range(5):
                yield
            t = softplus(dt[:, :], dt_x, dt_s1, dt_s2, 1.0, [ssd_ready["dt_x"]])
            yield
            u = ts(dt_s1, dt[:, :], neg_a, ALU.mult, after=[t, ssd_ready["neg_a"]])
            v = vec.count_up(nc.vector.memset(dt_s2, 1.0))
            vec.wait(u, v)
            t = vec.count_up(nc.vector.tensor_tensor_scan(cs[:, :], dt_s2, dt_s1, 0.0, ALU.mult, ALU.add))
            act.wait(t)
            nc.scalar.dma_start(cs_dram, cs[:, :]).then_inc(s_spill, 16)
            ssd_ready["cs"] = t
            yield
            yield
            yield from turn_dt()

        def turn_dt():
            t = ssd_ready["cs"]
            bank = high.take(pe)
            for i, src in enumerate((dt, cs)):
                for tile in range(TT):
                    j = (i * TT + tile) * HEADS
                    inst = transpose(bank.ap[:, j:j + HEADS], src[:, tile * P:(tile + 1) * P], HEADS, after=[t])
            token = pe.count_up(inst)
            view = bank.ap[:, 0:4 * HEADS].rearrange("p (i t h) -> p i t h", i=2, t=TT)
            a = copy(dt_tok[:, :, :], view[:, 0], after=[token])
            b = ts(neg_cs[:, :, :], view[:, 1], -1.0, ALU.mult, after=[token])
            bank.users = [b]
            ssd_ready["dt"] = [a, b]
            yield

        up("dt", 0, low, evacuate_dt, width=P)
        background.append(make_dt())

        prepare_gates()

        def conv(bank, token, out, w_name, w_stride, b_name, k0):
            for m in range(2):
                t = fn(out[:, m, :], bank.ap[:, m * SEQ:(m + 1) * SEQ], ACT.Identity, after=[token, half, loaded],
                       scale=param(w_name, 3 * w_stride + k0 + m), bias=param(b_name, k0 + m))
            tokens = [t, t]
            for j in (2, 1, 0):
                d = 3 - j
                for m in range(2):
                    u = bank.ap[:, m * SEQ:(m + 1) * SEQ]
                    tokens[m] = stt(out[:, m, d:SEQ], u[:, 0:SEQ - d], param(w_name, j * w_stride + k0 + m),
                                    out[:, m, d:SEQ], ALU.mult, ALU.add, after=[tokens[m]])
            bank.users = [tokens[1]]
            return tokens[1]

        xbc_ready = [None] * (XBC // P)

        def evacuate_xbc(k0):
            def go(bank, token):
                act.wait(lru_w_used)
                t = conv(bank, token, xbc[:, k0:k0 + 2, :], "conv_w", XBC // P, "conv_b", k0)

                def silu():
                    th = tmps.take(act)
                    a = fn(th.ap, xbc[:, k0:k0 + 2, :], ACT.Tanh, after=[t])
                    b = stt(xbc[:, k0:k0 + 2, :], pair(th.ap), 1.0, xbc[:, k0:k0 + 2, :], ALU.add, ALU.mult, after=[a])
                    th.users = [b]
                    xbc_ready[k0] = xbc_ready[k0 + 1] = b
                return silu
            return go

        u_ready = [None] * LC

        def evacuate_lx(k0):
            def go(bank, token):
                u_ready[k0] = u_ready[k0 + 1] = conv(bank, token, lru_u[:, k0:k0 + 2, :], "lconv_w", LC, "lconv_b", k0)
            return go

        lru_done = [None] * LC

        def lru_work():
            for h in range(LC):
                bank = high.take(pe)
                mm(bank.ap[:, 0:SEQ], lru_w[:, 0, h, :], lru_u[:, h, :], after=[(s_lru, 32), u_ready[h]])
                token = pe.count_up(mm(bank.ap[:, SEQ:512], lru_w[:, 1, h, :], lru_u[:, h, :]))
                th, sq = tmps.take(act), tmps.take(pool)
                r, g, s = th.ap[:, 0:SEQ], th.ap[:, SEQ:512], sq.ap[:, 0:SEQ]
                fn(r, bank.ap[:, 0:SEQ], ACT.Tanh, after=[token, half_b], scale=0.5, bias=param("b_r", h))
                a2 = fn(g, bank.ap[:, SEQ:512], ACT.Tanh, scale=0.5, bias=param("b_i", h))
                bank.users = [a2]
                lam = sp_lam[:, h:h + 1]
                e = fn(lru_a[:, h, :], r, ACT.Exp, after=[a2, ssd_ready["lam"]], scale=lam, bias=lam)
                tl = fn(r, r, ACT.Tanh, after=[e], scale=lam, bias=lam)
                a3 = tt(s, lru_a[:, h, :], lru_a[:, h, :], ALU.mult, after=[e], on=pool)
                v = stt(lru_b[:, h, :], s, 1.0, r, ALU.add, ALU.mult, after=[a3, tl])
                v3 = stt(lru_u[:, h, :], g, 1.0, lru_u[:, h, :], ALU.add, ALU.mult, after=[a2])
                th.users, sq.users = [v3], [v]
                if h not in (2, 4):
                    yield
            lru_w_used.append(token)
            for h in (0, LC // 2):
                b = lru_b[:, h:h + LC // 2, :]
                root = fn(b, b, ACT.Sqrt, after=[v], scale=-0.25)
                yield
            for h in range(LC):
                t = tt(lru_b[:, h, :], lru_b[:, h, :], lru_u[:, h, :], ALU.mult, after=[root, v3])
                vec.wait(t)
                lru_done[h] = vec.count_up(nc.vector.tensor_tensor_scan(lru_u[:, h, :], lru_a[:, h, :], lru_b[:, h, :],
                                                                        0.0, ALU.mult, ALU.add))
                if h % 3 == 2:
                    yield

        scan = lru_work()
        for i in range(LC // 2):
            if i == 1:
                background.append(scan)
            up("lx", 0, low, evacuate_lx(2 * i))
        for i in range(4):
            up("bc", 0, low, evacuate_xbc(16 + 2 * i))

        y_ready = [None] * GROUPS
        cs_read, xdt_read, cb_read = [], [], []

        def load_cs(g):
            act.wait((s_spill, 16), cs_read)
            rows = cs_dram[g * HPG:(g + 1) * HPG, :].partition_broadcast(P)
            nc.scalar.dma_start(cs_all[:, :, :], rows).then_inc(s_bcast, 16)

        def ssd(g):
            if g == 0:
                load_cs(0)
            cs_here = (s_bcast, 16 * (g + 1))
            bm, cm = xbc[:, 16 + g, :], xbc[:, 20 + g, :]
            bank = high.take(pe)
            mm(bank.ap[:, 0:SEQ], bm[:, 0:P], cm, after=[xbc_ready[16 + g], xbc_ready[20 + g]])
            token = pe.count_up(mm(bank.ap[:, SEQ:KQ], bm[:, P:SEQ], cm[:, P:SEQ]))
            cb = tt(cb_mask[:, :], bank.ap[:, 0:KQ], c["tri"], ALU.mult, after=[token, cb_read, consts_here])
            bank.users = [cb]
            cb_read.clear()
            x_ready = [xbc_ready[GC * g + k] for k in range(GC)]
            xdt_ready = []
            for t in range(TT):
                bank = high.take(pe)
                for k in range(GC):
                    inst = transpose(bank.ap[:, k * P:(k + 1) * P], xbc[:, GC * g + k, t * P:(t + 1) * P],
                                     after=[x_ready[k]])
                token = pe.count_up(inst)
                v = tt(xdt[:, t, :].rearrange("p (h e) -> p h e", e=HD), bank.ap.rearrange("p (h e) -> p h e", e=HD),
                       dt_tok[:, t, g * HPG:(g + 1) * HPG].unsqueeze(2).broadcast_to([P, HPG, HD]), ALU.mult,
                       after=[token, xdt_read, ssd_ready["dt"]])
                bank.users = [v]
                xdt_ready.append(v)
            xdt_read.clear()
            yield
            m_ready = {}

            def decays(heads):
                made = []
                for h in heads:
                    e = tmps.take(vec)
                    hh = g * HPG + h
                    ts(e.ap[:, 0:SEQ], cs_all[:, h, :], neg_cs[:, 0, hh:hh + 1], ALU.add, 0.0, ALU.min,
                       after=[cs_here, ssd_ready["dt"]])
                    d = ts(e.ap[:, SEQ:KQ], cs_all[:, h, P:SEQ], neg_cs[:, 1, hh:hh + 1], ALU.add, 0.0, ALU.min)
                    made.append((h, e, fn(e.ap[:, 0:KQ], e.ap[:, 0:KQ], ACT.Exp, after=[d])))
                for h, e, a in made:
                    v = tt(e.ap[:, 0:KQ], e.ap[:, 0:KQ], cb_mask[:, :], ALU.mult, after=[a, cb])
                    m_ready[h] = (e, v)
                return d, v

            for pair_h in range(0, HPG, 2):
                a, v = decays((pair_h, pair_h + 1))
                if pair_h == HPG - 2:
                    cs_read.append(a)
                    cb_read.append(v)
                    if g + 1 < GROUPS:
                        load_cs(g + 1)
                yield
                bank = high.take(pe)
                for h in (pair_h, pair_h + 1):
                    e, v = m_ready[h]
                    rows = slice((h % 2) * HD, (h % 2 + 1) * HD)
                    mm(bank.ap[rows, 0:SEQ], xdt[:, 0, h * HD:(h + 1) * HD], e.ap[:, 0:SEQ], True, False,
                       after=[v, xdt_ready])
                    inst = mm(bank.ap[rows, P:SEQ], xdt[:, 1, h * HD:(h + 1) * HD], e.ap[:, SEQ:KQ], False, True)
                    e.users = [pe.count_up(inst)]
                token = e.users[0]
                k = GC * g + pair_h // 2
                xbc_y = stt(xbc[:, k, :], xbc[:, k, :], param("d_skip", k), bank.ap[:, 0:SEQ], ALU.mult, ALU.add,
                            after=[token])
                bank.users = [xbc_y]
            xdt_read.append(token)
            y_ready[g] = xbc_y

        def all_ssd():
            for g in range(GROUPS):
                yield from ssd(g)

        gate_ready = [None] * (2 * DC)

        def evacuate_gate(k0):
            def go(bank, token):
                for m in range(2):
                    a = fn(gates[:, k0 + m, :], bank.ap[:, m * SEQ:(m + 1) * SEQ], ACT.Tanh,
                           after=[token, half_g, lru_done], scale=0.5, bias=param("b_gate", k0 + m))
                bank.users = [a]
                gate_ready[k0] = gate_ready[k0 + 1] = a
            return go

        ssd_work = all_ssd()
        for n, (kind, i) in enumerate(XS_AND_GATES):
            if n == SCAN_TILES:
                finish(scan)
                background.append(ssd_work)
            up(kind, 0, low, evacuate_xbc(2 * i) if kind == "xs" else evacuate_gate(2 * i))

        lru_out = [None] * LC

        def evacuate_ly(k0):
            def go(bank, token):
                q = tmps.take(act)
                x2 = bank.ap
                a = fn(q.ap, x2, ACT.Square, after=[token], scale=float(np.sqrt(0.044715)))
                v = stt(q.ap, q.ap, 1.0, x2, ALU.add, ALU.mult, after=[a])

                def gelu():
                    a = fn(q.ap, q.ap, ACT.Tanh, after=[v], scale=float(np.sqrt(2 / np.pi)))
                    t = stt(q.ap, q.ap, 1.0, x2, ALU.add, ALU.mult, after=[a])
                    bank.users = [t]
                    hs = lru_u[:, k0:k0 + 2, :]
                    t = stt(hs, pair(q.ap), 0.5, hs, ALU.mult, ALU.mult, after=[t, lru_done[k0], lru_done[k0 + 1]])
                    q.users = [t]
                    lru_out[k0] = lru_out[k0 + 1] = t
                return gelu
            return go

        for i in range(LC // 2):
            up("ly", 0, low, evacuate_ly(2 * i))

        z_ready = [None] * (2 * GC)
        z_read = [None, None]

        def evacuate_z(k0):
            def go(bank, token):
                th = tmps.take(act)
                a = fn(th.ap, bank.ap, ACT.Tanh, after=[token], scale=0.5)
                j = k0 % (2 * GC)
                assert y_ready[k0 // GC]
                v = stt(th.ap, th.ap, 1.0, bank.ap, ALU.add, ALU.mult, after=[a])
                bank.users = [v]
                v = stt(z_silu[:, j:j + 2, :], th.ap.rearrange("p (k t) -> p k t", k=2), 0.5, xbc[:, k0:k0 + 2, :],
                        ALU.mult, ALU.mult, after=[v, y_ready[k0 // GC], z_read[j // GC]])
                th.users = [v]
                z_ready[j] = z_ready[j + 1] = v
            return go

        def group_norm(g):
            z0 = GC * (g % 2)
            squares = squares_of(z_silu[:, z0:z0 + GC, :], z_ready[z0:z0 + GC])
            total = add_up(squares)
            yield
            bank, summed = mean_of(*total, c["mean_group"], low)
            root = fn(rstd[:, :], bank.ap[:, 0:SEQ], ACT.Sqrt, after=[summed, norm_users], bias=c["eps"])
            norm_users.clear()
            bank.users = [root]
            yield
            scale = recip(rstd[:, :], rstd[:, :], after=[root])
            for j in range(GC // 2):
                n = tmps.take(vec)
                for m in range(2):
                    k = GC * g + 2 * j + m
                    t = stt(n.ap[:, m * SEQ:(m + 1) * SEQ], z_silu[:, z0 + 2 * j + m, :], param("norm_w", k),
                            rstd[:, :], ALU.mult, ALU.mult, after=[scale])
                n.users = split_into(8 + GC * (g % 2) + 2 * j, 2, n.ap.rearrange("p (k t) -> p k t", k=2), after=[t])
            z_read[g % 2] = t
            norm_users.append(t)
            yield

        norms, ssm_acc, lru_acc = [], [], []
        def down_ssm(g):
            for i in range(2):
                k = 8 + GC * (g % 2) + 2 * i
                tokens = down("out_ssm", (k, k + 1), ssm_acc, high, g == 0 and i == 0, g == GROUPS - 1 and i == 1)
            return tokens

        def down_lru(i):
            return down("out_lru", (2 * i, 2 * i + 1), lru_acc, low, i == 0, i == LC // 2 - 1)

        for g in range(GROUPS):
            for i in range(2):
                up("z", 0, low, evacuate_z(GC * g + 2 * i))
            norms.append(group_norm(g))
            background.append(norms[g])
            if g == 2:
                finish(ssd_work)
            if g >= 2:
                finish(norms[g - 2])
                down_ssm(g - 2)
        for k in range(0, 8, 2):
            split_into(k, 2, lru_u[:, k:k + 2, :], after=[lru_out[k]])
        finish(norms[GROUPS - 2])
        down_ssm(GROUPS - 2)
        split_into(8, 2, lru_u[:, 8:10, :], after=[lru_out[8]])
        for i in range(LC // 2 - 1):
            down_lru(i)
        finish(norms[GROUPS - 1])
        tokens = down_ssm(GROUPS - 1)
        for b in range(4):
            g = gates[:, 2 * b:2 * b + 2, :]
            gate_ready[2 * b] = stt(g, g, 1.0, pair(ssm_acc[b].ap), ALU.add, ALU.mult,
                                    after=[tokens[b], gate_ready[2 * b]])
            ssm_acc[b].users = [gate_ready[2 * b]]
        tokens = down_lru(LC // 2 - 1)

        def split_mixed(b, ready):
            hi, lo = act_hi[:, 2 * b:2 * b + 2, :], act_lo[:, 2 * b:2 * b + 2, :]
            g, used_ = gates[:, DC + 2 * b:DC + 2 * b + 2, :], [chunk_users[2 * b], chunk_users[2 * b + 1]]
            h = fn(hi, g, ACT.Copy, after=[ready, used_], scale=0.5)
            v = stt(lo, g, 0.5, hi.bitcast(F32), ALU.mult, ALU.subtract, after=[h, ready, used_])
            for k in (2 * b, 2 * b + 1):
                chunk_users[k], chunk_ready[k] = None, [h, v]

        summed = []
        for b in range(4):
            g = gates[:, DC + 2 * b:DC + 2 * b + 2, :]
            t = stt(g, g, 1.0, pair(lru_acc[b].ap), ALU.add, ALU.mult, after=[tokens[b], gate_ready[DC + 2 * b]])
            lru_acc[b].users = [t]
            summed.append(tt(g, g, gates[:, 2 * b:2 * b + 2, :], ALU.add, after=[t, gate_ready[2 * b]]))
            if b:
                split_mixed(b - 1, summed[b - 1])
        split_mixed(3, summed[3])

        out_acc = []
        for i in range(DC // 2):
            out_tokens = down("out", (2 * i, 2 * i + 1), out_acc, high, i == 0, i == DC // 2 - 1)

        one_done = [vec.last(), act.last(), pe.last(), pool.last()]
        one.close()

        two = ExitStack()
        ctx.enter_context(two)
        con2 = sb("consts_2", [P, sum(n for _, n in CONSTS_2)], stack=two)
        sp.wait(one_done)
        nc.sync.dma_start(con2[:, :], consts_2).then_inc(s_consts_2, 16)
        loaded2 = (s_consts_2, 16)
        at = 0
        for name, n in CONSTS_2:
            c[name] = con2[:, at:at + n]
            at += n
        ckv_t = sb("ckv_t", [P, SEQ], stack=two)
        ukv = sb("ukv", [P, 2, DSA_W], stack=two)
        rstd_tok = sb("rstd_tok", [P, 2 * TT], stack=two)
        w_norms = sb("w_norms", [P, DC], stack=two)
        ki_t = sb("ki_t", [P, SEQ], stack=two)
        w_idx = sb("w_idx", [P, TT, IDX_H], stack=two)
        qi_t = sb("qi_t", [P, IDX_H * HD // P, SEQ], stack=two)
        dq_t = sb("dq_t", [P, 2, SEQ], stack=two)
        dk_t = sb("dk_t", [P, 2, SEQ], stack=two)
        dv = sb("dv", [P, TT, DSA_W], stack=two)
        relu = Ring([sb(f"relu_{i}", [P, 512], stack=two)[:, :] for i in range(2)])
        score = sb("score", [P, KQ], stack=two)
        work = [sb(f"work_{i}", [P, KQ], stack=two) for i in range(2)]
        keep = sb("keep", [P, KQ], stack=two)
        top8 = sb("top8", [P, 2, 8], stack=two)
        rq_t = sb("rq_t", [P, 2, SEQ], stack=two)
        rk_t = sb("rk_t", [P, 2, SEQ], stack=two)
        rv = sb("rv", [P, TT, RET_W], stack=two)
        rg_t = sb("rg_t", [P, 2, SEQ], stack=two)
        ro_t = sb("ro_t", [P, 2, SEQ], stack=two)
        lq_t = sb("lq_t", [P, 4, SEQ], stack=two)
        lk_t = sb("lk_t", [P, 4, SEQ], stack=two)
        lv = sb("lv", [P, TT, DIL_W], stack=two)
        probs = Ring([sb(f"probs_{i}", [P, KQ], stack=two)[:, :] for i in range(6)])
        probs_t = Ring([sb(f"probs_t_{i}", [P, KQ], stack=two)[:, :] for i in range(4)])
        decayed = Ring([sb(f"decayed_{i}", [P, KQ], stack=two)[:, :] for i in range(2)])
        stats = Ring([sb(f"stats_{i}", [P, 8], stack=two)[:, :] for i in range(6)])

        def ffn_scale():
            bank, after = mean_of(*late["total"], c["mean_d"], low)
            late["ready"] = scale_of(bank, after)
            yield from ()

        begin_norm(8, param("norm2", 0, DC), ffn_scale(), out_acc, out_tokens)
        silu_gate = {}

        def evacuate_ffn_gate(bank, token):
            th, s = tmps.take(act), tmps.take(vec)
            g = by_scale(pair(s.ap), pair(bank.ap), [token])
            bank.users = [g]

            def silu():
                a = fn(th.ap, s.ap, ACT.Tanh, after=[g], scale=0.5)
                v = stt(s.ap, th.ap, 1.0, s.ap, ALU.add, ALU.mult, after=[a, g])
                th.users = [v]
                v = by_scale(pair(s.ap), pair(s.ap), [v])
                norm_users.append(v)
                silu_gate["s"], silu_gate["v"] = s, v
            return silu

        def evacuate_ffn_up(k):
            def go(bank, token):
                s = silu_gate["s"]
                v = stt(s.ap, s.ap, 0.5, bank.ap, ALU.mult, ALU.mult, after=[token, silu_gate["v"]])
                bank.users = [v]

                def split():
                    s.users = split_into(k, 2, pair(s.ap), after=[v])
                return split
            return go

        nf = FFN // 256
        for i in range(nf + 1):
            if i < nf:
                up("ffn_gate", 8, low, evacuate_ffn_gate)
                up("ffn_up", 8, low, evacuate_ffn_up(2 * (i % 4)))
            if i == 1:
                acc = []
            if i:
                k = 2 * ((i - 1) % 4)
                tokens = down("ffn_out", (k, k + 1), acc, high, i == 1, i == nf)

        PAIRS = ((0, 0, P), (1, P, KQ))

        def value_product(o, pt, v0, v1, after):
            mm(o, v0, pt[:, 0:SEQ], True, False, after=after)
            return mm(o[:, P:SEQ], v1, pt[:, SEQ:KQ], False, True)

        def head_rows(t, h):
            return t[(h % 2) * HD:(h % 2 + 1) * HD, h // 2, :]

        def attention(heads, q, k, v, additive, count, ready, out_chunk, ring):

            def scores(h):
                bank = ring().take(pe)
                qh, kh = head_rows(q, h), head_rows(k, h)
                mm(bank.ap[:, 0:P], qh[:, 0:P], kh[:, 0:P], after=ready)
                token = pe.count_up(mm(bank.ap[:, P:KQ], qh[:, P:SEQ], kh[:, :]))
                p, st = probs.take(vec), stats.take(vec)
                t = stt(p.ap, bank.ap[:, 0:KQ], SCALE, additive, ALU.mult, ALU.add, after=[token, *ready, loaded2])
                bank.users = [t]
                vec.wait(t)
                for i, a, b in PAIRS:
                    t = vec.count_up(nc.vector.tensor_reduce(st.ap[:, i:i + 1], p.ap[:, a:b], AX_X, ALU.max, negate=True))
                for i, a, b in PAIRS:
                    e = fn(p.ap[:, a:b], p.ap[:, a:b], ACT.Exp, after=[t], bias=st.ap[:, i:i + 1],
                           accum=st.ap[:, 2 + i:3 + i] if count is None else None)
                return p, st, e

            def normalise(p, st, e):
                if count is not None:
                    for i, a, b in PAIRS:
                        e = stt(p.ap[:, a:b], p.ap[:, a:b], 1.0, count[:, a:b], ALU.mult, ALU.mult, after=[e],
                                accum=st.ap[:, 2 + i:3 + i])
                r_ = recip(st.ap[:, 4:6], st.ap[:, 2:4], after=[e])
                for i, a, b in PAIRS:
                    n = ts(p.ap[:, a:b], p.ap[:, a:b], st.ap[:, 4 + i:5 + i], ALU.mult, after=[r_])
                st.users = [n]
                return p, n

            def turn(p, n):
                bank = ring().take(pe)
                for j in range(3):
                    inst = transpose(bank.ap[:, j * P:(j + 1) * P], p.ap[:, j * P:(j + 1) * P], after=[n])
                token = pe.count_up(inst)
                p.users = [token]
                pt = probs_t.take(act)
                cp = fn(pt.ap, bank.ap[:, 0:KQ], ACT.Copy, after=[token])
                bank.users = [cp]
                return pt, cp

            def values(h0, turned):
                bank = ring().take(pe)
                for h, (pt, cp) in zip((h0, h0 + 1), turned):
                    o = bank.ap[(h % 2) * HD:(h % 2 + 1) * HD, 0:SEQ]
                    token = pe.count_up(value_product(o, pt.ap, v[:, 0, h * HD:(h + 1) * HD],
                                                      v[:, 1, h * HD:(h + 1) * HD], [cp, ready]))
                    pt.users = [token]
                split_from_psum(out_chunk + h0 // 2, bank, token)

            pair_n, turned = None, None
            for h0 in range(heads[0], heads[-1] + 3, 2):
                scored = [scores(h) for h in (h0, h0 + 1)] if h0 in heads else None
                if pair_n:
                    turned = [turn(*x) for x in pair_n]
                yield
                pair_n = [normalise(*x) for x in scored] if scored else None
                if turned:
                    values(h0 - 2, turned)
                    turned = None
                    yield
                elif h0 == heads[0]:
                    yield

        def split_from_psum(k, bank, token):
            hi, lo = act_hi[:, k, :], act_lo[:, k, :]
            a = fn(hi, bank.ap[:, 0:SEQ], ACT.Copy, after=[token, chunk_users[k]])
            b = tt(lo, bank.ap[:, 0:SEQ], hi.bitcast(F32), ALU.subtract, after=[a, token, chunk_users[k]])
            bank.users = [b]
            chunk_users[k] = None
            chunk_ready[k] = [a, b]

        def plain(dst, ready):
            def go(bank, token):
                t = by_scale(dst, pair(bank.ap), [token])
                bank.users = [t]
                norm_users.append(t)
                ready.append(t)
            return go

        def plain_tokens(dst, ready):
            def go(bank, token):
                for t in range(TT):
                    a = fn(dst[:, t, :], bank.ap[:, t * 256:(t + 1) * 256], ACT.Copy, after=[token, late["ready"]],
                           scale=rstd_tok[:, t:t + 1])
                bank.users = [a]
                ready.append(a)
            return go

        for e in (vec, act, pe, pool):
            e.wait(one_done)
        prev = []
        for l in range(DEPTH_2):
            base = 8
            for e in (vec, act, pe, pool):
                e.wait(prev)
            r = {"dsa_ring": low}
            idx_ready, dsa_ready = [], []
            sp.wait(prev)
            for i, name in enumerate(("dsa_w_uk_2", "dsa_w_uv_2")):
                nc.sync.dma_start(ukv[:, i, :], w[name][l]).then_inc(s_ukv, 16)

            def layer_scale(first=l == 0):
                yield
                bank, after = mean_of(*late["total"], c["mean_d"], high)
                ready = scale_of(bank, after)
                if first:
                    copy(rstd_sq[:, :], rstd[:, :], after=[ready])
                    for k in range(DC):
                        t = stt(res[:, k, :], res[:, k, :], param("norm_f", k), rstd[:, :], ALU.mult, ALU.mult,
                                after=[ready, late["split"], act.last()])
                        res_ready[k] = t
                    norm_users.append(t)
                    total = add_up(squares_of(res, res_ready))
                    yield
                    bank, after = mean_of(*total, c["mean_d"], high)
                    ready = scale_of(bank, after)
                    ready = tt(rstd[:, :], rstd[:, :], rstd_sq[:, :], ALU.mult, after=[ready])
                yield
                bank = high.take(pe)
                for t in range(TT):
                    inst = transpose(bank.ap[:, t * P:(t + 1) * P], rstd[:, t * P:(t + 1) * P], after=[ready])
                token = pe.count_up(inst)
                src = bank.ap[:, 0:SEQ].rearrange("p (t j) -> p t j", t=TT)[:, :, 0]
                a = copy(rstd_tok[:, 0:TT], src, after=[token])
                b = ts(rstd_tok[:, TT:2 * TT], src, IDX_SCALE, ALU.mult, after=[token])
                bank.users = [b]
                late["ready"] = [ready, a, b]

            if l == 0:
                t = tt(w_norms[:, :], param("norm_f", 0, DC), param("attn", 0, DC), ALU.mult, after=[loaded])
                act.wait(t)
                begin_norm(base, w_norms, layer_scale(), acc, tokens)
            else:
                begin_norm(base, param("attn", DC * l, DC), layer_scale(), acc, tokens)

            def evacuate_ckv(bank, token):
                t = by_scale(ckv_t[:, :].unsqueeze(1), bank.ap[:, 0:SEQ].unsqueeze(1), [token], n=1)
                bank.users = [t]
                norm_users.append(t)
                r["ckv_raw"] = t

            up("qi", base, low, plain(qi_t[:, 0:2, :], idx_ready))
            up("ckv", base, low, evacuate_ckv, width=LATENT)

            def latent():
                sq = tmps.take(act)
                a = fn(sq.ap[:, 0:SEQ], ckv_t[:, :], ACT.Square, after=[r["ckv_raw"]])
                yield
                bank = high.take(pe)
                token = pe.count_up(mm(bank.ap[:, 0:SEQ], c["mean_latent"], sq.ap[:, 0:SEQ], after=[a]))
                scale, read = rms_scale(bank.ap[:, 0:SEQ], sq.ap[:, SEQ:512], after=[token])
                bank.users = [read]
                ckv = stt(ckv_t[:, :], ckv_t[:, :], param("kvn", l), sq.ap[:, SEQ:512], ALU.mult, ALU.mult,
                          after=[scale, r["ckv_raw"]])
                sq.users = [ckv]
                yield
                bank, bank2 = high.take(pe), high.take(pe)
                for m in range(2):
                    inst = mm(bank.ap[:, m * SEQ:(m + 1) * SEQ], ukv[:, 0, m * P:(m + 1) * P], ckv_t[:, :],
                              after=[(s_ukv, 32 * (l + 1)), ckv])
                t1 = pe.count_up(inst)
                for t in range(TT):
                    inst = mm(bank2.ap[:, t * DSA_W:(t + 1) * DSA_W], ckv_t[:, t * P:(t + 1) * P], ukv[:, 1, :])
                t2 = pe.count_up(inst)
                a = copy(dk_t[:, :, :], pair(bank.ap), after=[t1], on=act)
                b = copy(dv[:, :, :], pair(bank2.ap), after=[t2], on=act)
                bank.users, bank2.users = [a], [b]
                dsa_ready.extend([a, b])

            i, tile, ready = take("ki")
            bank = low.take(pe)
            pe.wait(ready)
            for k in range(DC):
                product(bank.ap[:, 0:SEQ], tile[:, k, 0:2 * HD], acts[:, base + k, :], k == 0, k == DC - 1)
            for t in range(TT):
                for k in range(DC):
                    inst = product(bank.ap[:, SEQ + t * IDX_H:SEQ + (t + 1) * IDX_H],
                                   acts[:, base + k, t * P:(t + 1) * P], tile[:, k, 2 * HD:2 * HD + IDX_H],
                                   k == 0, k == DC - 1)
            token = pe.count_up(inst)
            used(i, token)

            def evacuate_ki(bank, token):
                for t in range(TT):
                    a = fn(w_idx[:, t, :], bank.ap[:, SEQ + t * IDX_H:SEQ + (t + 1) * IDX_H], ACT.Copy,
                           after=[token, late["ready"]], scale=rstd_tok[:, TT + t:TT + t + 1])
                b = by_scale(ki_t[:, :].unsqueeze(1), bank.ap[:, 0:SEQ].unsqueeze(1), [a], n=1)
                bank.users = [b]
                norm_users.append(b)
                idx_ready.extend([a, b])

            run_late()
            evacuate_when_scaled(evacuate_ki, bank, token)
            advance()
            up("qi", base, low, plain(qi_t[:, 2:4, :], idx_ready))
            assert late["work"] is None
            kv = latent()
            background.append(kv)

            def select():
                for q, a, b in PAIRS:
                    n = b - a
                    per = 512 // n
                    halves = [h for half in (0, 1) for h in range(half, IDX_H, 2)]
                    for h0 in range(0, IDX_H, per):
                        bank = high.take(pe)
                        for j, h in enumerate(halves[h0:h0 + per]):
                            inst = mm(bank.ap[:, j * n:(j + 1) * n], head_rows(qi_t, h)[:, q * P:(q + 1) * P],
                                      ki_t[(h % 2) * HD:(h % 2 + 1) * HD, 0:n], after=idx_ready)
                        token = pe.count_up(inst)
                        rl = relu.take(act)
                        x = fn(rl.ap, bank.ap, ACT.Relu, after=[token])
                        bank.users = [x]
                        for j, h in enumerate(halves[h0:h0 + per]):
                            src = rl.ap[:, j * n:(j + 1) * n]
                            wt = w_idx[:, q, h:h + 1]
                            if h == 0:
                                t = ts(score[:, a:b], src, wt, ALU.mult, after=[x, idx_ready])
                            else:
                                t = stt(score[:, a:b], src, wt, score[:, a:b], ALU.mult, ALU.add, after=[x, t])
                        rl.users = [t]
                        if h0 // per % 2:
                            yield
                    t = tt(score[:, a:b], score[:, a:b], c["causal"][:, a:b], ALU.add, after=[t, loaded2])
                src, ready = score, [t, t]
                for step in range(TOPK // 8):
                    found = []
                    for q, a, b in PAIRS:
                        vec.wait(ready[q])
                        found.append(vec.count_up(nc.vector.max(top8[:, q, :], src[:, a:b])))
                    if step < TOPK // 8 - 1:
                        for q, a, b in PAIRS:
                            vec.wait(found[q])
                            ready[q] = vec.count_up(nc.vector.match_replace(work[step % 2][:, a:b], top8[:, q, :],
                                                                            src[:, a:b], TAKEN))
                    src = work[step % 2]
                    if step % 2:
                        yield
                more, eq, need = work[0], work[1], top8
                t = [None, None]
                for q, a, b in PAIRS:
                    kth = top8[:, q, 7:8]
                    ts(more[:, a:b], score[:, a:b], kth, ALU.is_gt, after=found)
                    t[q] = ts(eq[:, a:b], score[:, a:b], kth, ALU.is_equal)
                for q, a, b in PAIRS:
                    vec.wait(t[q])
                    t[q] = vec.count_up(nc.vector.tensor_reduce(need[:, q, 0:1], more[:, a:b], AX_X, ALU.add))
                for q, a, b in PAIRS:
                    t[q] = ts(need[:, q, 1:2], need[:, q, 0:1], -1.0, ALU.mult, float(TOPK), ALU.add, after=[t[q]])
                yield
                for q, a, b in PAIRS:
                    vec.wait(t[q])
                    t[q] = vec.count_up(nc.vector.tensor_tensor_scan(keep[:, a:b], eq[:, a:b], eq[:, a:b], 0.0,
                                                                     ALU.add, ALU.max))
                for q, a, b in PAIRS:
                    t[q] = stt(eq[:, a:b], keep[:, a:b], need[:, q, 1:2], eq[:, a:b], ALU.is_le, ALU.mult, after=[t[q]])
                t = tt(more[:, :], more[:, :], eq[:, :], ALU.add, after=t)
                t = ts(more[:, :], more[:, :], -1.0, ALU.add, -MASKED, ALU.mult, after=[t])
                r["keep"] = tt(keep[:, :], more[:, :], c["causal"], ALU.min, after=[t])
                yield

            sel = select()
            background.append(sel)
            up("dsa_q", base, low, plain(dq_t[:, :, :], dsa_ready))

            def rotary(dst, ready, cos, sin):
                bank = high.take(pe)
                token = pe.count_up(mm(bank.ap, c["rotate"], dst.rearrange("p k t -> p (k t)"), after=[ready, loaded2]))
                both = lambda x: x.unsqueeze(1).broadcast_to([P, 2, SEQ])
                s = tmps.take(vec)
                t1 = tt(pair(s.ap), pair(bank.ap), both(sin), ALU.mult, after=[token])
                bank.users = [t1]
                t2 = tt(dst, dst, both(cos), ALU.mult, after=[ready, token])
                s.users = [tt(dst, dst, pair(s.ap), ALU.add, after=[t1, t2])]
                ready.extend(s.users)

            rk_ready, rq_ready, rv_ready = [], [], []

            def rotate_both():
                yield
                rotary(rk_t[:, :, :], rk_ready, c["cos_k"], c["sin_k"])
                yield
                rotary(rq_t[:, :, :], rq_ready, c["cos"], c["sin"])

            up("ret_k", base, low, plain(rk_t[:, :, :], rk_ready))
            background.append(rotate_both())
            up("ret_q", base, low, plain(rq_t[:, :, :], rq_ready))
            up_tokens("ret_v", base, low, plain_tokens(rv[:, :, :], rv_ready))

            def retention(ch):
                sq, factor = rk_t[:, ch, :], rq_t[:, ch, :]
                if ch:
                    yield
                ms = []
                for h in (2 * ch, 2 * ch + 1):
                    bank = low.take(pe)
                    q, k = head_rows(rq_t, h), head_rows(rk_t, h)
                    mm(bank.ap[:, 0:SEQ], k[:, 0:P], q, after=[rk_ready, rq_ready])
                    token = pe.count_up(mm(bank.ap[:, SEQ:KQ], k[:, P:SEQ], q[:, P:SEQ]))
                    m = decayed.take(vec)
                    dec = c["decay"][:, h * SEQ:(h + 1) * SEQ]
                    tt(m.ap[:, 0:SEQ], bank.ap[:, 0:SEQ], dec, ALU.mult, after=[token])
                    t = tt(m.ap[:, SEQ:KQ], bank.ap[:, SEQ:KQ], dec[:, 0:P], ALU.mult)
                    bank.users = [t]
                    ms.append((m, t))
                yield
                bank = low.take(pe)
                for h, (m, t) in zip((2 * ch, 2 * ch + 1), ms):
                    o = bank.ap[(h % 2) * HD:(h % 2 + 1) * HD, 0:SEQ]
                    token = pe.count_up(value_product(o, m.ap, rv[:, 0, h * HD:(h + 1) * HD],
                                                    rv[:, 1, h * HD:(h + 1) * HD], [t, rv_ready]))
                    m.users = [token]
                cp = copy(ro_t[:, ch, :], bank.ap[:, 0:SEQ], after=[token])
                bank.users = [cp]
                yield
                bank = low.take(pe)
                token = pe.count_up(mm(bank.ap[:, 0:SEQ], c["mean_head"], ro_t[:, ch, :], after=[cp]))
                t = tt(ro_t[:, ch, :], ro_t[:, ch, :], bank.ap[:, 0:SEQ], ALU.subtract, after=[token])
                bank.users = [t]
                a = fn(sq, ro_t[:, ch, :], ACT.Square, after=[t])
                yield
                bank = low.take(pe)
                token = pe.count_up(mm(bank.ap[:, 0:SEQ], c["mean_head"], sq, after=[a]))
                root = fn(factor, bank.ap[:, 0:SEQ], ACT.Sqrt, after=[token], bias=c["eps"])
                bank.users = [root]
                yield
                scale = recip(factor, factor, after=[root])
                t = stt(factor, factor, param("ret", 2 * l + ch), rg_t[:, ch, :], ALU.mult, ALU.mult,
                        after=[scale, r["rg"]])
                t = stt(sq, factor, 0.5, ro_t[:, ch, :], ALU.mult, ALU.mult, after=[t, token])
                split_into(ch, 1, sq.unsqueeze(1), after=[t])
                yield

            ret = [retention(0), retention(1)]

            def evacuate_rg(bank, token):
                th = tmps.take(vec)
                g = by_scale(rg_t[:, :, :], pair(bank.ap), [token])
                bank.users = [g]
                norm_users.append(g)
                a = fn(pair(th.ap), rg_t[:, :, :], ACT.Tanh, after=[g, th.users], scale=0.5)
                v = stt(rg_t[:, :, :], pair(th.ap), 1.0, rg_t[:, :, :], ALU.add, ALU.mult, after=[a])
                th.users = [v]
                r["rg"] = v

            up("ret_g", base, low, evacuate_rg)

            background.extend(ret)

            dil_ready, dil = [], []
            for j in range(2):
                up("dil_k", base, low, plain(lk_t[:, 2 * j:2 * j + 2, :], dil_ready))
                if j:
                    finish(kv, sel)
                    dsa = attention(range(DSA_H), dq_t, dk_t, dv, keep[:, :], None, [dsa_ready, r["keep"]], 2,
                                    ring=lambda: r["dsa_ring"])
                    background.append(dsa)
                up("dil_q", base, low, plain(lq_t[:, 2 * j:2 * j + 2, :], dil_ready))
                dil.append(attention(range(4 * j, 4 * j + 4), lq_t, lk_t, lv, c["union"], c["count"], dil_ready, 4,
                                     ring=lambda: high))
                background.append(dil[j])
                up_tokens("dil_v", base, low, plain_tokens(lv[:, :, j * 256:(j + 1) * 256], dil_ready))

            for n, i in enumerate(OUT_ORDER):
                finish(*{0: ret, 1: [dsa], 2: [dil[0]], 3: [dil[1]]}[i])
                if n == 0:
                    out_acc, r["dsa_ring"] = [], high
                tokens = down("out_2", (2 * i, 2 * i + 1), out_acc, low, n == 0, n == len(OUT_ORDER) - 1,
                              advance_inside=True)
            prev = [vec.last(), act.last(), pe.last(), pool.last()]

            def mlp_scale():
                yield
                bank, after = mean_of(*late["total"], c["mean_d"], high)
                late["ready"] = scale_of(bank, after)

            begin_norm(8, param("mlp", DC * l, DC), mlp_scale(), out_acc, tokens)

            def evacuate_up(k):
                def go(bank, token):
                    s = tmps.take(vec)
                    t = by_scale(pair(s.ap), pair(bank.ap), [token])
                    bank.users = [t]
                    norm_users.append(t)
                    v = stt(s.ap, s.ap, 0.0, s.ap, ALU.max, ALU.mult, after=[t])

                    def split():
                        s.users = split_into(k, 2, pair(s.ap), after=[v])
                    return split
                return go

            nf = FF2 // 256
            for i in range(nf + 2):
                if i < nf:
                    up("up", 8, high, evacuate_up(2 * (i % 4)))
                if i == 2:
                    acc = []
                if i >= 2:
                    k = 2 * ((i - 2) % 4)
                    tokens = down("down", (k, k + 1), acc, low, i == 2, i == nf + 1)

        last_use, squares = [norm_users, res_readers], []
        for b in range(4):
            add_residual(b, acc[b], tokens[b], last_use)
            squares += squares_of(res[:, 2 * b:2 * b + 2, :], res_ready[2 * b:2 * b + 2])
            if b >= 2:
                total = add_up([total, squares[b - 1]]) if b > 2 else add_up(squares[:2])
        total = add_up([total, squares[3]])
        bank, after = mean_of(*total, c["mean_d"], high)
        root = fn(rstd[:, :], bank.ap[:, 0:SEQ], ACT.Sqrt, after=[after, norm_users], bias=c["eps"])
        for k in range(DC):
            weighted = fn(res[:, k, :], res[:, k, :], ACT.Copy, after=[squares[k // 2][1], loaded],
                          scale=param("final", k))
            res_ready[k] = weighted
        late["ready"] = recip(rstd[:, :], rstd[:, :], after=[root])
        for b, on in ((3, pool), (0, vec), (1, vec), (2, vec)):
            y = res[:, 2 * b:2 * b + 2, :]
            done = tt(y, y, rstd[:, :].unsqueeze(1).broadcast_to([P, 2, SEQ]), ALU.mult,
                      after=[late["ready"], res_ready[2 * b + 1]], on=on)
            queue = (sp, act)[b % 2]
            queue.wait(done)
            queue.ops.dma_start(out_t[:, 2 * b:2 * b + 2, :], y).then_inc(s_store, 16)
        nc.sync.wait_ge(s_store, 16 * DC // 2)
        nc.sync.wait_ge(s_spill, 16)
        assert state["next_take"] == len(plan)


def shape_constants():
    ident = np.eye(P)
    tri = np.triu(np.ones((P, P)))
    block = np.kron(np.eye(2), np.ones((HD, HD)) / HD)
    first = {
        "ident": ident, "mean_head": block, "tri": np.concatenate([tri, np.ones((P, P)), tri], 1),
    }
    rot = np.zeros((P, P))
    half = HD // 2
    for h in range(P // HD):
        for i in range(half):
            rot[h * HD + half + i, h * HD + i] = -1.0
            rot[h * HD + i, h * HD + half + i] = 1.0
    inv = np.float32(10000.0) ** (-np.arange(half, dtype=np.float32) / half)
    ang = (np.arange(SEQ, dtype=np.float32)[None, :] * inv.astype(np.float32)[:, None]).astype(np.float32)
    ang = np.tile(ang, (P // half, 1)).astype(np.float64)
    pos = np.arange(SEQ)
    gamma = np.log(1.0 - 2.0 ** (-5.0 - np.arange(RET_H)))
    diff = pos[None, :] - np.arange(P)[:, None]
    decay = np.concatenate([np.exp(np.maximum(diff, 0) * g) * (diff >= 0) for g in gamma], 1)
    q, k = pos[:, None], pos[None, :]
    dist = q - k
    cnt = ((dist >= 0) & (dist <= 128)).astype(int)
    for dil in (4, 16):
        cnt += (dist >= 0) & (dist % dil == 0)
    pairs = lambda m: np.concatenate([m[0:P, 0:P], m[P:SEQ, :]], 1)
    second = {
        "rotate": rot, "cos": np.cos(ang), "sin": np.sin(ang), "cos_k": np.cos(ang) * SCALE, "sin_k": np.sin(ang) * SCALE,
        "decay": decay, "causal": pairs(np.where(dist >= 0, 0.0, MASKED)),
        "union": pairs(np.where(cnt > 0, 0.0, MASKED)), "count": pairs(cnt),
    }
    pack = lambda names, d: np.concatenate([d[n] for n, _ in names], 1).astype(np.float32)
    return pack(CONSTS, first), pack(CONSTS_2, second)


def pack_params(a):
    def chunks(v):
        return np.ascontiguousarray(v.reshape(-1, P).T)

    def padded(v):
        return np.concatenate([v, np.zeros(P - len(v), v.dtype)])[:, None]

    cols = {
        "norm1": chunks(a["norm1_w"]), "conv_w": chunks(a["ssm_conv_w"]), "conv_b": chunks(a["ssm_conv_b"]),
        "lconv_w": chunks(a["lru_conv_w"]), "lconv_b": chunks(a["lru_conv_b"]), "b_r": chunks(a["lru_b_r"]),
        "b_i": chunks(a["lru_b_i"]), "lam": chunks(a["lru_lambda"]), "b_gate": chunks(a["b_branch_gate"]),
        "norm_w": chunks(a["ssm_norm_w"]), "d_skip": chunks(np.repeat(a["ssm_d"].reshape(-1), HD)),
        "norm2": chunks(a["norm2_w"]), "dt_bias": padded(a["ssm_dt_bias"].reshape(-1)),
        "a_log": padded(a["ssm_a_log"].reshape(-1)), "attn": chunks(a["attn_norm_w_2"]), "mlp": chunks(a["mlp_norm_w_2"]),
        "ret": chunks(a["ret_norm_w_2"]), "kvn": chunks(a["dsa_kv_norm_w_2"]), "norm_f": chunks(a["norm_f_w"]), "final": chunks(a["final_norm_w_2"]),
    }
    return np.ascontiguousarray(np.concatenate([cols[n] for n, _ in PARAMS], 1))


WEIGHTS = ["w_in", "w_out_ssm", "lru_w_r", "lru_w_i", "w_out_lru", "w_out", "w_ffn_in", "w_ffn_out",
           "w_in_2", "dsa_w_uk_2", "dsa_w_uv_2", "w_out_2", "w_up_2", "w_down_2"]


def kernel(**inputs):
    import concourse.bacc as bacc
    from concourse.bass_utils import run_bass_kernel_spmd

    a = {k: np.asarray(v) for k, v in inputs.items()}
    consts, consts_2 = shape_constants()
    arrays = {k: (np.ascontiguousarray(a[k]) if k.endswith("_2") else np.ascontiguousarray(a[k][0])) for k in WEIGHTS}
    arrays["x_t"] = np.ascontiguousarray(a["x"][0].T.reshape(DC, P, SEQ).transpose(1, 0, 2))
    arrays["params"], arrays["consts"], arrays["consts_2"] = pack_params(a), consts, consts_2
    nc = bacc.Bacc("TRN2", target_bir_lowering=False, num_devices=1)
    aps = {k: nc.dram_tensor(f"in_{k}", v.shape, F32, kind="ExternalInput").ap() for k, v in arrays.items()}
    out = nc.dram_tensor("out_t", (P, DC, SEQ), F32, kind="ExternalOutput").ap()
    build(nc, {k: aps[k] for k in WEIGHTS}, aps["x_t"], aps["params"], aps["consts"], aps["consts_2"], out)
    r = run_bass_kernel_spmd(nc, [{f"in_{k}": v for k, v in arrays.items()}], core_ids=[0])
    got = r.results[0]["out_t"]
    return np.ascontiguousarray(got.transpose(1, 0, 2).reshape(D, SEQ).T)[None]
```
